# Optimizing a Trainium2 kernel written in Bass

```python
import jax, jax.numpy as jnp
from jax import lax
import numpy as np

D_MODEL = 1024
BATCH = 1
SEQ = 512
DEPTH = 1
DEC_BATCH = 8
DEC_SEQ = 4
PAST_LEN = 4096
PAGE_SIZE = 128

GLA_HEADS = 4
GLA_DK = D_MODEL // 16
GLA_DV = D_MODEL // 8
GLA_QK = GLA_HEADS * GLA_DK
GLA_V = GLA_HEADS * GLA_DV
GLA_RANK = 16
GLA_TAU = 16.0
GLA_CHUNK = 64
M_HEADS = 4
M_DH = D_MODEL // 8
M_WIDTH = M_HEADS * M_DH
M_CHUNK = 64
CONV_W = 4
FORGET_BIAS = 3.0
R_WIDTH = D_MODEL // 2
R_BLOCKS = 8
R_BS = R_WIDTH // R_BLOCKS
R_C = 8.0
D_FF = 2816
FFN_CONV_W = 3
N_BRANCH = 3
EPS = 1e-6

IN_SIZES = (GLA_QK, GLA_QK, GLA_V, GLA_V, GLA_RANK,
            M_WIDTH, M_HEADS, M_HEADS, M_WIDTH,
            R_WIDTH, R_WIDTH,
            N_BRANCH * D_MODEL)
D_IN = sum(IN_SIZES)
D_BRANCH = GLA_V + M_WIDTH + R_WIDTH

kernel_name = 'hybrid_gla_mlstm_rglru_convffn_step'

def _offsets(sizes):
    return [int(o) for o in np.cumsum(sizes)[:-1]]

def rmsnorm(x, g):
    xf = x.astype(jnp.float32)
    y = xf * lax.rsqrt(jnp.mean(xf * xf, axis=-1, keepdims=True) + EPS)
    return (y * g.astype(jnp.float32)).astype(x.dtype)

def head_rmsnorm(h, g, n_heads):
    hs = h.reshape(h.shape[:-1] + (n_heads, -1))
    hs = hs * lax.rsqrt(jnp.mean(hs * hs, axis=-1, keepdims=True) + EPS)
    return hs.reshape(h.shape) * g.astype(jnp.float32)

def blockdiag(x, w):
    nb, bs, _ = w.shape
    xb = x.reshape(x.shape[:-1] + (nb, bs))
    return jnp.einsum('blnd,nde->blne', xb, w.astype(jnp.float32)).reshape(x.shape)

def causal_dwconv(u, buf, w, b):
    width = w.shape[0]
    L = u.shape[1]
    ucat = jnp.concatenate([buf.astype(u.dtype), u], axis=1)
    w = w.astype(u.dtype)
    y = b.astype(u.dtype)
    for j in range(width):
        y = y + ucat[:, j:j + L] * w[j]
    return y, ucat[:, L:]

def _pad_time(a, n_pad, value):
    if n_pad == 0:
        return a
    pad = [(0, 0)] * a.ndim
    pad[1] = (0, n_pad)
    return jnp.pad(a, pad, constant_values=value)

def gla_chunked(q, k, v, lg, S0):
    B, L, H, DK = q.shape
    DV = v.shape[-1]
    c = min(GLA_CHUNK, L)
    n_pad = (-L) % c
    q, k, v, lg = (_pad_time(a, n_pad, 0.0) for a in (q, k, v, lg))
    nC = (L + n_pad) // c
    q, k, v, lg = (a.reshape(B, nC, c, H, a.shape[-1]) for a in (q, k, v, lg))
    bcum = jnp.cumsum(lg, axis=2)
    blast = bcum[:, :, -1:]
    q_d = q * jnp.exp(bcum)
    k_d = k * jnp.exp(-bcum)
    k_e = k * jnp.exp(blast - bcum)
    mask = jnp.tril(jnp.ones((c, c), bool))
    A = jnp.where(mask, jnp.einsum('bnihd,bnjhd->bnhij', q_d, k_d), 0.0)
    o_intra = jnp.einsum('bnhij,bnjhe->bnihe', A, v)
    dS = jnp.einsum('bnjhd,bnjhe->bnhde', k_e, v)
    decay = jnp.exp(blast[:, :, 0])

    def step(S, inp):
        dec, ds = inp
        return dec[..., None] * S + ds, S

    S_last, S_in = lax.scan(step, S0, (jnp.moveaxis(decay, 1, 0), jnp.moveaxis(dS, 1, 0)))
    S_in = jnp.moveaxis(S_in, 0, 1)
    o = o_intra + jnp.einsum('bnihd,bnhde->bnihe', q_d, S_in)
    return o.reshape(B, nC * c, H, DV)[:, :L], S_last

def mlstm_chunked(q, k, v, ig, lf, C0, n0, m0):
    B, L, H, D = q.shape
    c = min(M_CHUNK, L)
    n_pad = (-L) % c
    q, k, v, lf = (_pad_time(a, n_pad, 0.0) for a in (q, k, v, lf))
    ig = _pad_time(ig, n_pad, -jnp.inf)
    nC = (L + n_pad) // c
    chunks = lambda a: jnp.moveaxis(a.reshape((B, nC, c) + a.shape[2:]), 1, 0)
    Fcum = jnp.cumsum(lf.reshape(B, nC, c, H), axis=2)
    xs = (chunks(q), chunks(k), chunks(v), chunks(ig), jnp.moveaxis(Fcum, 1, 0))
    mask = jnp.tril(jnp.ones((c, c), bool))

    def step(carry, inp):
        C, n, m = carry
        qc, kc, vc, ic, Fc = inp
        Ft = jnp.swapaxes(Fc, 1, 2)
        it = jnp.swapaxes(ic, 1, 2)
        Dm = jnp.where(mask, Ft[..., :, None] - Ft[..., None, :] + it[..., None, :], -jnp.inf)
        b = Ft + m[..., None]
        mt = jnp.maximum(b, jnp.max(Dm, axis=-1))
        w_inter = jnp.exp(b - mt)
        P = jnp.exp(Dm - mt[..., None]) * jnp.einsum('bthd,bshd->bhts', qc, kc)
        num = (w_inter[..., None] * jnp.einsum('bthk,bhvk->bhtv', qc, C)
               + jnp.einsum('bhts,bshv->bhtv', P, vc))
        den = w_inter * jnp.einsum('bthk,bhk->bht', qc, n) + jnp.sum(P, axis=-1)
        h = num / jnp.maximum(jnp.abs(den), jnp.exp(-mt))[..., None]
        m_new = mt[..., -1]
        dec = jnp.exp(b[..., -1] - m_new)
        ws = jnp.exp(Dm[..., -1, :] - m_new[..., None])
        C_new = dec[..., None, None] * C + jnp.einsum('bhs,bshv,bshk->bhvk', ws, vc, kc)
        n_new = dec[..., None] * n + jnp.einsum('bhs,bshk->bhk', ws, kc)
        return (C_new, n_new, m_new), jnp.swapaxes(h, 1, 2)

    (C, n, m), h = lax.scan(step, (C0, n0, m0), xs)
    h = jnp.moveaxis(h, 0, 1).reshape(B, nC * c, H, D)[:, :L]
    return h, C, n, m

def rglru(xc, r, i, lam, h0):
    log_a = R_C * r * jax.nn.log_sigmoid(lam.astype(jnp.float32))
    a = jnp.exp(log_a)
    bx = jnp.sqrt(-jnp.expm1(2.0 * log_a)) * (i * xc)

    def comb(lhs, rhs):
        a1, b1 = lhs
        a2, b2 = rhs
        return a1 * a2, a2 * b1 + b2

    A, Bc = lax.associative_scan(comb, (a, bx), axis=1)
    h = Bc + A * h0[:, None]
    return h, h[:, -1]

def _layer(x, st, p):
    gS, mC, mn, mm, mconv, rh, rconv, fconv = st
    f32 = jnp.float32
    dt = x.dtype
    B, L, _ = x.shape

    xn = rmsnorm(x, p['norm_mix_g'])
    proj = (xn @ p['w_in'] + p['b_in']).astype(f32)
    gq, gk, gv, gg, ga, mu, mi, mf, mo, rx, ry, gates = jnp.split(proj, _offsets(IN_SIZES), axis=-1)

    q = gq.reshape(B, L, GLA_HEADS, GLA_DK) * (GLA_DK ** -0.5)
    k = gk.reshape(B, L, GLA_HEADS, GLA_DK)
    v = gv.reshape(B, L, GLA_HEADS, GLA_DV)
    lg = (jax.nn.log_sigmoid(ga @ p['w_gla_a2'].astype(f32) + p['b_gla_a2'].astype(f32))
          / GLA_TAU).reshape(B, L, GLA_HEADS, GLA_DK)
    o, gS_new = gla_chunked(q, k, v, lg, gS.astype(f32))
    o_gla = head_rmsnorm(o.reshape(B, L, GLA_V), p['gla_norm_g'], GLA_HEADS) * jax.nn.silu(gg)

    mcv, mconv_new = causal_dwconv(mu, mconv.astype(f32), p['mlstm_conv_w'].astype(f32), p['mlstm_conv_b'].astype(f32))
    mcv = jax.nn.silu(mcv)
    mq = blockdiag(mcv, p['w_mlstm_q']).reshape(B, L, M_HEADS, M_DH)
    mk = (blockdiag(mcv, p['w_mlstm_k']) * (M_DH ** -0.5)).reshape(B, L, M_HEADS, M_DH)
    mvv = blockdiag(mu, p['w_mlstm_v']).reshape(B, L, M_HEADS, M_DH)
    hm, mC_new, mn_new, mm_new = mlstm_chunked(mq, mk, mvv, mi, jax.nn.log_sigmoid(mf),
                                               mC.astype(f32), mn.astype(f32), mm.astype(f32))
    o_m = head_rmsnorm(hm.reshape(B, L, M_WIDTH), p['mlstm_norm_g'], M_HEADS) * jax.nn.sigmoid(mo)

    xc, rconv_new = causal_dwconv(rx, rconv.astype(f32), p['rglru_conv_w'].astype(f32), p['rglru_conv_b'].astype(f32))
    r_g = jax.nn.sigmoid(blockdiag(xc, p['w_rglru_r']) + p['b_rglru_r'].astype(f32))
    i_g = jax.nn.sigmoid(blockdiag(xc, p['w_rglru_i']) + p['b_rglru_i'].astype(f32))
    hr, rh_new = rglru(xc, r_g, i_g, p['rglru_lambda'], rh.astype(f32))
    o_r = hr * jax.nn.gelu(ry)

    wb = p['w_branch'].astype(f32)
    g3 = jax.nn.sigmoid(gates).reshape(B, L, N_BRANCH, D_MODEL)
    mix = (g3[:, :, 0] * (o_gla @ wb[:GLA_V])
           + g3[:, :, 1] * (o_m @ wb[GLA_V:GLA_V + M_WIDTH])
           + g3[:, :, 2] * (o_r @ wb[GLA_V + M_WIDTH:]))
    x = (x.astype(f32) + mix @ p['w_out'].astype(f32)).astype(dt)

    xn2 = rmsnorm(x, p['norm_ffn_g'])
    u = (xn2 @ p['w_up']).astype(f32)
    uc, fconv_new = causal_dwconv(u, fconv.astype(f32), p['ffn_conv_w'].astype(f32), p['ffn_conv_b'].astype(f32))
    u_a, u_b = jnp.split(uc, 2, axis=-1)
    x = (x.astype(f32) + (jax.nn.gelu(u_a) * u_b) @ p['w_down'].astype(f32)).astype(dt)

    new_st = [gS_new, mC_new, mn_new, mm_new, mconv_new, rh_new, rconv_new, fconv_new]
    return x, [s.astype(dt) for s in new_st]

def _trunk(x, states, weights, norm_f_g):
    per_layer = []
    for l in range(DEPTH):
        p = {name: w[l] for name, w in weights.items()}
        x, st = _layer(x, [s[l] for s in states], p)
        per_layer.append(st)
    new_states = [jnp.stack([st[j] for st in per_layer]) for j in range(len(states))]
    return rmsnorm(x, norm_f_g), new_states

def setup_inputs(seed: int = 0) -> dict:
    key = jax.random.key(seed)
    ks = jax.random.split(key, 40)
    f32 = jnp.float32

    def nrm(i, shape, s):
        return s * jax.random.normal(ks[i], shape, f32)

    b_in = nrm(12, (DEPTH, D_IN), 0.01)
    f_off = sum(IN_SIZES[:7])
    b_in = b_in.at[:, f_off:f_off + M_HEADS].add(FORGET_BIAS)
    u_lam = jax.random.uniform(ks[30], (DEPTH, R_WIDTH), f32, 0.9, 0.999)
    s_lam = u_lam ** (1.0 / R_C)
    rglru_lambda = jnp.log(s_lam) - jnp.log1p(-s_lam)
    return {
        'x_prompt': nrm(0, (BATCH, SEQ, D_MODEL), 1.0),
        'x_sample': nrm(1, (DEC_BATCH, DEC_SEQ, D_MODEL), 1.0),
        'state_gla_S': nrm(2, (DEPTH, DEC_BATCH, GLA_HEADS, GLA_DK, GLA_DV), 0.5),
        'state_mlstm_C': nrm(3, (DEPTH, DEC_BATCH, M_HEADS, M_DH, M_DH), 0.1),
        'state_mlstm_n': nrm(4, (DEPTH, DEC_BATCH, M_HEADS, M_DH), 0.1),
        'state_mlstm_m': nrm(5, (DEPTH, DEC_BATCH, M_HEADS), 1.0),
        'state_mlstm_conv': nrm(6, (DEPTH, DEC_BATCH, CONV_W - 1, M_WIDTH), 1.0),
        'state_rglru_h': nrm(7, (DEPTH, DEC_BATCH, R_WIDTH), 0.5),
        'state_rglru_conv': nrm(8, (DEPTH, DEC_BATCH, CONV_W - 1, R_WIDTH), 1.0),
        'state_ffn_conv': nrm(9, (DEPTH, DEC_BATCH, FFN_CONV_W - 1, 2 * D_FF), 1.0),
        'norm_mix_g': 1.0 + nrm(10, (DEPTH, D_MODEL), 0.05),
        'w_in': nrm(11, (DEPTH, D_MODEL, D_IN), D_MODEL ** -0.5),
        'b_in': b_in,
        'w_gla_a2': nrm(13, (DEPTH, GLA_RANK, GLA_QK), GLA_RANK ** -0.5),
        'b_gla_a2': nrm(14, (DEPTH, GLA_QK), 0.01),
        'gla_norm_g': 1.0 + nrm(15, (DEPTH, GLA_V), 0.05),
        'mlstm_conv_w': nrm(16, (DEPTH, CONV_W, M_WIDTH), CONV_W ** -0.5),
        'mlstm_conv_b': nrm(17, (DEPTH, M_WIDTH), 0.01),
        'w_mlstm_q': nrm(18, (DEPTH, M_HEADS, M_DH, M_DH), M_DH ** -0.5),
        'w_mlstm_k': nrm(19, (DEPTH, M_HEADS, M_DH, M_DH), M_DH ** -0.5),
        'w_mlstm_v': nrm(20, (DEPTH, M_HEADS, M_DH, M_DH), M_DH ** -0.5),
        'mlstm_norm_g': 1.0 + nrm(21, (DEPTH, M_WIDTH), 0.05),
        'rglru_conv_w': nrm(22, (DEPTH, CONV_W, R_WIDTH), CONV_W ** -0.5),
        'rglru_conv_b': nrm(23, (DEPTH, R_WIDTH), 0.01),
        'w_rglru_r': nrm(24, (DEPTH, R_BLOCKS, R_BS, R_BS), R_BS ** -0.5),
        'b_rglru_r': nrm(25, (DEPTH, R_WIDTH), 0.01),
        'w_rglru_i': nrm(26, (DEPTH, R_BLOCKS, R_BS, R_BS), R_BS ** -0.5),
        'b_rglru_i': nrm(27, (DEPTH, R_WIDTH), 0.01),
        'rglru_lambda': rglru_lambda,
        'w_branch': nrm(28, (DEPTH, D_BRANCH, D_MODEL), GLA_V ** -0.5),
        'w_out': nrm(29, (DEPTH, D_MODEL, D_MODEL), D_MODEL ** -0.5),
        'norm_ffn_g': 1.0 + nrm(31, (DEPTH, D_MODEL), 0.05),
        'w_up': nrm(32, (DEPTH, D_MODEL, 2 * D_FF), D_MODEL ** -0.5),
        'ffn_conv_w': nrm(33, (DEPTH, FFN_CONV_W, 2 * D_FF), FFN_CONV_W ** -0.5),
        'ffn_conv_b': nrm(34, (DEPTH, 2 * D_FF), 0.01),
        'w_down': nrm(35, (DEPTH, D_FF, D_MODEL), D_FF ** -0.5),
        'norm_f_g': 1.0 + nrm(36, (D_MODEL,), 0.05),
    }

def reference(x_prompt, x_sample, state_gla_S, state_mlstm_C, state_mlstm_n, state_mlstm_m,
              state_mlstm_conv, state_rglru_h, state_rglru_conv, state_ffn_conv,
              norm_mix_g, w_in, b_in, w_gla_a2, b_gla_a2, gla_norm_g,
              mlstm_conv_w, mlstm_conv_b, w_mlstm_q, w_mlstm_k, w_mlstm_v, mlstm_norm_g,
              rglru_conv_w, rglru_conv_b, w_rglru_r, b_rglru_r, w_rglru_i, b_rglru_i, rglru_lambda,
              w_branch, w_out, norm_ffn_g, w_up, ffn_conv_w, ffn_conv_b, w_down, norm_f_g):
    weights = {
        'norm_mix_g': norm_mix_g, 'w_in': w_in, 'b_in': b_in,
        'w_gla_a2': w_gla_a2, 'b_gla_a2': b_gla_a2, 'gla_norm_g': gla_norm_g,
        'mlstm_conv_w': mlstm_conv_w, 'mlstm_conv_b': mlstm_conv_b,
        'w_mlstm_q': w_mlstm_q, 'w_mlstm_k': w_mlstm_k, 'w_mlstm_v': w_mlstm_v,
        'mlstm_norm_g': mlstm_norm_g,
        'rglru_conv_w': rglru_conv_w, 'rglru_conv_b': rglru_conv_b,
        'w_rglru_r': w_rglru_r, 'b_rglru_r': b_rglru_r,
        'w_rglru_i': w_rglru_i, 'b_rglru_i': b_rglru_i, 'rglru_lambda': rglru_lambda,
        'w_branch': w_branch, 'w_out': w_out, 'norm_ffn_g': norm_ffn_g,
        'w_up': w_up, 'ffn_conv_w': ffn_conv_w, 'ffn_conv_b': ffn_conv_b, 'w_down': w_down,
    }
    bp = x_prompt.shape[0]
    dt = x_prompt.dtype
    zero_states = [
        jnp.zeros((DEPTH, bp, GLA_HEADS, GLA_DK, GLA_DV), dt),
        jnp.zeros((DEPTH, bp, M_HEADS, M_DH, M_DH), dt),
        jnp.zeros((DEPTH, bp, M_HEADS, M_DH), dt),
        jnp.zeros((DEPTH, bp, M_HEADS), dt),
        jnp.zeros((DEPTH, bp, CONV_W - 1, M_WIDTH), dt),
        jnp.zeros((DEPTH, bp, R_WIDTH), dt),
        jnp.zeros((DEPTH, bp, CONV_W - 1, R_WIDTH), dt),
        jnp.zeros((DEPTH, bp, FFN_CONV_W - 1, 2 * D_FF), dt),
    ]
    y_prompt, p_states = _trunk(x_prompt, zero_states, weights, norm_f_g)
    sample_states = [state_gla_S, state_mlstm_C, state_mlstm_n, state_mlstm_m,
                     state_mlstm_conv, state_rglru_h, state_rglru_conv, state_ffn_conv]
    y_sample, s_states = _trunk(x_sample, sample_states, weights, norm_f_g)
    p_gla_S, p_mlstm_C, p_mlstm_n, p_mlstm_m, p_mlstm_conv, p_rglru_h, p_rglru_conv, p_ffn_conv = p_states
    s_gla_S, s_mlstm_C, s_mlstm_n, s_mlstm_m, s_mlstm_conv, s_rglru_h, s_rglru_conv, s_ffn_conv = s_states
    return (y_prompt, y_sample,
            p_gla_S, p_mlstm_C, p_mlstm_n, p_mlstm_m, p_mlstm_conv, p_rglru_h, p_rglru_conv, p_ffn_conv,
            s_gla_S, s_mlstm_C, s_mlstm_n, s_mlstm_m, s_mlstm_conv, s_rglru_h, s_rglru_conv, s_ffn_conv)


_drawn_inputs = setup_inputs


def setup_inputs(seed=0):
    import zlib

    import numpy as np

    out = dict(_drawn_inputs(seed))
    spreads = {}
    factors = {'b_gla_a2': 8.0,
     'gla_norm_g': 3.398,
     'mlstm_conv_b': 2.931,
     'mlstm_norm_g': 3.93,
     'b_rglru_r': 22.16,
     'b_rglru_i': 8.0,
     'ffn_conv_b': 7.874}
    for name, (base, spread) in spreads.items():
        noise = np.random.default_rng([zlib.crc32(name.encode()), seed]).standard_normal(out[name].shape)
        drawn = base * np.exp(spread * noise) if base else spread * noise
        out[name] = __import__('jax').numpy.asarray(drawn.astype(out[name].dtype))
    for name, factor in factors.items():
        out[name] = (out[name] * factor).astype(out[name].dtype)
    return out
```

```python
from contextlib import ExitStack

import numpy as np

import concourse.bass as bass
from concourse import mybir

F32 = mybir.dt.float32
F32R = mybir.dt.float32r
ALU = mybir.AluOpType
ACT = mybir.ActivationFunctionType
X = mybir.AxisListType.X

P = 128
D_MODEL, SEQ, NB, LS = 1024, 512, 8, 4
TS = NB * LS
T = SEQ + TS
HT = T // 2
DK, DV, H = 64, 128, 4
RANK = 16
CHUNK = 64
NCH = SEQ // CHUNK
MCH = 128
NMC = SEQ // MCH
CW, FW = 4, 3
D_FF = 2816
NF = D_FF // P
KD = D_MODEL // P
EPS = 1e-6
NEG = -1e30

C_QKV, C_GG, C_GA = 0, 1024, 1536
C_MU = C_GA + RANK
C_MI = C_MU + 512
C_MF = C_MI + H
C_MO = C_MF + H
C_RX = C_MO + 512
C_GATE = C_RX + 1024

PW = CW - 1 + SEQ
SW = CW - 1 + LS
PADM = PW + NB * SW
CONVM = PADM - (CW - 1)
FPW = FW - 1 + SEQ
FSW = FW - 1 + LS
PADF = FPW + NB * FSW
CONVF = PADF - (FW - 1)

U_SMALL, U_QKV, U_MU, U_RX, U_RY, U_GG, U_MO, U_GB = 0, 1, 9, 13, 17, 21, 25, 29
U_OUT = U_GB + 3 * KD
U_UP = U_OUT + KD
U_DOWN = U_UP + 2 * NF
U_END = U_DOWN + 2 * KD
KT_IN, KT_GB, KT_DOWN, KT_MAX = 8, 12, 11, 12
BRANCH_ROWS = [0, 1024, 512]
GATE_OF = [0, 2, 1]

(PB_QKV, PB_MU, PB_RX, PB_RY, PB_GG, PB_MO, PB_GATE) = (0, 8, 12, 16, 20, 24, 28)
P_G2, P_GG, P_MG, P_MCW, P_MCB, P_RCW, P_RCB, P_BR, P_BI, P_LAM = 52, 60, 64, 68, 84, 88, 104, 108, 112, 116
P_FW, P_FB, P_A2 = 128, 128 + 3 * 2 * NF, 128 + 4 * 2 * NF
PAR_N = P_A2 + 2
P_G1 = PAR_N


PRAW = [(0, "b_in", C_QKV, 8), (8, "b_in", C_MU, 4), (12, "b_in", C_RX, 8), (20, "b_in", C_GG, 4), (24, "b_in", C_MO, 4),
        (28, "b_in", C_GATE, 24), (P_G2, "norm_ffn_g", 0, 8), (P_GG, "gla_norm_g", 0, 4),
        (P_MG, "mlstm_norm_g", 0, 4), (P_MCW, "mlstm_conv_w", 0, 16), (P_MCB, "mlstm_conv_b", 0, 4),
        (P_RCW, "rglru_conv_w", 0, 16), (P_RCB, "rglru_conv_b", 0, 4), (P_BR, "b_rglru_r", 0, 4),
        (P_BI, "b_rglru_i", 0, 4), (P_LAM, "rglru_lambda", 0, 4), (128, "ffn_conv_w", 0, 4 * NF),
        (256, "ffn_conv_w", 4 * NF * P, 2 * NF), (256 + 2 * NF, "ffn_conv_b", 0, 2 * NF),
        (256 + 4 * NF, "b_gla_a2", 0, 2)]
N_PRAW = len(PRAW)


def kt_of(u):
    return KT_GB if U_GB <= u < U_OUT else KT_DOWN if u >= U_DOWN else KT_IN


def layer(nc, io):
    ctx = ExitStack()
    with ctx:
        sems = {}

        def s(name):
            if name not in sems:
                sems[name] = ctx.enter_context(nc.semaphore("s_" + name))
            return sems[name]

        BASE = 16512

        def at(name, shape, off, dt=F32):
            return nc.alloc_sbuf_tensor_at(name, shape, dt, offset=BASE + off)

        def up32(n):
            return (n + 31) // 32 * 32

        TB = T * 4
        RXB = up32(4 * PADM * 4)
        RB = up32(553 * 4)
        UB = up32(2 * PADF * 4)
        stage = at("stage", [P, 2, KT_MAX, P], 0)
        whi = at("whi", [P, 2, KT_MAX, P], 12288, F32R)
        wlo = at("wlo", [P, 2, KT_MAX, P], 24576, F32R)
        xh = at("xh", [P, KD, T], 36864, F32R)
        xl = at("xl", [P, KD, T], 54272, F32R)
        o = 71680
        ident = at("ident", [P, P], o)
        ones = at("ones", [P, P], o + 512)
        par = at("par", [P, PAR_N + KD], o + 1024)
        cst = at("cst", [P, 8], o + 2304)
        o += 2336
        early = o
        gv = at("gv", [P, H, T], o)
        gg = at("gg", [P, H, T], o + 4 * TB)
        kw = at("kw", [P, H, P], o)
        vt = at("vt", [P, H, P + 1], o + 2048)
        arg = at("arg", [P, H, P], o + 4128)
        pt = at("pt", [P, H, P], o + 6176)
        ti = at("ti", [P, H, P + 1], o + 8224)
        num = at("num", [P, H, P + 1], o + 10304)
        ct = at("ct", [P, H, P + 1], o + 12384)
        qbm = at("qbm", [P, NB, TS], o + 14464)
        mus = at("mus", [P, H, TS], o + 15488)
        xt = at("xt", [P, KD, T], o)
        o += 8 * TB
        rest = o
        qk = at("qk", [P, 4, T], o)
        qz = at("qz", [P, 2, 2, T], o + 4 * TB)
        mix = at("mix", [P, KD, T], o)
        o += 8 * TB
        g1 = at("g1", [P, 2, T], o)

        kd = at("kd", [P, 2, T], o + 2 * TB)
        bc = at("bc", [P, 2, T], o + 4 * TB)
        gsq = at("gsq", [P, H, P], o + 6 * TB)
        gst = at("gst", [P, 2, P], o + 6 * TB + 2048)
        ogh = at("ogh", [P, H, T], o, F32R)
        ogl = at("ogl", [P, H, T], o + 4 * TB, F32R)
        mh = at("mh", [P, KD, T], o, F32R)
        o += 8 * TB
        rx = at("rx", [P, 4, PADM], o)
        orh = at("orh", [P, 4, PADM], o, F32R)
        o += RXB
        ry = at("ry", [P, 4, T], o)
        orl = at("orl", [P, 4, T], o, F32R)
        ml = at("ml", [P, KD, T], o - RXB, F32R)
        o += 4 * TB
        pm = at("pm", [P, 4, PADM], o)
        xs2 = at("xs2", [TS, D_MODEL], o)
        o += RXB
        w0 = o
        mcv = at("mcv", [P, H, T], o)
        mk = at("mk", [P, H, T], o + 4 * TB)
        mq = at("mq", [P, H, T], o + 8 * TB)
        mo = at("mo", [P, H, T], o + 12 * TB)
        omh = at("omh", [P, H, T], o, F32R)
        oml = at("oml", [P, H, T], o + 4 * TB, F32R)
        xtok = at("xtok", [P, 5, D_MODEL], w0)
        dt_ = at("dt", [P, 5, P], w0 + 20480)
        xp2 = at("xp2", [P, 4, D_MODEL], w0 + 8 * TB)
        rows = [at(f"row{i}", [4, 553], w0 + i * RB) for i in range(9)]
        rowf, lf, ra, rl0, ri0, rm, rF, rmm, rr = rows
        rowi = at("rowi", [4, T], w0 + 9 * RB)
        big = at("big", [P, T], w0 + 10 * RB)
        ss = at("ss", [P, 2, NB, P], w0)
        vb = at("vb", [TS, NB, P], w0 + 8192)
        qb = at("qb", [P, 2, 2, NB, TS], w0 + 12288)
        rt = [at(f"rt{i}", [P, PADM], w0 + 12288 + i * 2304) for i in range(6)]
        cts = at("cts", [P, NB, P + 1], w0)
        kwb = at("kwb", [TS, NB, P], w0 + 4128)
        m0_ = w0 + 12 * TB
        junk = at("junk", [P, D_MODEL], m0_)
        gvt = at("gvt", [CHUNK, H, DV], m0_)
        ket = at("ket", [CHUNK, 2, P], m0_ + 2048)
        gat = at("gat", [CHUNK, H, CHUNK], m0_ + 3072)
        ot = at("ot", [CHUNK, H, DV], m0_ + 4096)
        on = at("on", [CHUNK, H, DV], m0_ + 6144)
        o += 16 * TB
        negm = at("negm", [P, P], o)
        cau = at("cau", [P, P], o + 512)
        negs = at("negs", [TS, TS], o + 1024)
        caus = at("caus", [TS, TS], o + 1152)
        blk = at("blk", [TS, NB], o + 1280)
        blkc = at("blkc", [P, NB, TS], o + 1312)
        sel = at("sel", [4, H, P], o + 2336)
        wa2 = at("wa2", [RANK, 2 * P], o + 4384)
        wq = at("wq", [P, 3, H, P], o + 5408)
        bd = at("bd", [P, 2, 4, P], o + 11552)
        ch = at("ch", [P, NB, P], o + 11552)
        cols = at("cols", [P, 5, 100], o + 15648)
        ecol = at("ecol", [P, 5, 68], o + 17664)
        rowb = at("rowb", [4, T], o + 19040)
        ga = at("ga", [RANK, T], o + 21216)
        sg = at("sg", [P, T], o + 21216)
        sml = at("sml", [P, 208], o + 23392)
        ns = at("ns", [P, 2, 4, 27], o + 21216)
        rhn = at("rhn", [P, 4, 9], o + 24224)
        o += 24384
        assert BASE + o <= 229368, (BASE + o, 229368)
        ch_buf = [ch, at("ch1", [P, NB, P], w0 - RXB), at("ch2", [P, NB, P], w0 - RXB + 4096)]
        dec = sml[:, 0:32]
        dcb = sml[:, 32:80]
        nt = sml[:, 80:112]
        c4 = sml[:, 112:116]
        mstat = sml[:, 116:126]
        h0t = sml[:, 128:160]
        gsum, grs = sml[:, 160:164], sml[:, 164:168]
        mden, mrec, msum, mrs = (sml[:, 168 + 4 * i:172 + 4 * i] for i in range(4))
        lz, lz2, lp = (sml[:, 184 + 4 * i:188 + 4 * i] for i in range(3))
        m0s = sml[0:4, 196:204]
        praw = at("praw", [P, 3, P], w0 + 23040)
        craw = at("craw", [24, 2, 512], m0_ + 4096)
        graw = at("graw", [KD, P], w0 + 24576)
        r64 = at("r64", [P, T], early + 4 * TB)
        h0raw = at("h0raw", [NB, 512], early + 5 * TB)
        nraw = at("nraw", [NB * H, P], early + 5 * TB + 2048)
        f0 = rest
        hh = at("hh", [P, NF, T], f0, F32R)
        hl = at("hl", [P, NF, T], f0 + NF * TB, F32R)
        fraw = at("fraw", [2 * NB, 2 * D_FF], w0)
        f1 = f0 + 2 * NF * TB
        up = at("up", [P, 2, PADF], f1)
        ca = at("ca", [P, 2, PADF], f1 + UB)
        hp = at("hp", [P, PADF], f1 + 2 * UB)
        f2 = f1 + 2 * UB + up32(PADF * 4)
        fst = at("fst", [P, 2 * NF, 2 * NB], f2)
        fns = at("fns", [P, 2 * NF, 2 + 2 * NB], f2 + 2816)
        rstd = at("rstd", [P, T], f2 + 6016)
        ssa = at("ssa", [P, T], f2 + 6016 + TB)
        fstat = at("fstat", [P, 10], f2 + 6016 + 2 * TB)
        assert BASE + f2 + 6016 + 2 * TB + 64 <= 229368
        fout = at("fout", [2 + 2 * NB, 2 * D_FF], 36864)
        gfb = at("gfb", [P, D_MODEL], 36864 + 22528)
        yo = at("yo", [P, 2, D_MODEL], 36864 + 26624)
        rout = [at(f"rout{i}", [27, 512], w0 + 8192 + 2048 * i) for i in range(2)]
        hrow = at("hrow", [9, 512], w0)

        ps = ctx.enter_context(nc.psum_tensor("ps", [P, 8 * 512], F32))

        def pair(i):
            return ps[:, i * 1024:(i + 1) * 1024]

        def halves(i):
            return pair(i).rearrange("p (a b) -> p a b", a=2)[:, :, 0:HT]

        def split(ap):
            return ap.rearrange("p (a b) -> p a b", a=2)

        def bank(i):
            return ps[:, i * 512:(i + 1) * 512]

        def sam(ap, width=SW):
            return ap.rearrange("p (b w) -> p b w", w=width)


        def fsam(ap):
            return ap.rearrange("p (b w) -> p b w", w=FSW)

        macc = [at(f"macc{i}", [P, PADM], w0 + 8 * TB + 2304 * i) for i in range(2)]

        def each(ap, n):
            return ap.unsqueeze(2).broadcast_to([ap.shape[0], ap.shape[1], n])

        def prompt_cols(k):
            return slice(CHUNK * k, CHUNK * (k + 1)) if k < NCH else slice(SEQ, T)

        def mcols(c):
            return slice(MCH * c, MCH * (c + 1)) if c < NMC else slice(SEQ, T)

        visits = {}

        def plan(u, part, *what):
            visits.setdefault((u, part), []).extend(what)

        plan(1, 0, ("a2", 0))
        plan(3, 0, ("decays", 0))
        plan(5, 0, ("rows", 0))
        plan(8, 0, ("gprep", 0))
        for k in range(NCH + 3):
            plan(10 + k, 0, ("gla", k))
        for h in range(H):
            plan(20 + h, 0, ("gd", h))
        plan(23, 0, ("csn", 0), ("rgc", 0))
        plan(24, 0, ("gfin", 0))
        for i in range(4):
            plan(24 + 2 * i, 0, ("rg", i))
        plan(27, 0, ("cs", 0), ("cs", 1))
        plan(31, 0, ("mconv", 0))
        plan(32, 1, ("rh", 0))
        plan(32, 0, ("mprep", 0))
        plan(33, 1, ("mqk", 0))
        slots = [(33, 0)] + [(u, p) for u in range(34, U_GB + 2 * KD) for p in (1, 0)]
        seq = []
        for c in range(NMC):
            seq += [[("mA", c)], [("mB", c)], [("mC", c)]]
        seq += [[("mA", NMC)]]
        for h in range(H):
            seq += [[("sH", h)], [("sI", h)]]
        seq[-1].append(("sN", 0))
        seq += [[("mC", NMC)], [("mout", 0), ("mfin", 0)]]
        for slot, steps in zip(slots, seq):
            plan(*slot, *steps)
        assert len(slots) >= len(seq)

        ctx.enter_context(nc.allow_non_contiguous_dma(reason="a few small states and biases"))
        block = ctx.enter_context(nc.Block())

        @block.sync
        def _(sp):
            w_in, w_out, w_up, w_down = (io[n][0] for n in ("w_in", "w_out", "w_up", "w_down"))
            w_branch = io["w_branch"][0]

            def tiles(w, col, n):
                return w[:, col:col + n * P].rearrange("(k p) (m c) -> m p k c", p=P, c=P)

            def one(view, i):
                return view[bass.ds(i, 1)].rearrange("m p k c -> p (m k) c")

            def load(slot, src, kt):
                sp.dma_start(stage[:, slot, 0:kt], src).then_inc(s(f"stage{slot}"), 16)

            def free_stage(u):
                sp.wait_ge(s("lo"), u - 1)

            def load_all(u0, view, n, kt):
                with sp.Fori(0, n // 2) as i:
                    for r in range(2):
                        free_stage(i * 2 + (u0 + r))
                        load((u0 + r) % 2, one(view, i * 2 + r), kt)
                if n % 2:
                    free_stage(u0 + n - 1)
                    load((u0 + n - 1) % 2, one(view, n - 1), kt)

            sp.dma_start(graw[:], io["norm_mix_g"].rearrange("l (r c) -> (l r) c", c=P)).then_inc(s("gain_in"), 16)
            sp.wait_ge(s("cleared"), 1)
            small = w_in.rearrange("(k p) c -> p k c", p=P)
            sp.dma_start(stage[:, 0, 0:KT_IN, 0:RANK], small[:, :, C_GA:C_GA + RANK]).then_inc(s("stage0"), 16)
            sp.dma_start(stage[:, 0, 0:KT_IN, 32:32 + H], small[:, :, C_MI:C_MI + H]).then_inc(s("small_in"), 16)
            sp.dma_start(stage[:, 0, 0:KT_IN, 64:64 + H], small[:, :, C_MF:C_MF + H]).then_inc(s("small_in"), 16)
            qkv = tiles(w_in, C_QKV, 8)
            load(1, one(qkv, 0), KT_IN)
            for row, name, a, n in PRAW:
                flat = io[name].rearrange("l a b -> (l a b)") if len(io[name].shape) == 3 else \
                    io[name].rearrange("l a -> (l a)")
                sp.dma_start(praw[row % P:row % P + n, row // P, :],
                             flat[a:a + n * P].rearrange("(r c) -> r c", c=P)).then_inc(s("praw_in"), 16)
            for w, name in enumerate(("state_mlstm_conv", "state_rglru_conv")):
                sp.dma_start(craw[:, w, :], io[name][0].rearrange("b w c -> (b w) c")).then_inc(s("craw_in"), 16)
            sp.dma_start(h0raw[:], io["state_rglru_h"][0]).then_inc(s("craw_in"), 16)
            sp.dma_start(nraw[:], io["state_mlstm_n"][0].rearrange("b h d -> (b h) d")).then_inc(s("craw_in"), 16)
            sp.wait_ge(s("cleared"), 2)
            for p0, col, n in ((0, C_GA, RANK), (32, C_MI, H), (64, C_MF, H)):
                sp.dma_start(cst[p0:p0 + n, 2:3], io["b_in"].rearrange("l c -> c l")[col:col + n, :]).then_inc(s("bsmall_in"), 16)
            sp.dma_start(wa2[:], io["w_gla_a2"][0]).then_inc(s("wa2_m0_in"), 16)
            sp.dma_start(m0s, io["state_mlstm_m"].rearrange("l b h -> h (l b)")).then_inc(s("wa2_m0_in"), 16)
            load_all(2, tiles(w_in, C_QKV + P, 7), 7, KT_IN)
            load_all(U_MU, tiles(w_in, C_MU, 4), 4, KT_IN)
            for n, name in enumerate(("w_mlstm_q", "w_mlstm_k", "w_mlstm_v")):
                sp.dma_start(wq[:, n], io[name][0].rearrange("h d e -> d h e")).then_inc(s("wq_in"), 16)
            load_all(U_RX, tiles(w_in, C_RX, 8), 8, KT_IN)
            sp.wait_ge(s("cleared"), 3)
            for n, name in enumerate(("w_rglru_r", "w_rglru_i")):
                for r in range(2):
                    src = io[name][0].rearrange("(t r) d e -> r d t e", r=2)[r]
                    sp.dma_start(bd[64 * r:64 * r + 64, n, :, 64 * r:64 * r + 64], src).then_inc(s("bd_in"), 16)
            load_all(U_GG, tiles(w_in, C_GG, 4), 4, KT_IN)
            load_all(U_MO, tiles(w_in, C_MO, 4), 4, KT_IN)
            for n in range(3):
                gates = tiles(w_in, C_GATE + GATE_OF[n] * D_MODEL, KD)
                rows_ = BRANCH_ROWS[n]
                outs = w_branch[rows_:rows_ + 512, :].rearrange("(k p) (m c) -> m p k c", p=P, c=P)
                u0 = U_GB + KD * n

                def pair_of_units(i):
                    for r in range(2):
                        slot = (u0 + r) % 2
                        free_stage(i * 2 + (u0 + r))
                        load(slot, one(gates, i * 2 + r), KT_IN)
                        sp.dma_start(stage[:, slot, KT_IN:KT_GB], one(outs, i * 2 + r)).then_inc(s(f"branch{slot}"), 16)

                done = 0
                if n == 2:
                    done = 2
                    for i in range(done):
                        pair_of_units(i)
                    sp.wait_ge(s("om"), 1)
                    sp.dma_start(xp2[:], io["x_prompt"][0].rearrange("(t p) d -> p t d", p=P)).then_inc(s("late_in"), 16)
                    sp.dma_start(xs2[:], io["x_sample"].rearrange("b t d -> (b t) d")).then_inc(s("late_in"), 16)
                with sp.Fori(done, KD // 2) as i:
                    pair_of_units(i)
            load_all(U_OUT, tiles(w_out, 0, KD), 2, KT_IN)
            sp.wait_ge(s("xt"), KD)
            sp.dma_start(fraw[:], io["state_ffn_conv"][0].rearrange("b w f -> (b w) f")).then_inc(s("late_in"), 16)
            load_all(U_OUT + 2, tiles(w_out, 2 * P, KD - 2), KD - 2, KT_IN)
            ups = [tiles(w_up, 0, NF), tiles(w_up, D_FF, NF)]
            with sp.Fori(0, NF) as j:
                for r in range(2):
                    free_stage(j * 2 + (U_UP + r))
                    load((U_UP + r) % 2, one(ups[r], j), KT_IN)
            downs = [w_down[r * KT_DOWN * P:(r + 1) * KT_DOWN * P, :].rearrange("(k p) (m c) -> m p k c", p=P, c=P)
                     for r in range(2)]
            with sp.Fori(0, KD) as m:
                for r in range(2):
                    free_stage(m * 2 + (U_DOWN + r))
                    load((U_DOWN + r) % 2, one(downs[r], m), KT_DOWN)
            sp.wait_ge(s("gemm"), U_DOWN)
            sp.dma_start(gfb[:], io["norm_f_g"].partition_broadcast(P)).then_inc(s("late_in"), 16)
            for t in range(5):
                sp.wait_ge(s("y"), t + 1)
                dst = io["y_prompt"][0, t * P:(t + 1) * P, :] if t < 4 else io["y_sample"].rearrange("b t d -> (b t) d")
                sp.dma_start(dst, yo[0:P if t < 4 else TS, t % 2, :]).then_inc(s(f"yout{t % 2}"), 16)
            sp.wait_ge(s("yout0"), 48)
            sp.wait_ge(s("yout1"), 32)

        @block.gpsimd
        def _(pool):
            done = [0]

            def then(ins):
                done[0] += 1
                ins.then_inc(s("pool_step"), 1)
                pool.wait_ge(s("pool_step"), done[0])

            def pick(t, op, fill, base, pattern, mult):
                return pool.affine_select(out=t, in_=t, compare_op=op, fill=fill, base=base, pattern=pattern,
                                          channel_multiplier=mult)

            def lo(u, slot, kt):
                pool.wait_ge(s("hi"), u + 1)
                pool.tensor_tensor(wlo[:, slot, 0:kt], stage[:, slot, 0:kt], whi[:, slot, 0:kt].bitcast(F32),
                                   ALU.subtract).then_inc(s("lo"), 1)

            then(pool.memset(ident[:], 0.0))
            pick(ident[:], ALU.not_equal, 1.0, 0, [[-1, P]], 1).then_inc(s("ident"), 1)
            for u in range(2):
                lo(u, u, KT_IN)
            for t, v, fill in ((negm, 0.0, NEG), (cau, 1.0, 0.0)):
                then(pool.memset(t[:], v))
                pick(t[:], ALU.is_ge, fill, 0, [[1, P]], -1).then_inc(s("masks"), 1)
            for t, v, fill in ((negs, 0.0, NEG), (caus, 1.0, 0.0)):
                view = t[:].rearrange("p (b t) -> p b t", t=LS)
                then(pool.memset(t[:], v))
                then(pick(view, ALU.is_ge, fill, 0, [[LS, NB], [1, LS]], -1))
                pick(view, ALU.is_ge, fill, 0, [[-LS, NB], [0, LS]], 1).then_inc(s("masks"), 1)
            then(pool.memset(blk[:], 1.0))
            then(pick(blk[:], ALU.is_ge, 0.0, 0, [[-LS, NB]], 1))
            pick(blk[:], ALU.is_ge, 0.0, LS - 1, [[LS, NB]], -1).then_inc(s("masks"), 1)
            then(pool.memset(blkc[:], 0.0))
            pick(blkc[:].rearrange("p a (b t) -> p a b t", t=LS), ALU.not_equal, 1.0, 0,
                 [[1, NB], [-1, NB], [0, LS]], 0).then_inc(s("masks"), 1)
            then(pool.memset(sel[:], 0.0))
            pick(sel[:], ALU.not_equal, 1.0, 0, [[-1, H], [0, P]], 1).then_inc(s("masks"), 1)

            for u0, u1 in ((2, U_GB), (U_GB, U_OUT), (U_OUT, U_DOWN), (U_DOWN, U_END)):
                with pool.Fori(0, (u1 - u0) // 2) as i:
                    for r in range(2):
                        lo(i * 2 + (u0 + r), (u0 + r) % 2, kt_of(u0))
                if (u1 - u0) % 2:
                    lo(u1 - 1, (u1 - 1) % 2, kt_of(u0))
        @block.tensor
        def _(pe):
            mm = nc.tensor.matmul

            def tr(out, in_, k):
                return nc.tensor.transpose(out, in_, ident[0:k, 0:k])

            def gemm(dst, slot, k0, n, hi, lo, first=True, last=True):
                for k in range(n):
                    passes = ((whi, hi), (whi, lo), (wlo, hi))
                    for q, (w, x) in enumerate(passes):
                        for r in range(2):
                            ins = mm(dst[:, r, :], w[:, slot, k0 + k, :], x(k)[:, r * HT:(r + 1) * HT],
                                     start=first and k == 0 and q == 0, stop=last and k == n - 1 and q == 2)
                return ins

            def x_of(t, k0=0):
                return lambda k: t[:, k0 + k, 0:T]

            def unit(u, slot, dst, hi, lo):
                pe.wait_ge(s("lo"), u + 1)
                gemm(halves(dst), slot, 0, KT_IN, x_of(hi), x_of(lo)).then_inc(s("gemm"), 1)

            def start():
                pe.wait_ge(s("ident"), 1)
                pe.wait_ge(s("gain_in"), 16)
                tr(bank(7)[:, 0:KD], graw[:], KD).then_inc(s("par_tr"), 1)
                pe.wait_ge(s("diag"), 5)
                for j in range(KD):
                    if j == 3:
                        pe.wait_ge(s("gain"), 1)
                    if j >= 4:
                        pe.wait_ge(s("xl"), j - 3)
                    for t in range(5):
                        n = P if t < 4 else TS
                        ins = mm(pair(j % 4)[:, t * P:t * P + n], xtok[0:n, t, j * P:(j + 1) * P], dt_[0:n, t, 0:n],
                                 start=True, stop=True)
                    ins.then_inc(s("xn_mm"), 1)
                pe.wait_ge(s("lo"), 1)
                for k in range(KT_IN):
                    pe.wait_ge(s("xl"), max(k + 1, KD - 3))
                    ins = gemm(halves(0), 0, k, 1, x_of(xh, k), x_of(xl, k), first=k == 0, last=k == KT_IN - 1)
                ins.then_inc(s("gemm"), 1)
                pe.wait_ge(s("xl"), KD)
                pe.wait_ge(s("praw_in"), 16 * N_PRAW)
                n0, n1, n2 = P_LAM + 4, 2 * 2 * NF, 2 * 2 * NF + 2
                tr(bank(4)[:, 0:n0], praw[0:n0, 0, :], n0)
                tr(bank(4)[:, P:P + n1], praw[0:n1, 1, :], n1)
                tr(bank(4)[:, P + n1:PAR_N], praw[0:n2, 2, :], n2).then_inc(s("par_tr"), 1)
                pe.wait_ge(s("craw_in"), 64)
                for w in range(2):
                    for i in range(4):
                        tr(bank(5)[:, (4 * w + i) * 24:(4 * w + i) * 24 + 24], craw[0:24, w, i * P:(i + 1) * P], 24)
                for i in range(4):
                    tr(bank(5)[:, 192 + 8 * i:200 + 8 * i], h0raw[0:NB, i * P:(i + 1) * P], NB)
                tr(bank(5)[:, 224:256], nraw[0:NB * H, :], NB * H).then_inc(s("par_tr"), 1)

            def v_a2(_):
                pe.wait_ge(s("evac"), 1)
                pe.wait_ge(s("wa2_m0_in"), 32)
                pe.wait_ge(s("par"), 2)
                for j in range(2):
                    for r in range(2):
                        ins = mm(bank(4 + 2 * j + r)[:, 0:HT], wa2[:, j * P:(j + 1) * P], ga[:, r * HT:(r + 1) * HT],
                                 start=True, stop=True)
                ins.then_inc(s("a2"), 1)

            def v_rows(_):
                pe.wait_ge(s("rows"), 1)
                pe.wait_ge(s("masks"), 7)
                for c in range(NMC):
                    tr(bank(4)[:, c * 100:(c + 1) * 100], big[0:100, mcols(c)], 100)
                tr(bank(5)[0:TS, 0:100], big[0:100, SEQ:T], 100)
                for h in range(H):
                    ins = mm(bank(5)[:, P + 12 * h:P + 12 * h + 12], sel[:, h, :], rr[:, 0:12], start=True, stop=True)
                ins.then_inc(s("rows_tr"), 1)

            def v_gla(k):
                if k >= 2:
                    c = k - 2
                    n = CHUNK if c < NCH else TS
                    pe.wait_ge(s("on"), c + 1)
                    pe.wait_ge(s("gstate"), min(c + 1, NCH))
                    for h in range(H):
                        ins = tr(bank(7)[:, h * CHUNK:h * CHUNK + n], on[0:n, h, :], n)
                    ins.then_inc(s("t3"), 1)
                if 1 <= k <= NCH + 1:
                    c = k - 1
                    n = CHUNK if c < NCH else TS
                    cs = prompt_cols(c)
                    pe.wait_ge(s("gat"), c + 1)
                    pe.wait_ge(s("gvt"), c + 1)
                    pe.wait_ge(s("gstate"), c)
                    if c >= 1:
                        pe.wait_ge(s("ot"), c)
                    if c == NCH:
                        pe.wait_ge(s("qb"), 1)
                        pe.wait_ge(s("ss_in"), 16 * H)
                    for h in range(H):
                        dst = bank(6)[0:n, h * P:(h + 1) * P]
                        if c < NCH:
                            mm(dst, qz[:, h // 2, h % 2, cs], gst[:, h // 2, :], start=True, stop=False)
                        else:
                            for b in range(NB):
                                mm(dst, qb[:, h // 2, h % 2, b, :], ss[:, h // 2, b, :], start=b == 0, stop=False)
                        ins = mm(dst, gat[0:n, h, 0:n], gvt[0:n, h, :], start=False, stop=True)
                    ins.then_inc(s("t2"), 1)
                if k <= NCH:
                    n = CHUNK if k < NCH else TS
                    cs = prompt_cols(k)
                    if k == 0:
                        pe.wait_ge(s("ke"), 1)
                        pe.wait_ge(s("evac"), U_MU)
                        pe.wait_ge(s("cols"), 1)
                        pe.wait_ge(s("ecol"), 1)
                    else:
                        pe.wait_ge(s("gvt"), k)
                        pe.wait_ge(s("gat"), k)
                    for h in range(H):
                        tr(bank(4)[0:n, h * P:(h + 1) * P], gv[:, h, cs], P)
                    for j in range(2):
                        tr(bank(5)[0:n, j * P:(j + 1) * P], qk[:, 2 + j, cs], P)
                    for j in range(2):
                        dst = bank(5)[0:n, 256 + j * P:256 + (j + 1) * P].rearrange("p (r t) -> p r t", r=2)[:, :, 0:n]
                        ins = mm(dst, kd[:, j, cs], qz[:, j, :, cs], start=True, stop=True)
                    ins.then_inc(s("t1"), 1)
                if 1 <= k <= NCH:
                    if k >= 2:
                        pe.wait_ge(s("t3_copied"), k - 1)
                    for j in range(2):
                        ins = mm(bank(7)[:, j * 256:(j + 1) * 256], ket[:, j, :], gvt[:, 2 * j:2 * j + 2, :],
                                 start=True, stop=True)
                    ins.then_inc(s("ds"), 1)

            def v_gd(h):
                pe.wait_ge(s("vb"), h + 1)
                if h:
                    pe.wait_ge(s("ss_new"), h)
                else:
                    pe.wait_ge(s("gvt"), NCH + 1)
                    pe.wait_ge(s("gat"), NCH + 1)
                for g in range(2):
                    ins = mm(bank(4 + g), ket[0:TS, h // 2, :], vb[:, 4 * g:4 * g + 4, :], start=True, stop=True)
                ins.then_inc(s("sds"), 1)

            def v_cs(w):
                pe.wait_ge(s("ns"), 1)
                pe.wait_ge(s("rg_copied"), 2)
                for i in range(4):
                    ins = tr(bank(4 + w)[0:27, i * P:(i + 1) * P], ns[:, w, i, :], P)
                ins.then_inc(s("state_tr"), 1)

            def v_rg(i):
                pe.wait_ge(s("xc"), i + 1)
                if i == 0:
                    pe.wait_ge(s("bd_in"), 64)
                    pe.wait_ge(s("ss_new"), H)
                    pe.wait_ge(s("t3_copied"), NCH + 1)
                else:
                    pe.wait_ge(s("rg_copied"), i)
                if i == 2:
                    pe.wait_ge(s("state_rows"), 2)
                for w in range(2):
                    for r in range(2):
                        n = CONVM // 2
                        ins = mm(bank(4 + 2 * w + r)[:, 0:n], bd[:, w, i, :], rt[i % 2][:, r * n:(r + 1) * n],
                                 start=True, stop=True)
                ins.then_inc(s("rg_mm"), 1)

            def v_rh(_):
                pe.wait_ge(s("or"), 4)
                pe.wait_ge(s("rg_copied"), 4)
                for i in range(4):
                    ins = tr(bank(4)[0:9, i * P:(i + 1) * P], rhn[:, i, :], P)
                ins.then_inc(s("state_tr"), 1)

            def v_mqk(_):
                pe.wait_ge(s("wq_in"), 48)
                pe.wait_ge(s("state_rows"), 3)
                for h in range(H):
                    pe.wait_ge(s("mcv"), h + 1)
                    for w in range(2):
                        if h:
                            pe.wait_ge(s("mq" if w == 0 else "mk"), h)
                        for r in range(2):
                            ins = mm(bank(4 + 2 * w + r)[:, 0:HT], wq[:, w, h, :], mcv[:, h, r * HT:(r + 1) * HT],
                                     start=True, stop=True)
                        ins.then_inc(s("mqk_mm"), 1)

            def v_mA(c):
                n = MCH if c < NMC else TS
                cs = mcols(c)
                if c == 0:
                    pe.wait_ge(s("mq"), H)
                    pe.wait_ge(s("mk"), H)
                else:
                    pe.wait_ge(s("mC"), c)
                    pe.wait_ge(s("m3_copied"), c)
                for h in range(H):
                    tr(bank(4)[0:n, h * P:(h + 1) * P], mk[:, h, cs], P)
                for h in range(H):
                    x = pm[:, h, CW - 1 + MCH * c:CW - 1 + MCH * (c + 1)] if c < NMC else mus[:, h, :]
                    mm(bank(5)[0:n, h * P:(h + 1) * P], x, wq[:, 2, h, :], start=True, stop=True)
                for h in range(H):
                    mm(bank(6)[0:n, h * P:h * P + n], mk[:, h, cs], mq[:, h, cs], start=True, stop=True)
                for h in range(H):
                    ins = mm(bank(7)[0:n, h * P:h * P + n], sel[:, h, 0:n], rowb[:, cs], start=True, stop=True)
                ins.then_inc(s("mA"), 1)

            def v_mB(c):
                pe.wait_ge(s("pt"), c + 1)
                pe.wait_ge(s("mkv"), c + 1)
                for h in range(H):
                    mm(bank(4 + h // 2)[:, (h % 2) * 129:(h % 2) * 129 + 129], pt[:, h, :], vt[:, h, :],
                       start=True, stop=True)
                if c:
                    pe.wait_ge(s("mC"), c)
                else:
                    pe.wait_ge(s("ct0"), 1)
                for h in range(H):
                    ins = mm(bank(6 + h // 2)[:, (h % 2) * 129:(h % 2) * 129 + 129], mq[:, h, mcols(c)], ct[:, h, :],
                             start=True, stop=True)
                ins.then_inc(s("mB"), 1)

            def v_mC(c):
                n = MCH if c < NMC else TS
                pe.wait_ge(s("num"), c + 1)
                if c < NMC:
                    for h in range(H):
                        ins = mm(bank(4 + h // 2)[:, (h % 2) * 129:(h % 2) * 129 + 129], kw[:, h, :], vt[:, h, :],
                                 start=True, stop=True)
                    ins.then_inc(s("mU"), 1)
                pe.wait_ge(s("hn"), c + 1)
                for h in range(H):
                    ins = tr(bank(6)[:, h * P:h * P + n], ti[0:n, h, 0:P], n)
                ins.then_inc(s("m3"), 1)

            def v_sH(h):
                pe.wait_ge(s(f"ch_in{h}"), 16)
                if h == 0:
                    pe.wait_ge(s("mkv"), NMC + 1)
                    pe.wait_ge(s("pt"), NMC + 1)
                else:
                    pe.wait_ge(s("ch_new"), h)
                for b in range(NB):
                    ins = tr(ps[:, 2048 + b * P:2048 + (b + 1) * P], ch_buf[h % 3][:, b, :], P)
                ins.then_inc(s("ch_tr"), 1)

            def v_sI(h):
                pe.wait_ge(s("cts"), 2 * h + 2)
                pe.wait_ge(s("qbm"), h + 1)
                if h:
                    pe.wait_ge(s("snum"), h)
                for b in range(NB):
                    mm(bank(6)[0:TS, 0:129], qbm[:, b, :], cts[:, b, :], start=b == 0, stop=b == NB - 1)
                mm(bank(7)[0:TS, 0:129], pt[0:TS, h, 0:TS], vt[0:TS, h, :], start=True, stop=True)
                mm(bank(7)[:, 256:256 + NB], kw[0:TS, h, :], blk[:], start=True, stop=True)
                for g in range(2):
                    ins = mm(bank(4 + g), vt[0:TS, h, 0:P], kwb[:, 4 * g:4 * g + 4, :], start=True, stop=True)
                ins.then_inc(s("sI"), 1)

            def v_mout(_):
                pe.wait_ge(s("ch_new"), H)
                pe.wait_ge(s("m3_copied"), NMC + 1)
                for h in range(H):
                    tr(bank(4)[:, h * P:(h + 1) * P], ct[:, h, 0:P], P)
                tr(bank(5)[0:H, 0:P], ct[:, :, P], P)
                tr(bank(5)[0:NB * H, P:2 * P], nt, P).then_inc(s("state_tr"), 1)

            def nothing(_):
                pass

            parts = {"a2": v_a2, "csn": nothing, "decays": nothing, "rgc": nothing, "mconv": nothing, "rows": v_rows, "gprep": nothing, "gla": v_gla, "gd": v_gd, "gfin": nothing,
                     "cs": v_cs, "rg": v_rg, "rh": v_rh, "mprep": nothing, "mqk": v_mqk, "mA": v_mA, "mB": v_mB,
                     "mC": v_mC, "sH": v_sH, "sI": v_sI, "sN": nothing, "mout": v_mout, "mfin": nothing}

            def visit(u, part):
                for what, k in visits.get((u, part), []):
                    parts[what](k)

            def gb_unit(n, slot, hi, lo, u, between):
                pe.wait_ge(s("lo"), u + 1)
                if not isinstance(n, int) or n:
                    pe.wait_ge(s("gate_ev"), n)
                gemm(halves(0), slot, 0, KT_IN, x_of(xh), x_of(xl)).then_inc(s("gate_mm"), 1)
                between()
                if not isinstance(n, int) or n:
                    pe.wait_ge(s("br_ev"), n)
                gemm(halves(1), slot, KT_IN, 4, x_of(hi), x_of(lo)).then_inc(s("gemm"), 1)

            start()
            for u in range(1, U_GB):
                if u >= 2:
                    pe.wait_ge(s("evac"), u - 1)
                unit(u, u % 2, u % 2, xh, xl)
                visit(u, 0)
            pe.wait_ge(s("evac"), U_GB)
            for n in range(2 * KD):
                u = U_GB + n

                def between():
                    visit(u, 1)
                    if n == 0:
                        pe.wait_ge(s("og"), 1)
                    if n == KD:
                        pe.wait_ge(s("or"), 4)

                gb_unit(n, u % 2, *((ogh, ogl) if n < KD else (orh, orl)), u, between)
                visit(u, 0)
            with pe.Fori(0, KD // 2) as i:
                for r in range(2):
                    gb_unit(i * 2 + (2 * KD + r), (U_GB + r) % 2, omh, oml, i * 2 + (U_GB + 2 * KD + r),
                            lambda: pe.wait_ge(s("om"), 1))

            pe.wait_ge(s("late_in"), 32)
            pe.wait_ge(s("state_rows"), 5)
            for j in range(KD):
                if j >= 2:
                    pe.wait_ge(s("xt"), j - 1)
                for t in range(4):
                    tr(pair(2 + j % 2)[:, t * P:(t + 1) * P], xp2[:, t, j * P:(j + 1) * P], P)
                tr(pair(2 + j % 2)[:, SEQ:T], xs2[:, j * P:(j + 1) * P], TS).then_inc(s("xt_tr"), 1)

            pe.wait_ge(s("ml"), KD)
            pe.wait_ge(s("br_ev"), 3 * KD)
            pe.wait_ge(s("gate_ev"), 3 * KD)
            for m in range(2):
                unit(U_OUT + m, (U_OUT + m) % 2, m, mh, ml)
            pe.wait_ge(s("late_in"), 48)
            pe.wait_ge(s("xt"), KD)
            for f in range(2 * NF):
                g, q = f // 32, f % 32
                ins = tr(bank(4 + g)[:, q * 16:q * 16 + 16], fraw[:, f * P:(f + 1) * P], 2 * NB)
            ins.then_inc(s("fst_tr"), 1)
            with pe.Fori(0, KD // 2 - 1) as i:
                for r in range(2):
                    pe.wait_ge(s("x1"), i * 2 + (r + 1))
                    unit(i * 2 + (U_OUT + 2 + r), (U_OUT + r) % 2, r, mh, ml)

            pe.wait_ge(s("x1"), KD)
            pe.wait_ge(s("xl2"), KD)
            unit(U_UP, U_UP % 2, 0, xh, xl)
            pe.wait_ge(s("ssa"), KD + 1)
            pe.wait_ge(s("fst"), 2)
            for r in range(2):
                ins = mm(halves(2)[:, r, :], ones[:], ssa[:, r * HT:(r + 1) * HT], start=True, stop=True)
            ins.then_inc(s("ss_mm"), 1)
            unit(U_UP + 1, (U_UP + 1) % 2, 1, xh, xl)
            with pe.Fori(0, NF - 1) as j:
                for r in range(2):
                    pe.wait_ge(s("uev"), j * 2 + (r + 1))
                    unit(j * 2 + (U_UP + 2 + r), (U_UP + r) % 2, r, xh, xl)

            def down(m, half, dst):
                pe.wait_ge(s("lo"), m * 2 + (U_DOWN + half + 1))
                gemm(halves(dst), (U_DOWN + half) % 2, 0, KT_DOWN, x_of(hh, half * KT_DOWN), x_of(hl, half * KT_DOWN),
                     first=half == 0, last=half == 1).then_inc(s("gemm"), 1)

            for m in range(2):
                pe.wait_ge(s("uev"), 2 * NF - 1 + m)
                if m == 0:
                    pe.wait_ge(s("hl"), KT_DOWN)
                down(m, 0, m)
                if m == 0:
                    pe.wait_ge(s("hl"), NF)
                down(m, 1, m)
            pe.wait_ge(s("fns"), 2 * NF)
            pe.wait_ge(s("rstd"), 1)
            for g in range(6):
                if g >= 2:
                    pe.wait_ge(s("fout"), g - 1)
                for q in range(8 if g < 5 else 2 * NF - 40):
                    ins = tr(pair(2 + g % 2)[0:2 + 2 * NB, q * P:(q + 1) * P], fns[:, 8 * g + q, :], P)
                ins.then_inc(s("fns_tr"), 1)
            with pe.Fori(0, KD // 2 - 1) as i:
                for r in range(2):
                    pe.wait_ge(s("x2"), i * 2 + (r + 1))
                    down(i * 2 + (r + 2), 0, r)
                    down(i * 2 + (r + 2), 1, r)

            pe.wait_ge(s("x2"), KD)
            pe.wait_ge(s("fout"), 6)
            for t in range(5):
                n = P if t < 4 else TS
                if t >= 2:
                    pe.wait_ge(s("y"), t - 1)
                for j in range(KD):
                    ins = tr(pair(2 + t % 2)[0:n, j * P:(j + 1) * P], xt[:, j, t * P:t * P + n], P)
                ins.then_inc(s("y_tr"), 1)
        @block.scalar
        def _(act):
            func = nc.scalar.activation
            done = [0]

            def then(ins):
                done[0] += 1
                ins.then_inc(s("act_step"), 1)
                act.wait_ge(s("act_step"), done[0])

            eps, one = cst[:, 0:1], cst[:, 1:2]
            outs = [0]

            def store(dst, src, eng=None):
                outs[0] += 16
                (eng or act).dma_start(dst, src).then_inc(s("out"), 16)

            def hi(u):
                slot, kt = u % 2, kt_of(u)
                act.wait_ge(s(f"stage{slot}"), 16 * (u // 2 + 1))
                if u == 0:
                    act.wait_ge(s("small_in"), 32)
                if kt == KT_GB:
                    act.wait_ge(s(f"branch{slot}"), 16 * ((u - U_GB - (u - U_GB) % 2) // 2 + 1))
                if u >= 2:
                    act.wait_ge(s("gemm"), u - 1)
                func(whi[:, slot, 0:kt], stage[:, slot, 0:kt], ACT.Copy).then_inc(s("hi"), 1)

            def hi_at(k, u0, kt):
                slot = u0 % 2
                act.wait_ge(s(f"stage{slot}"), k * 16 + 16 * (u0 // 2 + 1))
                if kt == KT_GB:
                    act.wait_ge(s(f"branch{slot}"), k * 16 + 16 * ((u0 - U_GB) // 2 + 1))
                act.wait_ge(s("gemm"), k * 2 + (u0 - 1))
                func(whi[:, slot, 0:kt], stage[:, slot, 0:kt], ACT.Copy).then_inc(s("hi"), 1)

            for t in range(4):
                act.dma_start(xtok[:, t, :], io["x_prompt"][0, t * P:(t + 1) * P, :]).then_inc(s(f"tokens{t}"), 16)
            act.dma_start(xtok[0:TS, 4, :], io["x_sample"].rearrange("b t d -> (b t) d")).then_inc(s("tokens4"), 16)
            act.wait_ge(s("cleared"), 2)
            func(cst[:, 3:4], one, ACT.Sqrt)
            for t in range(5):
                n = P if t < 4 else TS
                act.wait_ge(s(f"tokens{t}"), 16)
                then(func(junk[0:n], xtok[0:n, t, :], ACT.Square, accum_out=mstat[0:n, t:t + 1]))
            hi(0)
            hi(1)
            then(func(mstat[:, 5:9], mstat[:, 0:4], ACT.Sqrt, bias=eps, scale=1.0 / D_MODEL))
            func(mstat[0:TS, 9:10], mstat[0:TS, 4:5], ACT.Sqrt, bias=eps[0:TS], scale=1.0 / D_MODEL).then_inc(s("rms"), 1)
            act.wait_ge(s("gain"), 1)
            for j in range(KD):
                act.wait_ge(s("xn_mm"), j + 1)
                func(xh[:, j, :], pair(j % 4)[:, 0:T], ACT.Copy, scale=par[:, P_G1 + j:P_G1 + j + 1]).then_inc(s("xh"), 1)

            def to_padded(dst, src, bias):
                func(dst[:, CW - 1:CW - 1 + HT], src[:, 0, :], ACT.Identity, bias=bias)
                func(dst[:, CW - 1 + HT:PW], src[:, 1, 0:SEQ - HT], ACT.Identity, bias=bias)
                return func(sam(dst[:, PW:PADM])[:, :, CW - 1:SW], src[:, 1, SEQ - HT:HT].rearrange("p (b t) -> p b t", t=LS),
                            ACT.Identity, bias=bias)

            def evac(u):
                src = halves(u % 2)
                act.wait_ge(s("gemm"), u + 1)
                if u == U_SMALL:
                    act.wait_ge(s("bsmall_in"), 48)
                    act.wait_ge(s("xl"), KD)
                    func(split(ga[:]), src[0:RANK], ACT.Identity, bias=cst[0:RANK, 2:3])
                    func(split(rowi[:]), src[32:32 + H], ACT.Identity, bias=cst[32:32 + H, 2:3])
                    ins = func(split(rowf[:, 0:T]), src[64:64 + H], ACT.Identity, bias=cst[64:64 + H, 2:3])
                elif u < U_MU:
                    i = u - U_QKV
                    if i == 0:
                        act.wait_ge(s("par"), 2)
                    dst = qk[:, i, :] if i < 4 else gv[:, i - 4, :]
                    ins = func(split(dst), src, ACT.Identity, bias=par[:, PB_QKV + i:PB_QKV + i + 1])
                elif u < U_RX:
                    i = u - U_MU
                    ins = to_padded(pm[:, i, :], src, par[:, PB_MU + i:PB_MU + i + 1])
                elif u < U_RY:
                    i = u - U_RX
                    ins = to_padded(rx[:, i, :], src, par[:, PB_RX + i:PB_RX + i + 1])
                elif u < U_GG:
                    i = u - U_RY
                    ins = func(split(ry[:, i, :]), src, ACT.Gelu_apprx_tanh, bias=par[:, PB_RY + i:PB_RY + i + 1])
                elif u < U_MO:
                    i = u - U_GG
                    ins = func(split(gg[:, i, :]), src, ACT.Silu, bias=par[:, PB_GG + i:PB_GG + i + 1])
                else:
                    i = u - U_MO
                    if i == 0:
                        act.wait_ge(s("og"), 1)
                        act.wait_ge(s("ss_new"), H)
                    ins = func(split(mo[:, i, :]), src, ACT.Sigmoid, bias=par[:, PB_MO + i:PB_MO + i + 1])
                ins.then_inc(s("evac"), 1)

            a2v = ps[:, 2048:4096].rearrange("p (j a b) -> p j a b", j=2, a=2)[:, :, :, 0:HT]

            def v_a2(_):
                act.wait_ge(s("a2"), 1)
                for j in range(2):
                    func(split(g1[:, j, :]), a2v[:, j], ACT.Abs, bias=par[:, P_A2 + j:P_A2 + j + 1]).then_inc(s("g_abs"), 1)
                act.wait_ge(s("g_abs"), 2)
                func(lz, par[:, P_LAM:P_LAM + 4], ACT.Abs)
                then(func(ra[:, 0:T], rowf[:, 0:T], ACT.Abs))
                func(g1[:], g1[:], ACT.Exp, scale=-1.0)
                func(lz, lz, ACT.Exp, scale=-1.0).then_inc(s("lam"), 1)
                then(func(ra[:, 0:T], ra[:, 0:T], ACT.Exp, scale=-1.0))
                func(g1[:], g1[:], ACT.Ln, bias=one).then_inc(s("g_ln"), 1)
                func(ra[:, 0:T], ra[:, 0:T], ACT.Ln, bias=one[0:4]).then_inc(s("row_ln"), 1)

            def v_decays(_):
                act.wait_ge(s("bc"), 2)
                func(g1[:], bc[:], ACT.Exp, scale=1.0 / 16).then_inc(s("decays"), 1)
                func(kd[:], bc[:], ACT.Exp, scale=-1.0 / 16).then_inc(s("decays"), 1)

            def v_rows(_):
                act.wait_ge(s("cols"), 1)
                func(dcb, bank(5)[:, P:P + 48], ACT.Exp)
                func(ecol[:, 0:4, :], cols[:, 0:4, 32:100], ACT.Exp)
                func(ecol[0:TS, 4, :], cols[0:TS, 4, 32:100], ACT.Exp).then_inc(s("ecol"), 1)
                store(io["p_mlstm_m"].rearrange("l b h -> h (l b)"), rm[:, SEQ:SEQ + 1])
                store(io["s_mlstm_m"].rearrange("l b h -> h (l b)"), rm[:, SEQ + 5:SEQ + 5 * NB + 1:5])

            def v_gprep(_):
                act.wait_ge(s("out"), outs[0])
                for h in range(H):
                    act.dma_start(ss[64 * (h % 2):64 * (h % 2) + 64, h // 2], io["state_gla_S"][0].rearrange("b h k v -> h k b v")[h])\
                       .then_inc(s("ss_in"), 16)
                act.wait_ge(s("db"), 1)
                func(g1[:], g1[:], ACT.Exp, scale=1.0 / 16).then_inc(s("ee"), 1)
                for j in range(2):
                    func(dec[:, 16 * j:16 * j + NCH], bc[:, j, CHUNK - 1:SEQ:CHUNK], ACT.Exp, scale=1.0 / 16)
                    ins = func(dec[:, 16 * j + NCH:16 * j + 16], bc[:, j, SEQ + LS - 1:T:LS], ACT.Exp, scale=1.0 / 16)
                ins.then_inc(s("dec"), 1)

            def v_gla(k):
                if k >= 2:
                    c = k - 2
                    n = CHUNK if c < NCH else TS
                    act.wait_ge(s("t3"), c + 1)
                    func(gv[:, :, prompt_cols(c)], bank(7)[:, 0:H * CHUNK].rearrange("p (h t) -> p h t", h=H)[:, :, 0:n],
                         ACT.Copy).then_inc(s("t3_copied"), 1)
                if 1 <= k <= NCH + 1:
                    c = k - 1
                    n = CHUNK if c < NCH else TS
                    act.wait_ge(s("t2"), c + 1)
                    if c:
                        act.wait_ge(s("on"), c)
                    func(ot[0:n], bank(6)[0:n].rearrange("p (h d) -> p h d", h=H), ACT.Copy).then_inc(s("ot"), 1)
                if k <= NCH:
                    n = CHUNK if k < NCH else TS
                    act.wait_ge(s("t1"), k + 1)
                    if k:
                        act.wait_ge(s("ds"), k)
                    func(ket[0:n], bank(5)[0:n, 0:2 * P].rearrange("p (j d) -> p j d", j=2), ACT.Copy).then_inc(s("ket"), 1)
                    func(gvt[0:n], bank(4)[0:n].rearrange("p (h d) -> p h d", h=H), ACT.Copy).then_inc(s("gvt"), 1)
                if 1 <= k <= NCH + 1:
                    c = k - 1
                    n = CHUNK if c < NCH else TS
                    act.wait_ge(s("gsum"), c + 1)
                    func(grs[0:n], gsum[0:n], ACT.Sqrt, bias=eps[0:n], scale=1.0 / DV).then_inc(s("grs"), 1)
                if k == NCH:
                    act.wait_ge(s("gstate"), NCH)
                    for r in range(2):
                        store(io["p_gla_S"][0, 0].rearrange("(j r) k v -> r k j v", r=2)[r], gst[64 * r:64 * r + 64])

            def v_cs(w):
                act.wait_ge(s("state_tr"), w + 1)
                r = rout[w]
                func(r[:], bank(4 + w)[0:27], ACT.Copy).then_inc(s("state_rows"), 1)
                act.wait_ge(s("state_rows"), w + 1)
                name = ("mlstm_conv", "rglru_conv")[w]
                store(io["p_" + name][0, 0], r[0:3])
                store(io["s_" + name][0].rearrange("b w c -> (b w) c"), r[3:27])

            def v_gfin(_):
                act.wait_ge(s("out"), outs[0])
                act.nop().then_inc(s("stored"), 1)
                act.wait_ge(s("ss_new"), H)
                for h in range(H):
                    store(io["s_gla_S"][0].rearrange("b h k v -> h k b v")[h], ss[64 * (h % 2):64 * (h % 2) + 64, h // 2])

            def v_rg(i):
                act.wait_ge(s("rg_mm"), i + 1)
                if i:
                    act.wait_ge(s("rg_o"), i)
                c0 = CONVM // 2
                v = [pair(2 + w).rearrange("p (a b) -> p a b", a=2)[:, :, 0:c0] for w in range(2)]
                func(rt[2][:, 0:CONVM].rearrange("p (a b) -> p a b", a=2), v[0], ACT.Sigmoid, bias=par[:, P_BR + i:P_BR + i + 1])
                func(rt[3][:, 0:CONVM].rearrange("p (a b) -> p a b", a=2), v[1], ACT.Sigmoid, bias=par[:, P_BI + i:P_BI + i + 1])\
                    .then_inc(s("rg_copied"), 1)
                act.wait_ge(s("rg_copied"), i + 1)
                act.wait_ge(s("c4"), 1)
                then(func(rt[2][:, 0:CONVM], rt[2][:, 0:CONVM], ACT.Tanh, scale=c4[:, i:i + 1]))
                func(rt[4][:, 0:CONVM], rt[2][:, 0:CONVM], ACT.Sqrt).then_inc(s("rg_u"), 1)

            def v_rh(_):
                act.wait_ge(s("out"), outs[0])
                act.wait_ge(s("state_tr"), 3)
                func(hrow[:], bank(4)[0:9], ACT.Copy).then_inc(s("state_rows"), 1)
                act.wait_ge(s("state_rows"), 3)
                store(io["p_rglru_h"][0], hrow[0:1])
                store(io["s_rglru_h"][0], hrow[1:9])

            def v_mprep(_):
                act.wait_ge(s("out"), outs[0])
                for h in range(H):
                    act.wait_ge(s("mconv"), h + 1)
                    acc = macc[h % 2]
                    func(mcv[:, h, 0:SEQ], acc[:, 0:SEQ], ACT.Silu)
                    func(mcv[:, h, SEQ:T].rearrange("p (b t) -> p b t", t=LS),
                         acc[:, PW:PW + NB * SW].rearrange("p (b w) -> p b w", w=SW)[:, :, 0:LS], ACT.Silu).then_inc(s("mcv"), 1)

            def v_mqk(_):
                for h in range(H):
                    act.wait_ge(s("mqk_mm"), 2 * h + 1)
                    if h == 0:
                        act.wait_ge(s("mcv"), H)
                    func(split(mq[:, h, :]), halves(2), ACT.Copy).then_inc(s("mq"), 1)
                act.dma_start(ch_buf[0][:], io["state_mlstm_C"][0].rearrange("b h v k -> h v b k")[0])\
                   .then_inc(s("ch_in0"), 16)

            def v_mA(c):
                n = MCH if c < NMC else TS
                act.wait_ge(s("mA"), c + 1)
                if c:
                    act.wait_ge(s("mU"), min(c, NMC))
                for h in range(H):
                    func(kw[0:n, h, :], bank(4)[0:n, h * P:(h + 1) * P], ACT.Copy, scale=ecol[0:n, c, 64 + h:65 + h])
                func(vt[0:n, :, 0:P], bank(5)[0:n].rearrange("p (h d) -> p h d", h=H), ACT.Copy).then_inc(s("mkv"), 1)
                act.wait_ge(s("arg"), c + 1)
                for h in range(H):
                    ins = func(arg[0:n, h, 0:n], arg[0:n, h, 0:n], ACT.Exp, bias=cols[0:n, c, h:h + 1])
                ins.then_inc(s("mE"), 1)

            def rms_of(c, n):
                act.wait_ge(s("msum"), c + 1)
                func(mrs[0:n], msum[0:n], ACT.Sqrt, bias=eps[0:n], scale=1.0 / P).then_inc(s("mrs"), 1)

            def v_mB(c):
                rms_of(c, MCH)

            def v_mC(c):
                n = MCH if c < NMC else TS
                act.wait_ge(s("m3"), c + 1)
                func(mq[:, :, mcols(c)], bank(6).rearrange("p (h t) -> p h t", h=H)[:, :, 0:n], ACT.Copy)\
                    .then_inc(s("m3_copied"), 1)

            def v_sH(h):
                if h == 0:
                    act.wait_ge(s("mkv"), NMC + 1)
                    for q in (1, 2):
                        act.dma_start(ch_buf[q][:], io["state_mlstm_C"][0].rearrange("b h v k -> h v b k")[q])\
                           .then_inc(s(f"ch_in{q}"), 16)
                if h == 1:
                    act.wait_ge(s("ch_out"), 16)
                    act.dma_start(ch_buf[0][:], io["state_mlstm_C"][0].rearrange("b h v k -> h v b k")[3])\
                       .then_inc(s("ch_in3"), 16)
                act.wait_ge(s("ch_tr"), h + 1)
                if h:
                    act.wait_ge(s("sI"), h)
                func(cts[:, :, 0:P], ps[:, 2048:3072].rearrange("p (b k) -> p b k", b=NB), ACT.Copy).then_inc(s("cts"), 1)

            def v_sI(h):
                act.wait_ge(s("ch_new"), h + 1)
                act.dma_start(io["s_mlstm_C"][0].rearrange("b h v k -> h v b k")[h], ch_buf[h % 3][:])\
                   .then_inc(s("ch_out"), 16)


            def v_sN(_):
                rms_of(NMC, TS)

            def v_mout(_):
                act.wait_ge(s("state_tr"), 4)
                act.wait_ge(s("hn"), NMC + 1)
                func(arg[:], bank(4).rearrange("p (h k) -> p h k", h=H), ACT.Copy).then_inc(s("state_rows"), 1)
                func(pt[0:NB * H, 0:2, :], bank(5)[0:NB * H, 0:2 * P].rearrange("p (a k) -> p a k", a=2), ACT.Copy)\
                    .then_inc(s("state_rows"), 1)
                act.wait_ge(s("state_rows"), 5)
                store(io["p_mlstm_C"][0, 0].rearrange("h v k -> v h k"), arg[:])
                store(io["p_mlstm_n"][0, 0], pt[0:H, 0, :])
                store(io["s_mlstm_n"][0].rearrange("b h k -> (b h) k"), pt[0:NB * H, 1, :])

            def v_mfin(_):
                act.wait_ge(s("ch_out"), 64)
                act.wait_ge(s("gated"), 1)
                func(omh[:], mq[:], ACT.Copy).then_inc(s("branch_hi"), 1)

            def nothing(_):
                pass

            parts = {"a2": v_a2, "csn": nothing, "decays": v_decays, "rgc": nothing, "mconv": nothing, "rows": v_rows, "gprep": v_gprep, "gla": v_gla, "gd": nothing, "gfin": v_gfin,
                     "cs": v_cs, "rg": v_rg, "rh": v_rh, "mprep": v_mprep, "mqk": v_mqk, "mA": v_mA, "mB": v_mB,
                     "mC": v_mC, "sH": v_sH, "sI": v_sI, "sN": v_sN, "mout": v_mout, "mfin": v_mfin}

            def visit(u, part):
                for what, k in visits.get((u, part), []):
                    parts[what](k)

            for u in range(U_GB):
                act.wait_ge(s("gemm"), u + 1)
                hi(u + 2)
                evac(u)
                visit(u, 0)

            def gate(n, col):
                act.wait_ge(s("gate_mm"), n + 1)
                if not isinstance(n, int) or n:
                    act.wait_ge(s("br_ev"), n)
                func(split(sg[:]), halves(0), ACT.Sigmoid, bias=col).then_inc(s("gate_ev"), 1)

            for n in range(2 * KD):
                u = U_GB + n
                g = PB_GATE + GATE_OF[n // KD] * KD + n % KD
                gate(n, par[:, g:g + 1])
                visit(u, 1)
                act.wait_ge(s("gemm"), u + 1)
                hi(u + 2)
                visit(u, 0)

            def gb_mlstm(i, r, hi_next):
                gate(i * 2 + (2 * KD + r), par[:, bass.ds(i * 2 + (PB_GATE + KD + r), 1)])
                hi_next()
                act.wait_ge(s("br_ev"), i * 2 + (2 * KD + r + 1))
                func(mh[:, bass.ds(i * 2 + r, 1), :], mix[:, bass.ds(i * 2 + r, 1), :], ACT.Copy).then_inc(s("mh"), 1)

            u0 = U_GB + 2 * KD
            with act.Fori(0, KD // 2 - 1) as i:
                for r in range(2):
                    gb_mlstm(i, r, lambda: hi_at(i, u0 + 2 + r, KT_GB))
            for r in range(2):
                i = KD // 2 - 1
                gate(i * 2 + (2 * KD + r), par[:, PB_GATE + KD + 2 * i + r:PB_GATE + KD + 2 * i + r + 1])
                hi(U_OUT + r)
                act.wait_ge(s("br_ev"), 3 * KD - 1 + r)
                func(mh[:, 2 * i + r, :], mix[:, 2 * i + r, :], ACT.Copy).then_inc(s("mh"), 1)

            act.wait_ge(s("out"), outs[0])
            act.nop().then_inc(s("stored"), 1)
            with act.Fori(0, KD // 2) as i:
                for r in range(2):
                    hi_at(i, U_OUT + 2 + r, KT_IN)
                    m = bass.ds(i * 2 + r, 1)
                    act.wait_ge(s("x1"), i * 2 + (r + 1))
                    act.wait_ge(s("ssa"), i * 2 + (r + 1))
                    func(hp[:, 0:T], xt[:, m, :].rearrange("p a t -> p (a t)"), ACT.Square).then_inc(s("sq"), 1)
                    func(xh[:, m, :], xt[:, m, :], ACT.Copy, scale=par[:, bass.ds(i * 2 + (P_G2 + r), 1)])\
                        .then_inc(s("xh2"), 1)

            def up_hi(j):
                act.wait_ge(s("prod"), j + 1)
                dst = hh[:, bass.ds(j, 1), :].rearrange("p a t -> p (a t)")
                func(dst[:, 0:SEQ], hp[:, 0:SEQ], ACT.Copy)
                func(dst[:, SEQ:T].rearrange("p (b t) -> p b t", t=LS),
                     fsam(hp[:, FPW:PADF])[:, :, 0:LS], ACT.Copy).then_inc(s("hh"), 1)

            def gelu(j):
                act.wait_ge(s("ca"), j * 2 + 1)
                func(ca[:, 0, 0:CONVF], ca[:, 0, 0:CONVF], ACT.Gelu_apprx_tanh).then_inc(s("gelu"), 1)

            hi(U_UP + 2)
            act.wait_ge(s("ss_mm"), 1)
            func(split(rstd[:]), halves(2), ACT.Sqrt, bias=eps, scale=1.0 / D_MODEL).then_inc(s("std"), 1)
            hi(U_UP + 3)
            gelu(0)
            up_hi(0)
            with act.Fori(1, NF - 1) as j:
                for r in range(2):
                    hi_at(j, U_UP + 2 + r, KT_IN)
                gelu(j)
                up_hi(j)
            for r in range(2):
                hi(U_DOWN + r)
            gelu(NF - 1)
            up_hi(NF - 1)
            for r in range(2, 6):
                hi(U_DOWN + r)
            for g in range(6):
                n = (8 if g < 5 else 2 * NF - 40) * P
                act.wait_ge(s("fns_tr"), g + 1)
                func(fout[:, 8 * g * P:8 * g * P + n], pair(2 + g % 2)[0:2 + 2 * NB, 0:n], ACT.Copy).then_inc(s("fout"), 1)
            act.wait_ge(s("fout"), 6)
            store(io["p_ffn_conv"][0, 0], fout[0:2])
            store(io["s_ffn_conv"][0].rearrange("b w f -> (b w) f"), fout[2:2 + 2 * NB])
            with act.Fori(0, (U_END - U_DOWN) // 2 - 3) as i:
                for r in range(2):
                    hi_at(i, U_DOWN + 6 + r, KT_DOWN)
            act.wait_ge(s("gemm"), U_END)
            for t in range(5):
                n = P if t < 4 else TS
                act.wait_ge(s("y_tr"), t + 1)
                then(func(stage[0:n, 0, 0:8, :].rearrange("p k c -> p (k c)"), pair(2 + t % 2)[0:n], ACT.Square,
                          accum_out=fstat[0:n, t:t + 1]))
                func(fstat[0:n, 5 + t:6 + t], fstat[0:n, t:t + 1], ACT.Sqrt, bias=eps[0:n], scale=1.0 / D_MODEL)\
                    .then_inc(s("yrms"), 1)
            act.wait_ge(s("out"), outs[0])
        @block.vector
        def _(dve):
            v = nc.vector
            done = [0]

            def then(ins):
                done[0] += 1
                ins.then_inc(s("dve_step"), 1)
                dve.wait_ge(s("dve_step"), done[0])

            def conv(out, row, n, taps, w, b):
                then(v.tensor_scalar(out, row[:, 0:n], w(0), b, ALU.mult, ALU.add))
                for j in range(1, taps):
                    ins = v.scalar_tensor_tensor(out=out, in0=row[:, j:j + n], scalar=w(j), in1=out,
                                                 op0=ALU.mult, op1=ALU.add)
                    if j < taps - 1:
                        then(ins)
                return ins

            v.memset(stage[:, 0, 0:KT_IN], 0.0).then_inc(s("cleared"), 1)
            v.memset(cst[:, 0:1], EPS)
            v.memset(cst[:, 2:3], 0.0)
            v.memset(cst[:, 1:2], 1.0).then_inc(s("cleared"), 1)
            v.memset(bd[:], 0.0).then_inc(s("cleared"), 1)
            v.memset(ones[:], 1.0)
            v.memset(pm[:, :, 0:CW - 1], 0.0)
            v.memset(rx[:, :, 0:CW - 1], 0.0)
            v.memset(qz[0:64, :, 1, :], 0.0)
            v.memset(qz[64:P, :, 0, :], 0.0)
            then(v.memset(gst[:], 0.0))
            dve.wait_ge(s("par_tr"), 1)
            v.tensor_copy(par[:, P_G1:P_G1 + KD], bank(7)[:, 0:KD]).then_inc(s("gain"), 1)
            dve.wait_ge(s("rms"), 1)
            dve.wait_ge(s("ident"), 1)
            v.reciprocal(mstat[:, 5:9], mstat[:, 5:9])
            then(v.reciprocal(mstat[0:TS, 9:10], mstat[0:TS, 9:10]))
            for t in range(5):
                n = P if t < 4 else TS
                v.tensor_scalar(dt_[0:n, t, :], ident[0:n, :], mstat[0:n, 5 + t:6 + t], None, ALU.mult).then_inc(s("diag"), 1)
            for j in range(KD):
                dve.wait_ge(s("xh"), j + 1)
                v.scalar_tensor_tensor(out=xl[:, j, :], in0=pair(j % 4)[:, 0:T], scalar=par[:, P_G1 + j:P_G1 + j + 1],
                                       in1=xh[:, j, :].bitcast(F32), op0=ALU.mult, op1=ALU.subtract).then_inc(s("xl"), 1)
            dve.wait_ge(s("par_tr"), 2)
            v.tensor_copy(par[:, 0:P_LAM + 4], bank(4)[:, 0:P_LAM + 4])
            v.tensor_copy(par[:, P:PAR_N], bank(4)[:, P:PAR_N]).then_inc(s("par"), 1)
            dve.wait_ge(s("par_tr"), 3)
            for w, dst in enumerate((pm, rx)):
                for i in range(4):
                    c = (4 * w + i) * 24
                    v.tensor_copy(sam(dst[:, i, PW:PADM])[:, :, 0:CW - 1],
                                  bank(5)[:, c:c + 24].rearrange("p (b w) -> p b w", w=CW - 1))
            v.tensor_copy(h0t, bank(5)[:, 192:224])
            v.tensor_copy(nt, bank(5)[:, 224:256]).then_inc(s("par"), 1)
            dve.wait_ge(s("par"), 2)
            then(v.memset(r64[:], 1.0))
            then(v.memset(r64[:, 0:SEQ:CHUNK], 0.0))
            then(v.memset(r64[:, SEQ:T:LS], 0.0))

            a2v = ps[:, 2048:4096].rearrange("p (j a b) -> p j a b", j=2, a=2)[:, :, :, 0:HT]

            def v_a2(_):
                dve.wait_ge(s("g_abs"), 2)
                for j in range(2):
                    ins = v.tensor_scalar(split(kd[:, j, :]), a2v[:, j], par[:, P_A2 + j:P_A2 + j + 1], 0.0, ALU.add, ALU.min)
                then(ins)
                dve.wait_ge(s("g_ln"), 1)
                then(v.tensor_tensor(kd[:], kd[:], g1[:], ALU.subtract))
                for j in range(2):
                    v.tensor_tensor_scan(bc[:, j, :], r64[:], kd[:, j, :], 0.0, ALU.mult, ALU.add).then_inc(s("bc"), 1)
                dve.wait_ge(s("lam"), 1)
                then(v.tensor_scalar(lz2, lz, 2.0, None, ALU.add))
                then(v.reciprocal(lz2, lz2))
                then(v.tensor_tensor(lz, lz, lz2, ALU.mult))
                then(v.tensor_tensor(lz2, lz, lz, ALU.mult))
                then(v.tensor_scalar(lp, lz2, 1.0 / 17, None, ALU.mult))
                for k in range(15, 1, -2):
                    then(v.scalar_tensor_tensor(out=lp, in0=lp, scalar=1.0 / k, in1=lz2, op0=ALU.add, op1=ALU.mult))
                then(v.scalar_tensor_tensor(out=lp, in0=lp, scalar=1.0, in1=lz, op0=ALU.add, op1=ALU.mult))
                then(v.tensor_scalar(lz2, par[:, P_LAM:P_LAM + 4], 0.0, -4.0, ALU.min, ALU.mult))
                v.scalar_tensor_tensor(out=c4, in0=lp, scalar=8.0, in1=lz2, op0=ALU.mult, op1=ALU.add).then_inc(s("c4"), 1)

            def tokens(ap, off=0):
                return (ap[:, off:off + SEQ].rearrange("p (c t) -> p c t", t=MCH),
                        ap[:, off + SEQ:off + T].rearrange("p (b t) -> p b t", t=LS))

            def v_rows(_):
                then(v.memset(big[:], 0.0))
                then(v.memset(rl0[:], NEG))
                then(v.memset(ri0[:], 0.0))
                then(v.memset(rr[:], 1.0))
                then(v.memset(rr[:, 0:SEQ:MCH], 0.0))
                then(v.memset(rr[:, SEQ:T:LS], 0.0))
                dve.wait_ge(s("evac"), 1)
                dve.wait_ge(s("row_ln"), 1)
                then(v.tensor_scalar(lf[:, 0:T], rowf[:, 0:T], 0.0, None, ALU.min))
                then(v.tensor_tensor(lf[:, 0:T], lf[:, 0:T], ra[:, 0:T], ALU.subtract))
                m0 = [x[:, 1 + SEQ:1 + SEQ + 5 * NB].rearrange("p (b w) -> p b w", w=LS + 1) for x in (rl0, ri0, rm)]
                v.tensor_copy(rl0[:, 1:1 + SEQ], lf[:, 0:SEQ])
                v.tensor_copy(m0[0][:, :, 1:], tokens(lf)[1])
                v.tensor_copy(ri0[:, 1:1 + SEQ], rowi[:, 0:SEQ])
                dve.wait_ge(s("wa2_m0_in"), 32)
                v.tensor_copy(m0[1][:, :, 0:1], m0s.unsqueeze(2))
                then(v.tensor_copy(m0[1][:, :, 1:], tokens(rowi)[1]))
                then(v.tensor_tensor_scan(rm[:], rl0[:], ri0[:], 0.0, ALU.add, ALU.max))
                then(v.tensor_tensor_scan(rF[:, 0:T], rr[:, 0:T], lf[:, 0:T], 0.0, ALU.mult, ALU.add))
                v.tensor_copy(rmm[:, 0:SEQ], rm[:, 1:1 + SEQ])
                then(v.tensor_copy(tokens(rmm)[1], m0[2][:, :, 1:]))
                then(v.tensor_tensor(rowb[:], rF[:, 0:T], rmm[:, 0:T], ALU.subtract))
                then(v.tensor_tensor(big[0:4], rowi[:], rF[:, 0:T], ALU.subtract))
                before = (rm[:, 0:SEQ:MCH], rm[:, 1 + SEQ:1 + SEQ + 5 * NB:5])
                last = (rowb[:, MCH - 1:SEQ:MCH], rowb[:, SEQ + LS - 1:T:LS])
                for q, n in ((0, MCH), (1, LS)):
                    v.tensor_tensor(tokens(big[32:36])[q], tokens(rowb)[q], each(before[q], n), ALU.add)
                    v.tensor_tensor(tokens(big[96:100])[q], tokens(big[0:4])[q], each(last[q], n), ALU.add)
                v.tensor_scalar(big[64:68], rmm[:, 0:T], -1.0, None, ALU.mult)
                v.tensor_tensor(rr[:, 0:NMC], last[0], before[0], ALU.add)
                v.tensor_tensor(rr[:, NMC:NMC + NB], last[1], before[1], ALU.add).then_inc(s("rows"), 1)
                dve.wait_ge(s("rows_tr"), 1)
                v.tensor_copy(cols[:, 0:4, :], bank(4)[:, 0:400].rearrange("p (c x) -> p c x", c=4))
                v.tensor_copy(cols[0:TS, 4, :], bank(5)[0:TS, 0:100]).then_inc(s("cols"), 1)

            def v_gprep(_):
                dve.wait_ge(s("evac"), U_MU)
                dve.wait_ge(s("decays"), 1)
                for r in range(2):
                    q = slice(64 * r, 64 * r + 64)
                    v.scalar_tensor_tensor(out=qz[q, :, r, :], in0=qk[q, 0:2, :], scalar=float(DK) ** -0.5, in1=g1[q],
                                           op0=ALU.mult, op1=ALU.mult).then_inc(s("qz"), 1)
                dve.wait_ge(s("qz"), 2)
                dve.wait_ge(s("decays"), 2)
                v.tensor_tensor(kd[:], qk[:, 2:4, :], kd[:], ALU.mult)
                for j in range(2):
                    v.tensor_tensor(g1[:, j, 0:SEQ].rearrange("p (c t) -> p c t", t=CHUNK),
                                    each(bc[:, j, CHUNK - 1:SEQ:CHUNK], CHUNK),
                                    bc[:, j, 0:SEQ].rearrange("p (c t) -> p c t", t=CHUNK), ALU.subtract)
                    ins = v.tensor_tensor(g1[:, j, SEQ:T].rearrange("p (c t) -> p c t", t=LS),
                                          each(bc[:, j, SEQ + LS - 1:T:LS], LS),
                                          bc[:, j, SEQ:T].rearrange("p (c t) -> p c t", t=LS), ALU.subtract)
                ins.then_inc(s("db"), 1)
                dve.wait_ge(s("ee"), 1)
                v.tensor_tensor(qk[:, 2:4, :], qk[:, 2:4, :], g1[:], ALU.mult).then_inc(s("ke"), 1)

            def v_gla(k):
                if k <= NCH:
                    n = CHUNK if k < NCH else TS
                    dve.wait_ge(s("ket"), k + 1)
                    if k == 0:
                        dve.wait_ge(s("masks"), 7)
                    if k:
                        dve.wait_ge(s("t2"), k)
                    mask = cau[0:n, 0:n] if k < NCH else caus[:]
                    a = bank(5)[0:n, 256:512].rearrange("p (h t) -> p h t", h=H)[:, :, 0:n]
                    v.tensor_tensor(gat[0:n, :, 0:n], a, mask.unsqueeze(1).broadcast_to([n, H, n]), ALU.mult)\
                        .then_inc(s("gat"), 1)
                if 1 <= k <= NCH:
                    dve.wait_ge(s("ds"), k)
                    if k == 1:
                        dve.wait_ge(s("dec"), 1)
                    for j in range(2):
                        for r in range(2):
                            q = slice(64 * r, 64 * r + 64)
                            ins = v.scalar_tensor_tensor(out=gst[q, j, :], in0=gst[q, j, :],
                                                         scalar=dec[q, 16 * j + k - 1:16 * j + k],
                                                         in1=bank(7)[q, (2 * j + r) * P:(2 * j + r + 1) * P],
                                                         op0=ALU.mult, op1=ALU.add)
                    ins.then_inc(s("gstate"), 1)
                    dve.wait_ge(s("gstate"), k)
                if k == NCH:
                    for h in range(H):
                        q = qz[:, h // 2, h % 2, SEQ:T].unsqueeze(1).broadcast_to([P, NB, TS])
                        ins = v.tensor_tensor(qb[:, h // 2, h % 2], q, blkc[:], ALU.mult)
                    ins.then_inc(s("qb"), 1)
                if 1 <= k <= NCH + 1:
                    c = k - 1
                    n = CHUNK if c < NCH else TS
                    dve.wait_ge(s("ot"), c + 1)
                    then(v.tensor_tensor(gsq[0:n], ot[0:n], ot[0:n], ALU.mult))
                    v.tensor_reduce(gsum[0:n], gsq[0:n], X, ALU.add).then_inc(s("gsum"), 1)
                    dve.wait_ge(s("grs"), c + 1)
                    then(v.reciprocal(grs[0:n], grs[0:n]))
                    if c:
                        dve.wait_ge(s("t3"), c)
                    v.tensor_tensor(on[0:n], ot[0:n], each(grs[0:n], DV), ALU.mult).then_inc(s("on"), 1)

            def v_csn(_):
                dve.wait_ge(s("evac"), U_RY)
                for w, src in enumerate((pm, rx)):
                    for i in range(4):
                        v.tensor_copy(ns[:, w, i, 0:3], src[:, i, SEQ:PW])
                        ins = v.tensor_copy(ns[:, w, i, 3:27].rearrange("p (b w) -> p b w", w=3),
                                            sam(src[:, i, PW:PADM])[:, :, LS:SW])
                ins.then_inc(s("ns"), 1)

            def v_gd(h):
                if h == 0:
                    dve.wait_ge(s("t2"), NCH + 1)
                    dve.wait_ge(s("gvt"), NCH + 1)
                else:
                    dve.wait_ge(s("sds"), h)
                v.tensor_tensor(vb[:], gvt[0:TS, h, :].unsqueeze(1).broadcast_to([TS, NB, DV]), each(blk[:], DV), ALU.mult)\
                    .then_inc(s("vb"), 1)
                j, q = h // 2, slice(64 * (h % 2), 64 * (h % 2) + 64)
                then(v.tensor_tensor(ss[q, j], ss[q, j], each(dec[q, 16 * j + NCH:16 * j + 16], DV), ALU.mult))
                dve.wait_ge(s("sds"), h + 1)
                v.tensor_tensor(ss[q, j], ss[q, j], ps[q, 2048:3072].rearrange("p (b v) -> p b v", b=NB), ALU.add)\
                    .then_inc(s("ss_new"), 1)

            def v_gfin(_):
                dve.wait_ge(s("evac"), U_MO)
                dve.wait_ge(s("t3_copied"), NCH + 1)
                for h in range(H):
                    ins = v.scalar_tensor_tensor(out=gv[:, h, :], in0=gv[:, h, :], scalar=par[:, P_GG + h:P_GG + h + 1],
                                                 in1=gg[:, h, :], op0=ALU.mult, op1=ALU.mult)
                then(ins)
                then(v.tensor_copy(ogh[:], gv[:]))
                dve.wait_ge(s("stored"), 1)
                v.tensor_tensor(ogl[:], gv[:], ogh[:].bitcast(F32), ALU.subtract).then_inc(s("og"), 1)

            def v_rgc(i):
                dve.wait_ge(s("evac"), U_RY)
                if i == 0:
                    dve.wait_ge(s("t2"), NCH + 1)
                conv(rt[i % 2][:, 0:CONVM], rx[:, i, :], CONVM, CW, lambda j: par[:, P_RCW + 4 * j + i:P_RCW + 4 * j + i + 1],
                     par[:, P_RCB + i:P_RCB + i + 1]).then_inc(s("xc"), 1)
                dve.wait_ge(s("xc"), i + 1)

            def v_rg(i):
                if i < 3:
                    v_rgc(i + 1)
                xc = rt[i % 2][:, 0:CONVM]
                a, h, b, r = (t[:, 0:CONVM] for t in rt[2:])
                dve.wait_ge(s("rg_u"), i + 1)
                if i:
                    dve.wait_ge(s("or"), i)
                then(v.tensor_scalar(r, a, 1.0, None, ALU.add))
                then(v.reciprocal(r, r))
                then(v.scalar_tensor_tensor(out=a, in0=a, scalar=1.0, in1=r, op0=ALU.subtract, op1=ALU.mult, reverse0=True))
                v.tensor_tensor(h, h, xc, ALU.mult)
                then(v.scalar_tensor_tensor(out=b, in0=b, scalar=2.0, in1=r, op0=ALU.mult, op1=ALU.mult))
                then(v.tensor_tensor(b, b, h, ALU.mult))
                v.memset(rt[2][:, PW - 1:PW - 1 + 7 * NB:SW], 0.0)
                then(v.tensor_copy(rt[4][:, PW - 1:PW - 1 + 7 * NB:SW], h0t[:, NB * i:NB * i + NB]))
                then(v.tensor_tensor_scan(h, a, b, 0.0, ALU.mult, ALU.add))
                v.tensor_copy(rhn[:, i, 0:1], h[:, SEQ - 1:SEQ])
                v.tensor_copy(rhn[:, i, 1:9], rt[3][:, PW + LS - 1:PADM:SW])
                v.tensor_tensor(r[:, 0:SEQ], h[:, 0:SEQ], ry[:, i, 0:SEQ], ALU.mult)
                v.tensor_tensor(r[:, SEQ:T].rearrange("p (b t) -> p b t", t=LS), sam(rt[3][:, PW:PADM])[:, :, 0:LS],
                                ry[:, i, SEQ:T].rearrange("p (b t) -> p b t", t=LS), ALU.mult).then_inc(s("rg_o"), 1)
                dve.wait_ge(s("rg_o"), i + 1)
                then(v.tensor_copy(orh[:, i, 0:T], rt[5][:, 0:T]))
                v.tensor_tensor(orl[:, i, :], rt[5][:, 0:T], orh[:, i, 0:T].bitcast(F32), ALU.subtract).then_inc(s("or"), 1)

            def v_mconv(_):
                for h in range(H):
                    if h >= 2:
                        dve.wait_ge(s("mcv"), h - 1)
                    conv(macc[h % 2][:, 0:CONVM], pm[:, h, :], CONVM, CW,
                         lambda j: par[:, P_MCW + 4 * j + h:P_MCW + 4 * j + h + 1],
                         par[:, P_MCB + h:P_MCB + h + 1]).then_inc(s("mconv"), 1)

            def v_mprep(_):
                for h in range(H):
                    v.tensor_copy(mus[:, h, :].rearrange("p (b t) -> p b t", t=LS), sam(pm[:, h, PW:PADM])[:, :, CW - 1:SW])
                v.memset(vt[:, :, P:P + 1], 1.0)
                v.memset(ct[:], 0.0).then_inc(s("ct0"), 1)
                dve.wait_ge(s("ct0"), 1)

            def v_mqk(_):
                for h in range(H):
                    dve.wait_ge(s("mqk_mm"), 2 * h + 2)
                    v.tensor_scalar(split(mk[:, h, :]), halves(3), float(P) ** -0.5, None, ALU.mult).then_inc(s("mk"), 1)

            def v_mA(c):
                n = MCH if c < NMC else TS
                dve.wait_ge(s("mA"), c + 1)
                if c:
                    dve.wait_ge(s("mB"), c)
                mask = negm[:] if c < NMC else negs[:]
                v.tensor_tensor(arg[0:n, :, 0:n], bank(7)[0:n].rearrange("p (h t) -> p h t", h=H)[:, :, 0:n],
                                mask.unsqueeze(1).broadcast_to([n, H, n]), ALU.add).then_inc(s("arg"), 1)
                dve.wait_ge(s("mE"), c + 1)
                v.tensor_tensor(pt[0:n, :, 0:n], arg[0:n, :, 0:n],
                                bank(6)[0:n].rearrange("p (h t) -> p h t", h=H)[:, :, 0:n], ALU.mult).then_inc(s("pt"), 1)

            def head_out(c, n):
                then(v.scalar_tensor_tensor(out=mden[0:n], in0=num[0:n, :, P], scalar=-1.0, in1=num[0:n, :, P],
                                            op0=ALU.mult, op1=ALU.max))
                then(v.tensor_tensor(mden[0:n], mden[0:n], ecol[0:n, c, 32:36], ALU.max))
                then(v.reciprocal(mrec[0:n], mden[0:n]))
                then(v.tensor_tensor(arg[0:n], num[0:n, :, 0:P], num[0:n, :, 0:P], ALU.mult))
                then(v.tensor_reduce(msum[0:n], arg[0:n], X, ALU.add))
                then(v.tensor_tensor(msum[0:n], msum[0:n], mrec[0:n], ALU.mult))
                v.tensor_tensor(msum[0:n], msum[0:n], mrec[0:n], ALU.mult).then_inc(s("msum"), 1)
                dve.wait_ge(s("mrs"), c + 1)
                then(v.reciprocal(mrs[0:n], mrs[0:n]))
                then(v.tensor_tensor(mrec[0:n], mrec[0:n], mrs[0:n], ALU.mult))
                v.tensor_tensor(ti[0:n, :, 0:P], num[0:n, :, 0:P], each(mrec[0:n], P), ALU.mult).then_inc(s("hn"), 1)

            def v_mB(c):
                dve.wait_ge(s("mB"), c + 1)
                if c:
                    dve.wait_ge(s("m3"), c)
                for g in range(2):
                    w = each(ecol[:, c, 2 * g:2 * g + 2], P + 1)
                    ins = v.tensor_tensor(ti[:, 2 * g:2 * g + 2, :], bank(6 + g)[:, 0:258].rearrange("p (h x) -> p h x", h=2), w,
                                          ALU.mult)
                then(ins)
                for g in range(2):
                    ins = v.tensor_tensor(num[:, 2 * g:2 * g + 2, :], ti[:, 2 * g:2 * g + 2, :],
                                          bank(4 + g)[:, 0:258].rearrange("p (h x) -> p h x", h=2), ALU.add)
                ins.then_inc(s("num"), 1)
                dve.wait_ge(s("num"), c + 1)
                head_out(c, MCH)

            def v_mC(c):
                if c < NMC:
                    dve.wait_ge(s("mU"), c + 1)
                    for h in range(H):
                        ins = v.scalar_tensor_tensor(out=ct[:, h, :], in0=ct[:, h, :], scalar=dcb[:, 12 * h + c:12 * h + c + 1],
                                                     in1=bank(4 + h // 2)[:, (h % 2) * 129:(h % 2) * 129 + 129],
                                                     op0=ALU.mult, op1=ALU.add)
                    ins.then_inc(s("mC"), 1)
                    dve.wait_ge(s("mC"), c + 1)

            def v_sH(h):
                if h:
                    dve.wait_ge(s("sI"), h)
                dve.wait_ge(s("mqk_mm"), 2 * H)
                v.tensor_copy(cts[:, :, P], nt.rearrange("p (b h) -> p b h", h=H)[:, :, h]).then_inc(s("cts"), 1)
                v.tensor_tensor(kwb[:], kw[0:TS, h, :].unsqueeze(1).broadcast_to([TS, NB, P]), each(blk[:], P), ALU.mult)
                v.tensor_tensor(qbm[:], mq[:, h, SEQ:T].unsqueeze(1).broadcast_to([P, NB, TS]), blkc[:], ALU.mult)\
                    .then_inc(s("qbm"), 1)

            def v_sI(h):
                d = dcb[:, 12 * h + NMC:12 * h + NMC + NB]
                nh = nt.rearrange("p (b h) -> p b h", h=H)[:, :, h]
                c_ = ch_buf[h % 3]
                dve.wait_ge(s("ch_tr"), h + 1)
                then(v.tensor_tensor(c_[:], c_[:], each(d, P), ALU.mult))
                then(v.tensor_tensor(nh, nh, d, ALU.mult))
                dve.wait_ge(s("sI"), h + 1)
                v.tensor_tensor(nh, nh, bank(7)[:, 256:256 + NB], ALU.add)
                then(v.tensor_scalar(ti[0:TS, h, :], bank(6)[0:TS, 0:129], ecol[0:TS, NMC, h:h + 1], None, ALU.mult))
                v.tensor_tensor(num[0:TS, h, :], ti[0:TS, h, :], bank(7)[0:TS, 0:129], ALU.add).then_inc(s("snum"), 1)
                v.tensor_tensor(c_[:], c_[:], ps[:, 2048:3072].rearrange("p (b k) -> p b k", b=NB), ALU.add)\
                    .then_inc(s("ch_new"), 1)

            def v_sN(_):
                dve.wait_ge(s("snum"), H)
                dve.wait_ge(s("m3"), NMC)
                head_out(NMC, TS)
                v.nop().then_inc(s("num"), 1)

            def v_mfin(_):
                dve.wait_ge(s("evac"), U_GB)
                dve.wait_ge(s("m3_copied"), NMC + 1)
                for h in range(H):
                    ins = v.scalar_tensor_tensor(out=mq[:, h, :], in0=mq[:, h, :], scalar=par[:, P_MG + h:P_MG + h + 1],
                                                 in1=mo[:, h, :], op0=ALU.mult, op1=ALU.mult)
                ins.then_inc(s("gated"), 1)
                dve.wait_ge(s("branch_hi"), 1)
                dve.wait_ge(s("mqk_mm"), 2 * H)
                v.tensor_tensor(oml[:], mq[:], omh[:].bitcast(F32), ALU.subtract).then_inc(s("om"), 1)

            def nothing(_):
                pass

            parts = {"a2": v_a2, "csn": v_csn, "decays": nothing, "rgc": v_rgc, "mconv": v_mconv, "rows": v_rows, "gprep": v_gprep, "gla": v_gla, "gd": v_gd, "gfin": v_gfin,
                     "cs": nothing, "rg": v_rg, "rh": nothing, "mprep": v_mprep, "mqk": v_mqk, "mA": v_mA, "mB": v_mB,
                     "mC": v_mC, "sH": v_sH, "sI": v_sI, "sN": v_sN, "mout": nothing, "mfin": v_mfin}

            def visit(u, part):
                for what, k in visits.get((u, part), []):
                    parts[what](k)

            for u in range(U_GB):
                visit(u, 0)

            def mixed(n, u, dst, add):
                dve.wait_ge(s("gemm"), u + 1)
                dve.wait_ge(s("gate_ev"), n + 1)
                if not add:
                    v.tensor_tensor(split(dst), split(sg[:]), halves(1), ALU.mult).then_inc(s("br_ev"), 1)
                    return
                v.tensor_tensor(split(sg[:]), split(sg[:]), halves(1), ALU.mult).then_inc(s("br_mul"), 1)
                dve.wait_ge(s("br_mul"), n + (1 - KD))
                v.tensor_tensor(dst, dst, sg[:], ALU.add).then_inc(s("br_ev"), 1)

            for n in range(2 * KD):
                visit(U_GB + n, 1)
                mixed(n, U_GB + n, mix[:, n % KD, :], n >= KD)
                visit(U_GB + n, 0)
            with dve.Fori(0, KD // 2) as i:
                for r in range(2):
                    n = i * 2 + (2 * KD + r)
                    m = bass.ds(i * 2 + r, 1)
                    mixed(n, i * 2 + (U_GB + 2 * KD + r), mix[:, m, :].rearrange("p a t -> p (a t)"), True)
                    dve.wait_ge(s("mh"), i * 2 + (r + 1))
                    v.tensor_tensor(ml[:, m, :], mix[:, m, :], mh[:, m, :].bitcast(F32), ALU.subtract).then_inc(s("ml"), 1)

            dve.wait_ge(s("stored"), 2)
            for j in range(KD):
                dve.wait_ge(s("xt_tr"), j + 1)
                v.tensor_copy(xt[:, j, :], pair(2 + j % 2)[:, 0:T]).then_inc(s("xt"), 1)
            v.memset(up[:, :, 0:FW - 1], 0.0)
            v.memset(ssa[:], 0.0).then_inc(s("ssa"), 1)

            def residual(k, r):
                m = bass.ds(k * 2 + r, 1) if not isinstance(k, int) else slice(2 * k + r, 2 * k + r + 1)
                dve.wait_ge(s("gemm"), k * 2 + (U_OUT + r + 1))
                x = xt[:, m, :].rearrange("p a t -> p (a t)")
                v.tensor_tensor(split(x), split(x), halves(r), ALU.add).then_inc(s("x1"), 1)
                dve.wait_ge(s("x1"), k * 2 + (r + 1))
                dve.wait_ge(s("sq"), k * 2 + (r + 1))
                v.tensor_tensor(ssa[:], ssa[:], hp[:, 0:T], ALU.add).then_inc(s("ssa"), 1)
                dve.wait_ge(s("xh2"), k * 2 + (r + 1))
                g = par[:, bass.ds(k * 2 + (P_G2 + r), 1)] if not isinstance(k, int) else par[:, P_G2 + 2 * k + r:P_G2 + 2 * k + r + 1]
                v.scalar_tensor_tensor(out=xl[:, m, :].rearrange("p a t -> p (a t)"), in0=x, scalar=g,
                                       in1=xh[:, m, :].rearrange("p a t -> p (a t)").bitcast(F32),
                                       op0=ALU.mult, op1=ALU.subtract).then_inc(s("xl2"), 1)
                dve.wait_ge(s("ssa"), k * 2 + (r + 2))

            for r in range(2):
                residual(0, r)
            dve.wait_ge(s("fst_tr"), 1)
            v.tensor_copy(fst[:, 0:32, :], bank(4).rearrange("p (f x) -> p f x", x=16)).then_inc(s("fst"), 1)
            v.tensor_copy(fst[:, 32:2 * NF, :], bank(5)[:, 0:(2 * NF - 32) * 16].rearrange("p (f x) -> p f x", x=16))\
                .then_inc(s("fst"), 1)
            dve.wait_ge(s("fst"), 2)
            with dve.Fori(1, KD // 2) as i:
                for r in range(2):
                    residual(i, r)

            def up_tile(j, r):
                f = j + NF * r
                dve.wait_ge(s("gemm"), j * 2 + (U_UP + r + 1))
                src, row = halves(r), up[:, r, :]
                fs = fst[:, bass.ds(f, 1), :].rearrange("p f (b w) -> p (f b) w", w=FW - 1)
                v.tensor_copy(fsam(row[:, FPW:PADF])[:, :, 0:FW - 1], fs)
                v.tensor_tensor(row[:, FW - 1:FW - 1 + HT], src[:, 0, :], rstd[:, 0:HT], ALU.mult)
                v.tensor_tensor(row[:, FW - 1 + HT:FPW], src[:, 1, 0:SEQ - HT], rstd[:, HT:SEQ], ALU.mult)
                v.tensor_tensor(fsam(row[:, FPW:PADF])[:, :, FW - 1:FSW],
                                src[:, 1, SEQ - HT:HT].rearrange("p (b t) -> p b t", t=LS),
                                rstd[:, SEQ:T].rearrange("p (b t) -> p b t", t=LS), ALU.mult).then_inc(s("uev"), 1)
                dve.wait_ge(s("uev"), j * 2 + (r + 1))
                fo = fns[:, bass.ds(f, 1), :].rearrange("p f x -> p (f x)")
                v.tensor_copy(fo[:, 0:2], row[:, SEQ:FPW])
                v.tensor_copy(fo[:, 2:18].rearrange("p (b w) -> p b w", w=2), fsam(row[:, FPW:PADF])[:, :, LS:FSW])\
                    .then_inc(s("fns"), 1)

                def w(t):
                    return par[:, bass.ds(j + (P_FW + 2 * NF * t + NF * r), 1)]

                out = ca[:, r, 0:CONVF]
                v.tensor_scalar(out, row[:, 0:CONVF], w(0), par[:, bass.ds(j + (P_FB + NF * r), 1)], ALU.mult, ALU.add)\
                    .then_inc(s("tap"), 1)
                for t in (1, 2):
                    dve.wait_ge(s("tap"), j * 4 + (2 * r + t))
                    v.scalar_tensor_tensor(out=out, in0=row[:, t:t + CONVF], scalar=w(t), in1=out, op0=ALU.mult, op1=ALU.add)\
                        .then_inc(s("tap" if t == 1 else "ca"), 1)

            def up_step(j):
                up_tile(j, 0)
                up_tile(j, 1)
                dve.wait_ge(s("gelu"), j + 1)
                dve.wait_ge(s("ca"), j * 2 + 2)
                v.tensor_tensor(hp[:, 0:CONVF], ca[:, 0, 0:CONVF], ca[:, 1, 0:CONVF], ALU.mult).then_inc(s("prod"), 1)
                dve.wait_ge(s("hh"), j + 1)
                hi_, lo_ = (t[:, bass.ds(j, 1), :].rearrange("p a t -> p (a t)") for t in (hh, hl))
                v.tensor_tensor(lo_[:, 0:SEQ], hp[:, 0:SEQ], hi_[:, 0:SEQ].bitcast(F32), ALU.subtract)
                v.tensor_tensor(lo_[:, SEQ:T].rearrange("p (b t) -> p b t", t=LS), fsam(hp[:, FPW:PADF])[:, :, 0:LS],
                                hi_[:, SEQ:T].rearrange("p (b t) -> p b t", t=LS).bitcast(F32), ALU.subtract)\
                    .then_inc(s("hl"), 1)

            dve.wait_ge(s("std"), 1)
            v.reciprocal(rstd[:], rstd[:]).then_inc(s("rstd"), 1)
            dve.wait_ge(s("rstd"), 1)
            with dve.Fori(0, NF) as j:
                up_step(j)

            with dve.Fori(0, KD // 2) as i:
                for r in range(2):
                    dve.wait_ge(s("gemm"), i * 4 + (U_DOWN + 2 * r + 2))
                    x = xt[:, bass.ds(i * 2 + r, 1), :].rearrange("p a (h t) -> p (a h) t", h=2)
                    v.tensor_tensor(x, x, halves(r), ALU.add).then_inc(s("x2"), 1)
            dve.wait_ge(s("late_in"), 64)
            for t in range(5):
                n = P if t < 4 else TS
                dve.wait_ge(s("yrms"), t + 1)
                then(v.reciprocal(fstat[0:n, 5 + t:6 + t], fstat[0:n, 5 + t:6 + t]))
                if t >= 2:
                    dve.wait_ge(s(f"yout{t % 2}"), 16 * (t // 2))
                v.scalar_tensor_tensor(out=yo[0:n, t % 2, :], in0=pair(2 + t % 2)[0:n], scalar=fstat[0:n, 5 + t:6 + t],
                                       in1=gfb[0:n, :], op0=ALU.mult, op1=ALU.mult).then_inc(s("y"), 1)


def _shapes():
    D, NBT, HD = 1, NB, H
    out = [("y_prompt", (1, SEQ, D_MODEL)), ("y_sample", (NB, LS, D_MODEL))]
    for pre, b in (("p_", 1), ("s_", NBT)):
        out += [(pre + "gla_S", (D, b, HD, DK, DV)), (pre + "mlstm_C", (D, b, HD, P, P)), (pre + "mlstm_n", (D, b, HD, P)),
                (pre + "mlstm_m", (D, b, HD)), (pre + "mlstm_conv", (D, b, CW - 1, 512)), (pre + "rglru_h", (D, b, 512)),
                (pre + "rglru_conv", (D, b, CW - 1, 512)), (pre + "ffn_conv", (D, b, FW - 1, 2 * D_FF))]
    return out


def kernel(**inputs):
    import concourse.bacc as bacc
    from concourse.bass_utils import run_bass_kernel_spmd as run

    nc = bacc.Bacc("TRN2", target_bir_lowering=False, num_devices=1)
    arrays, io = {}, {}
    for name, value in inputs.items():
        a = np.ascontiguousarray(value)
        arrays[name] = a
        io[name] = nc.dram_tensor(name, a.shape, mybir.dt.from_np(a.dtype), kind="ExternalInput").ap()
    for name, shape in _shapes():
        io[name] = nc.dram_tensor(name, shape, F32, kind="ExternalOutput").ap()
    layer(nc, io)
    r = run(nc, [arrays], core_ids=[0])
    return tuple(r.results[0][name] for name, _ in _shapes())
```

```python
from contextlib import ExitStack

import numpy as np

import concourse.bass as bass
from concourse import mybir

F32 = mybir.dt.float32
F32R = mybir.dt.float32r
ALU = mybir.AluOpType
ACT = mybir.ActivationFunctionType
X = mybir.AxisListType.X

P = 128
D_MODEL, SEQ, NB, LS = 1024, 512, 8, 4
TS = NB * LS
T = SEQ + TS
HT = T // 2
DK, DV, H = 64, 128, 4
RANK = 16
CHUNK = 64
NCH = SEQ // CHUNK
MCH = 128
NMC = SEQ // MCH
CW, FW = 4, 3
D_FF = 2816
NF = D_FF // P
KD = D_MODEL // P
EPS = 1e-6
NEG = -1e30

C_QKV, C_GG, C_GA = 0, 1024, 1536
C_MU = C_GA + RANK
C_MI = C_MU + 512
C_MF = C_MI + H
C_MO = C_MF + H
C_RX = C_MO + 512
C_GATE = C_RX + 1024

PW = CW - 1 + SEQ
SW = CW - 1 + LS
PADM = PW + NB * SW
CONVM = PADM - (CW - 1)
FPW = FW - 1 + SEQ
FSW = FW - 1 + LS
PADF = FPW + NB * FSW
CONVF = PADF - (FW - 1)

U_SMALL, U_QKV, U_MU, U_RX, U_RY, U_GG, U_MO, U_GB = 0, 1, 9, 13, 17, 21, 25, 29
U_OUT = U_GB + 3 * KD
U_UP = U_OUT + KD
U_DOWN = U_UP + 2 * NF
U_END = U_DOWN + 2 * KD
KT_IN, KT_GB, KT_DOWN, KT_MAX = 8, 12, 11, 12
BRANCH_ROWS = [0, 1024, 512]
GATE_OF = [0, 2, 1]

(PB_QKV, PB_MU, PB_RX, PB_RY, PB_GG, PB_MO, PB_GATE) = (0, 8, 12, 16, 20, 24, 28)
P_G2, P_GG, P_MG, P_MCW, P_MCB, P_RCW, P_RCB, P_BR, P_BI, P_LAM = 52, 60, 64, 68, 84, 88, 104, 108, 112, 116
P_FW, P_FB, P_A2 = 128, 128 + 3 * 2 * NF, 128 + 4 * 2 * NF
PAR_N = P_A2 + 2
P_G1 = PAR_N


PRAW = [(0, "b_in", C_QKV, 8), (8, "b_in", C_MU, 4), (12, "b_in", C_RX, 8), (20, "b_in", C_GG, 4), (24, "b_in", C_MO, 4),
        (28, "b_in", C_GATE, 24), (P_G2, "norm_ffn_g", 0, 8), (P_GG, "gla_norm_g", 0, 4),
        (P_MG, "mlstm_norm_g", 0, 4), (P_MCW, "mlstm_conv_w", 0, 16), (P_MCB, "mlstm_conv_b", 0, 4),
        (P_RCW, "rglru_conv_w", 0, 16), (P_RCB, "rglru_conv_b", 0, 4), (P_BR, "b_rglru_r", 0, 4),
        (P_BI, "b_rglru_i", 0, 4), (P_LAM, "rglru_lambda", 0, 4), (128, "ffn_conv_w", 0, 4 * NF),
        (256, "ffn_conv_w", 4 * NF * P, 2 * NF), (256 + 2 * NF, "ffn_conv_b", 0, 2 * NF),
        (256 + 4 * NF, "b_gla_a2", 0, 2)]
N_PRAW = len(PRAW)


def kt_of(u):
    return KT_GB if U_GB <= u < U_OUT else KT_DOWN if u >= U_DOWN else KT_IN


def layer(nc, io):
    ctx = ExitStack()
    with ctx:
        sems = {}

        def s(name):
            if name not in sems:
                sems[name] = ctx.enter_context(nc.semaphore("s_" + name))
            return sems[name]

        BASE = 16512

        def at(name, shape, off, dt=F32):
            return nc.alloc_sbuf_tensor_at(name, shape, dt, offset=BASE + off)

        def up32(n):
            return (n + 31) // 32 * 32

        TB = T * 4
        RXB = up32(4 * PADM * 4)
        RB = up32(553 * 4)
        UB = up32(2 * PADF * 4)
        stage = at("stage", [P, 2, KT_MAX, P], 0)
        whi = at("whi", [P, 2, KT_MAX, P], 12288, F32R)
        wlo = at("wlo", [P, 2, KT_MAX, P], 24576, F32R)
        xh = at("xh", [P, KD, T], 36864, F32R)
        xl = at("xl", [P, KD, T], 54272, F32R)
        o = 71680
        ident = at("ident", [P, P], o)
        ones = at("ones", [P, P], o + 512)
        par = at("par", [P, PAR_N + KD], o + 1024)
        cst = at("cst", [P, 8], o + 2304)
        o += 2336
        early = o
        gv = at("gv", [P, H, T], o)
        gg = at("gg", [P, H, T], o + 4 * TB)
        kw = at("kw", [P, H, P], o)
        vt = at("vt", [P, H, P + 1], o + 2048)
        arg = at("arg", [P, H, P], o + 4128)
        pt = at("pt", [P, H, P], o + 6176)
        ti = at("ti", [P, H, P + 1], o + 8224)
        num = at("num", [P, H, P + 1], o + 10304)
        ct = at("ct", [P, H, P + 1], o + 12384)
        qbm = at("qbm", [P, NB, TS], o + 14464)
        mus = at("mus", [P, H, TS], o + 15488)
        xt = at("xt", [P, KD, T], o)
        o += 8 * TB
        rest = o
        qk = at("qk", [P, 4, T], o)
        qz = at("qz", [P, 2, 2, T], o + 4 * TB)
        mix = at("mix", [P, KD, T], o)
        o += 8 * TB
        g1 = at("g1", [P, 2, T], o)

        kd = at("kd", [P, 2, T], o + 2 * TB)
        bc = at("bc", [P, 2, T], o + 4 * TB)
        gsq = at("gsq", [P, H, P], o + 6 * TB)
        gst = at("gst", [P, 2, P], o + 6 * TB + 2048)
        ogh = at("ogh", [P, H, T], o, F32R)
        ogl = at("ogl", [P, H, T], o + 4 * TB, F32R)
        mh = at("mh", [P, KD, T], o, F32R)
        o += 8 * TB
        rx = at("rx", [P, 4, PADM], o)
        orh = at("orh", [P, 4, PADM], o, F32R)
        o += RXB
        ry = at("ry", [P, 4, T], o)
        orl = at("orl", [P, 4, T], o, F32R)
        ml = at("ml", [P, KD, T], o - RXB, F32R)
        o += 4 * TB
        pm = at("pm", [P, 4, PADM], o)
        xs2 = at("xs2", [TS, D_MODEL], o)
        o += RXB
        w0 = o
        mcv = at("mcv", [P, H, T], o)
        mk = at("mk", [P, H, T], o + 4 * TB)
        mq = at("mq", [P, H, T], o + 8 * TB)
        mo = at("mo", [P, H, T], o + 12 * TB)
        omh = at("omh", [P, H, T], o, F32R)
        oml = at("oml", [P, H, T], o + 4 * TB, F32R)
        xtok = at("xtok", [P, 5, D_MODEL], w0)
        dt_ = at("dt", [P, 5, P], w0 + 20480)
        xp2 = at("xp2", [P, 4, D_MODEL], w0 + 8 * TB)
        rows = [at(f"row{i}", [4, 553], w0 + i * RB) for i in range(9)]
        rowf, lf, ra, rl0, ri0, rm, rF, rmm, rr = rows
        rowi = at("rowi", [4, T], w0 + 9 * RB)
        big = at("big", [P, T], w0 + 10 * RB)
        ss = at("ss", [P, 2, NB, P], w0)
        vb = at("vb", [TS, NB, P], w0 + 8192)
        qb = at("qb", [P, 2, 2, NB, TS], w0 + 12288)
        rt = [at(f"rt{i}", [P, PADM], w0 + 12288 + (i + 4) % 6 * 2304) for i in range(6)]
        cts = at("cts", [P, NB, P + 1], w0)
        kwb = at("kwb", [TS, NB, P], w0 + 4128)
        m0_ = w0 + 12 * TB
        junk = at("junk", [P, D_MODEL], m0_)
        gvt = at("gvt", [CHUNK, H, DV], m0_)
        ket = at("ket", [CHUNK, 2, P], m0_ + 2048)
        gat = at("gat", [CHUNK, H, CHUNK], m0_ + 3072)
        ot = at("ot", [CHUNK, H, DV], m0_ + 4096)
        on = at("on", [CHUNK, H, DV], m0_ + 6144)
        o += 16 * TB
        negm = at("negm", [P, P], o)
        cau = at("cau", [P, P], o + 512)
        negs = at("negs", [TS, TS], o + 1024)
        caus = at("caus", [TS, TS], o + 1152)
        blk = at("blk", [TS, NB], o + 1280)
        blkc = at("blkc", [P, NB, TS], o + 1312)
        sel = at("sel", [4, H, P], o + 2336)
        wa2 = at("wa2", [RANK, 2 * P], o + 4384)
        wq = at("wq", [P, 3, H, P], o + 5408)
        bd = at("bd", [P, 2, 4, P], o + 11552)
        ch = at("ch", [P, NB, P], o + 11552)
        cols = at("cols", [P, 5, 100], o + 15648)
        ecol = at("ecol", [P, 5, 68], o + 17664)
        rowb = at("rowb", [4, T], o + 19040)
        ga = at("ga", [RANK, T], o + 21216)
        sg = at("sg", [P, T], o + 21216)
        sml = at("sml", [P, 208], o + 23392)
        ns = at("ns", [P, 2, 4, 27], o + 21216)
        rhn = at("rhn", [P, 4, 9], o + 24224)
        o += 24384
        assert BASE + o <= 229368, (BASE + o, 229368)
        ch_buf = [ch, at("ch1", [P, NB, P], w0 - RXB), at("ch2", [P, NB, P], w0 - RXB + 4096)]
        dec = sml[:, 0:32]
        dcb = sml[:, 32:80]
        nt = sml[:, 80:112]
        c4 = sml[:, 112:116]
        mstat = sml[:, 116:126]
        h0t = sml[:, 128:160]
        gsum, grs = sml[:, 160:164], sml[:, 164:168]
        mden, mrec, msum, mrs = (sml[:, 168 + 4 * i:172 + 4 * i] for i in range(4))
        lz, lz2, lp = (sml[:, 184 + 4 * i:188 + 4 * i] for i in range(3))
        m0s = sml[0:4, 196:204]
        praw = at("praw", [P, 3, P], w0 + 23040)
        craw = at("craw", [24, 2, 512], m0_ + 4096)
        graw = at("graw", [KD, P], w0 + 24576)
        r64 = at("r64", [P, T], early + 4 * TB)
        h0raw = at("h0raw", [NB, 512], early + 5 * TB)
        nraw = at("nraw", [NB * H, P], early + 5 * TB + 2048)
        f0 = rest
        hh = at("hh", [P, NF, T], f0, F32R)
        hl = at("hl", [P, NF, T], f0 + NF * TB, F32R)
        fraw = at("fraw", [2 * NB, 2 * D_FF], w0)
        f1 = f0 + 2 * NF * TB
        up = at("up", [P, 2, PADF], f1)
        ca = at("ca", [P, 2, PADF], f1 + UB)
        hp = at("hp", [P, PADF], f1 + 2 * UB)
        f2 = f1 + 2 * UB + up32(PADF * 4)
        fst = at("fst", [P, 2 * NF, 2 * NB], f2)
        fns = at("fns", [P, 2 * NF, 2 + 2 * NB], f2 + 2816)
        rstd = at("rstd", [P, T], f2 + 6016)
        ssa = at("ssa", [P, T], f2 + 6016 + TB)
        fstat = at("fstat", [P, 10], f2 + 6016 + 2 * TB)
        assert BASE + f2 + 6016 + 2 * TB + 64 <= 229368
        ytok = at("ytok", [P, 5, D_MODEL], 36864)
        fout = at("fout", [2 + 2 * NB, 2 * D_FF], 36864)
        gfb = at("gfb", [P, D_MODEL], 36864 + 22528)
        ysq = at("ysq", [P, T], f1)
        yss = at("yss", [P, T], f1 + TB)
        yb = at("yb", [P, 2, T], f2 + 6016)
        rout = [at(f"rout{i}", [27, 512], w0 + 8192 + 2048 * i) for i in range(2)]
        hrow = at("hrow", [9, 512], w0 + 10240)

        ps = ctx.enter_context(nc.psum_tensor("ps", [P, 8 * 512], F32))

        def pair(i):
            return ps[:, i * 1024:(i + 1) * 1024]

        def halves(i):
            return pair(i).rearrange("p (a b) -> p a b", a=2)[:, :, 0:HT]

        def split(ap):
            return ap.rearrange("p (a b) -> p a b", a=2)

        def bank(i):
            return ps[:, i * 512:(i + 1) * 512]

        def sam(ap, width=SW):
            return ap.rearrange("p (b w) -> p b w", w=width)

        def fsam(ap):
            return ap.rearrange("p (b w) -> p b w", w=FSW)

        def each(ap, n):
            return ap.unsqueeze(2).broadcast_to([ap.shape[0], ap.shape[1], n])

        def prompt_cols(k):
            return slice(CHUNK * k, CHUNK * (k + 1)) if k < NCH else slice(SEQ, T)

        def mcols(c):
            return slice(MCH * c, MCH * (c + 1)) if c < NMC else slice(SEQ, T)

        visits = {}

        def plan(u, part, *what):
            visits.setdefault((u, part), []).extend(what)

        plan(1, 0, ("a2", 0))
        plan(3, 0, ("decays", 0))
        plan(5, 0, ("rows", 0))
        plan(6, 0, ("rowt", 0))
        plan(8, 0, ("gprep", 0))
        for k in range(NCH + 3):
            plan(10 + k, 0, ("gla", k))
        for h in range(H):
            plan(20 + h, 0, ("gd", h))
        plan(16, 0, ("rgc", 0))
        plan(17, 0, ("rgc", 1))
        plan(21, 0, ("gelu", 0))
        plan(22, 0, ("csn", 0))
        plan(24, 0, ("gfin", 0))
        for i in range(3):
            plan(24 + 2 * i, 0, ("rg", i), ("rgd", i))
        plan(27, 0, ("cs", 0), ("cs", 1))
        plan(29, 0, ("mconv", 0))
        plan(30, 1, ("rg", 3))
        plan(30, 0, ("rgd", 3))
        plan(31, 0, ("msilu", 0), ("msilu", 1), ("mconv", 1), ("mconv", 2), ("mconv", 3))
        plan(32, 1, ("rh", 0), ("msilu", 2), ("msilu", 3), ("mprep", 0))
        plan(32, 0, ("mqk", 0))
        plan(33, 1, ("mqk", 1), ("mqk", 2))
        plan(33, 0, ("mqk", 3))
        slots = [(u, p) for u in range(34, U_GB + 2 * KD) for p in (1, 0)]
        seq = []
        for c in range(NMC):
            seq += [[("mA", c)], [("mB", c)], [("mC", c)]]
        seq += [[("mA", NMC)]]
        for h in range(H):
            seq += [[("sH", h)], [("sI", h)]]
        seq += [[("m3", NMC), ("mout", 0), ("mfin", 0)]]
        for slot, steps in zip(slots, seq):
            plan(*slot, *steps)
        assert len(slots) >= len(seq)

        ctx.enter_context(nc.allow_non_contiguous_dma(reason="a few small states and biases"))
        block = ctx.enter_context(nc.Block())

        @block.sync
        def _(sp):
            w_in, w_out, w_up, w_down = (io[n][0] for n in ("w_in", "w_out", "w_up", "w_down"))
            w_branch = io["w_branch"][0]

            def tiles(w, col, n):
                return w[:, col:col + n * P].rearrange("(k p) (m c) -> m p k c", p=P, c=P)

            def one(view, i):
                return view[bass.ds(i, 1)].rearrange("m p k c -> p (m k) c")

            def load(slot, src, kt):
                sp.dma_start(stage[:, slot, 0:kt], src).then_inc(s(f"stage{slot}"), 16)

            def free_stage(u):
                sp.wait_ge(s("lo"), u - 1)

            def load_all(u0, view, n, kt):
                with sp.Fori(0, n // 2) as i:
                    for r in range(2):
                        free_stage(i * 2 + (u0 + r))
                        load((u0 + r) % 2, one(view, i * 2 + r), kt)
                if n % 2:
                    free_stage(u0 + n - 1)
                    load((u0 + n - 1) % 2, one(view, n - 1), kt)

            for t in (1, 3):
                sp.dma_start(xtok[:, t, :], io["x_prompt"][0, t * P:(t + 1) * P, :]).then_inc(s(f"tokens{t}"), 16)
            sp.dma_start(graw[:], io["norm_mix_g"].rearrange("l (r c) -> (l r) c", c=P)).then_inc(s("gain_in"), 16)

            small = w_in.rearrange("(k p) c -> p k c", p=P)
            sp.wait_ge(s("cleared"), 1)
            sp.dma_start(stage[:, 0, 0:KT_IN, 0:RANK], small[:, :, C_GA:C_GA + RANK]).then_inc(s("stage0"), 16)
            sp.dma_start(stage[:, 0, 0:KT_IN, 32:32 + H], small[:, :, C_MI:C_MI + H]).then_inc(s("small_in"), 16)
            sp.dma_start(stage[:, 0, 0:KT_IN, 64:64 + H], small[:, :, C_MF:C_MF + H]).then_inc(s("small_in"), 16)
            qkv = tiles(w_in, C_QKV, 8)
            load(1, one(qkv, 0), KT_IN)
            for row, name, a, n in PRAW:
                flat = io[name].rearrange("l a b -> (l a b)") if len(io[name].shape) == 3 else \
                    io[name].rearrange("l a -> (l a)")
                sp.dma_start(praw[row % P:row % P + n, row // P, :],
                             flat[a:a + n * P].rearrange("(r c) -> r c", c=P)).then_inc(s("praw_in"), 16)
            for w, name in enumerate(("state_mlstm_conv", "state_rglru_conv")):
                sp.dma_start(craw[:, w, :], io[name][0].rearrange("b w c -> (b w) c")).then_inc(s("craw_in"), 16)
            sp.dma_start(h0raw[:], io["state_rglru_h"][0]).then_inc(s("craw_in"), 16)
            sp.dma_start(nraw[:], io["state_mlstm_n"][0].rearrange("b h d -> (b h) d")).then_inc(s("craw_in"), 16)
            sp.wait_ge(s("cleared"), 2)
            for p0, col, n in ((0, C_GA, RANK), (32, C_MI, H), (64, C_MF, H)):
                sp.dma_start(cst[p0:p0 + n, 2:3], io["b_in"].rearrange("l c -> c l")[col:col + n, :]).then_inc(s("bsmall_in"), 16)
            sp.dma_start(wa2[:], io["w_gla_a2"][0]).then_inc(s("wa2_m0_in"), 16)
            sp.dma_start(m0s, io["state_mlstm_m"].rearrange("l b h -> h (l b)")).then_inc(s("wa2_m0_in"), 16)
            load_all(2, tiles(w_in, C_QKV + P, 7), 7, KT_IN)
            load_all(U_MU, tiles(w_in, C_MU, 4), 4, KT_IN)
            for n, name in enumerate(("w_mlstm_q", "w_mlstm_k", "w_mlstm_v")):
                sp.dma_start(wq[:, n], io[name][0].rearrange("h d e -> d h e")).then_inc(s("wq_in"), 16)
            load_all(U_RX, tiles(w_in, C_RX, 8), 8, KT_IN)
            sp.wait_ge(s("cleared"), 3)
            for n, name in enumerate(("w_rglru_r", "w_rglru_i")):
                for r in range(2):
                    src = io[name][0].rearrange("(t r) d e -> r d t e", r=2)[r]
                    sp.dma_start(bd[64 * r:64 * r + 64, n, :, 64 * r:64 * r + 64], src).then_inc(s("bd_in"), 16)
            load_all(U_GG, tiles(w_in, C_GG, 4), 4, KT_IN)
            load_all(U_MO, tiles(w_in, C_MO, 4), 4, KT_IN)
            for n in range(3):
                gates = tiles(w_in, C_GATE + GATE_OF[n] * D_MODEL, KD)
                rows_ = BRANCH_ROWS[n]
                outs = w_branch[rows_:rows_ + 512, :].rearrange("(k p) (m c) -> m p k c", p=P, c=P)
                u0 = U_GB + KD * n

                def pair_of_units(i):
                    for r in range(2):
                        slot = (u0 + r) % 2
                        free_stage(i * 2 + (u0 + r))
                        load(slot, one(gates, i * 2 + r), KT_IN)
                        sp.dma_start(stage[:, slot, KT_IN:KT_GB], one(outs, i * 2 + r)).then_inc(s(f"branch{slot}"), 16)

                done = 0
                if n == 2:
                    done = 2
                    for i in range(done):
                        pair_of_units(i)
                    sp.wait_ge(s("om"), H)
                    sp.dma_start(xp2[:], io["x_prompt"][0].rearrange("(t p) d -> p t d", p=P)).then_inc(s("late_in"), 16)
                    sp.dma_start(xs2[:], io["x_sample"].rearrange("b t d -> (b t) d")).then_inc(s("late_in"), 16)
                with sp.Fori(done, KD // 2) as i:
                    pair_of_units(i)
            load_all(U_OUT, tiles(w_out, 0, KD), 4, KT_IN)
            sp.wait_ge(s("xt"), KD)
            sp.dma_start(fraw[:], io["state_ffn_conv"][0].rearrange("b w f -> (b w) f")).then_inc(s("late_in"), 16)
            load_all(U_OUT + 4, tiles(w_out, 4 * P, KD - 4), KD - 4, KT_IN)
            ups = [tiles(w_up, 0, NF), tiles(w_up, D_FF, NF)]
            with sp.Fori(0, NF) as j:
                for r in range(2):
                    free_stage(j * 2 + (U_UP + r))
                    load((U_UP + r) % 2, one(ups[r], j), KT_IN)
            downs = [w_down[r * KT_DOWN * P:(r + 1) * KT_DOWN * P, :].rearrange("(k p) (m c) -> m p k c", p=P, c=P)
                     for r in range(2)]

            def down_tile(m):
                for r in range(2):
                    free_stage(m * 2 + (U_DOWN + r))
                    load((U_DOWN + r) % 2, one(downs[r], m), KT_DOWN)

            down_tile(0)
            sp.wait_ge(s("gemm"), U_DOWN)
            sp.dma_start(gfb[:], io["norm_f_g"].partition_broadcast(P)).then_inc(s("late_in"), 16)
            with sp.Fori(1, KD) as m:
                down_tile(m)
            for i, t in enumerate((0, 2)):
                sp.wait_ge(s("y"), i + 1)
                sp.dma_start(io["y_prompt"][0, t * P:(t + 1) * P, :], ytok[:, t, :]).then_inc(s("yout"), 16)
            sp.wait_ge(s("y"), 3)
            sp.dma_start(io["y_sample"].rearrange("b t d -> (b t) d"), ytok[0:TS, 4, :]).then_inc(s("yout"), 16)
            sp.wait_ge(s("yout"), 48)

        @block.gpsimd
        def _(pool):
            done = [0]

            def then(ins):
                done[0] += 1
                ins.then_inc(s("pool_step"), 1)
                pool.wait_ge(s("pool_step"), done[0])

            def pick(t, op, fill, base, pattern, mult):
                return pool.affine_select(out=t, in_=t, compare_op=op, fill=fill, base=base, pattern=pattern,
                                          channel_multiplier=mult)

            def lo(u, slot, kt):
                pool.wait_ge(s("hi"), u + 1)
                pool.tensor_tensor(wlo[:, slot, 0:kt], stage[:, slot, 0:kt], whi[:, slot, 0:kt].bitcast(F32),
                                   ALU.subtract).then_inc(s("lo"), 1)

            then(pool.memset(ident[:], 0.0))
            pick(ident[:], ALU.not_equal, 1.0, 0, [[-1, P]], 1).then_inc(s("ident"), 1)
            for u in range(2):
                lo(u, u, KT_IN)
            for t, v, fill in ((negm, 0.0, NEG), (cau, 1.0, 0.0)):
                then(pool.memset(t[:], v))
                pick(t[:], ALU.is_ge, fill, 0, [[1, P]], -1).then_inc(s("masks"), 1)
            for t, v, fill in ((negs, 0.0, NEG), (caus, 1.0, 0.0)):
                view = t[:].rearrange("p (b t) -> p b t", t=LS)
                then(pool.memset(t[:], v))
                then(pick(view, ALU.is_ge, fill, 0, [[LS, NB], [1, LS]], -1))
                pick(view, ALU.is_ge, fill, 0, [[-LS, NB], [0, LS]], 1).then_inc(s("masks"), 1)
            then(pool.memset(blk[:], 1.0))
            then(pick(blk[:], ALU.is_ge, 0.0, 0, [[-LS, NB]], 1))
            pick(blk[:], ALU.is_ge, 0.0, LS - 1, [[LS, NB]], -1).then_inc(s("masks"), 1)
            then(pool.memset(blkc[:], 0.0))
            pick(blkc[:].rearrange("p a (b t) -> p a b t", t=LS), ALU.not_equal, 1.0, 0,
                 [[1, NB], [-1, NB], [0, LS]], 0).then_inc(s("masks"), 1)
            then(pool.memset(sel[:], 0.0))
            pick(sel[:], ALU.not_equal, 1.0, 0, [[-1, H], [0, P]], 1).then_inc(s("masks"), 1)

            for u0, u1 in ((2, U_GB), (U_GB, U_OUT), (U_OUT, U_DOWN), (U_DOWN, U_END)):
                with pool.Fori(0, (u1 - u0) // 2) as i:
                    for r in range(2):
                        lo(i * 2 + (u0 + r), (u0 + r) % 2, kt_of(u0))
                if (u1 - u0) % 2:
                    lo(u1 - 1, (u1 - 1) % 2, kt_of(u0))
        @block.tensor
        def _(pe):
            mm = nc.tensor.matmul

            def tr(out, in_, k):
                return nc.tensor.transpose(out, in_, ident[0:k, 0:k])

            def gemm(dst, slot, k0, n, hi, lo, first=True, last=True, ready=None):
                for k in range(n):
                    if ready:
                        pe.wait_ge(s(ready), k + 1)
                    passes = ((whi, hi), (whi, lo), (wlo, hi))
                    for q, (w, x) in enumerate(passes):
                        for r in range(2):
                            ins = mm(dst[:, r, :], w[:, slot, k0 + k, :], x(k)[:, r * HT:(r + 1) * HT],
                                     start=first and k == 0 and q == 0, stop=last and k == n - 1 and q == 2)
                return ins

            def x_of(t, k0=0):
                return lambda k: t[:, k0 + k, 0:T]

            def unit(u, slot, dst, hi, lo, ready=None):
                pe.wait_ge(s("lo"), u + 1)
                gemm(halves(dst), slot, 0, KT_IN, x_of(hi), x_of(lo), ready=ready).then_inc(s("gemm"), 1)

            def start():
                pe.wait_ge(s("ident"), 1)
                pe.wait_ge(s("gain_in"), 16)
                tr(bank(7)[:, 0:KD], graw[:], KD).then_inc(s("par_tr"), 1)
                def normalised(j, t):
                    n = P if t < 4 else TS
                    return mm(pair(j % 4)[:, t * P:t * P + n], xtok[0:n, t, j * P:(j + 1) * P], dt_[0:n, t, 0:n],
                              start=True, stop=True)

                pe.wait_ge(s("gain"), 1)
                for t in range(5):
                    pe.wait_ge(s("diag"), t + 1)
                    for j in range(4):
                        ins = normalised(j, t)
                        if t == 4:
                            ins.then_inc(s("xn_mm"), 1)
                for j in range(4, KD):
                    pe.wait_ge(s("xl"), j - 3)
                    for t in range(5):
                        ins = normalised(j, t)
                    ins.then_inc(s("xn_mm"), 1)
                pe.wait_ge(s("xl"), KD - 3)
                unit(0, 0, 0, xh, xl, ready="xl")
                pe.wait_ge(s("xl"), KD)
                pe.wait_ge(s("praw_in"), 16 * N_PRAW)
                n0, n1, n2 = P_LAM + 4, 2 * 2 * NF, 2 * 2 * NF + 2
                tr(bank(4)[:, 0:n0], praw[0:n0, 0, :], n0)
                tr(bank(4)[:, P:P + n1], praw[0:n1, 1, :], n1)
                tr(bank(4)[:, P + n1:PAR_N], praw[0:n2, 2, :], n2).then_inc(s("par_tr"), 1)
                pe.wait_ge(s("craw_in"), 64)
                for w in range(2):
                    for i in range(4):
                        tr(bank(5)[:, (4 * w + i) * 24:(4 * w + i) * 24 + 24], craw[0:24, w, i * P:(i + 1) * P], 24)
                for i in range(4):
                    tr(bank(5)[:, 192 + 8 * i:200 + 8 * i], h0raw[0:NB, i * P:(i + 1) * P], NB)
                tr(bank(5)[:, 224:256], nraw[0:NB * H, :], NB * H).then_inc(s("par_tr"), 1)

            def v_a2(_):
                pe.wait_ge(s("evac"), 1)
                pe.wait_ge(s("wa2_m0_in"), 32)
                pe.wait_ge(s("par"), 2)
                for j in range(2):
                    for r in range(2):
                        ins = mm(bank(4 + 2 * j + r)[:, 0:HT], wa2[:, j * P:(j + 1) * P], ga[:, r * HT:(r + 1) * HT],
                                 start=True, stop=True)
                ins.then_inc(s("a2"), 1)

            def v_rows(_):
                pe.wait_ge(s("rows"), 1)
                pe.wait_ge(s("masks"), 7)
                for c in range(NMC):
                    tr(bank(4)[:, c * 100:(c + 1) * 100], big[0:100, mcols(c)], 100)
                tr(bank(5)[0:TS, 0:100], big[0:100, SEQ:T], 100)
                for h in range(H):
                    ins = mm(bank(5)[:, P + 12 * h:P + 12 * h + 12], sel[:, h, :], rr[:, 0:12], start=True, stop=True)
                ins.then_inc(s("rows_tr"), 1)

            def v_gla(k):
                if k >= 2:
                    c = k - 2
                    n = CHUNK if c < NCH else TS
                    pe.wait_ge(s("on"), c + 1)
                    pe.wait_ge(s("gstate"), min(c + 1, NCH))
                    for h in range(H):
                        ins = tr(bank(7)[:, h * CHUNK:h * CHUNK + n], on[0:n, h, :], n)
                    ins.then_inc(s("t3"), 1)
                if 1 <= k <= NCH + 1:
                    c = k - 1
                    n = CHUNK if c < NCH else TS
                    cs = prompt_cols(c)
                    pe.wait_ge(s("gat"), c + 1)
                    pe.wait_ge(s("gvt"), c + 1)
                    pe.wait_ge(s("gstate"), c)
                    if c >= 1:
                        pe.wait_ge(s("ot"), c)
                    if c == NCH:
                        pe.wait_ge(s("qb"), 1)
                        pe.wait_ge(s("ss_in"), 16 * H)
                    for h in range(H):
                        dst = bank(6)[0:n, h * P:(h + 1) * P]
                        if c < NCH:
                            mm(dst, qz[:, h // 2, h % 2, cs], gst[:, h // 2, :], start=True, stop=False)
                        else:
                            for b in range(NB):
                                mm(dst, qb[:, h // 2, h % 2, b, :], ss[:, h // 2, b, :], start=b == 0, stop=False)
                        ins = mm(dst, gat[0:n, h, 0:n], gvt[0:n, h, :], start=False, stop=True)
                    ins.then_inc(s("t2"), 1)
                if k <= NCH:
                    n = CHUNK if k < NCH else TS
                    cs = prompt_cols(k)
                    if k == 0:
                        pe.wait_ge(s("ke"), 1)
                        pe.wait_ge(s("evac"), U_MU)
                        pe.wait_ge(s("cols"), 1)
                        pe.wait_ge(s("ecol"), 1)
                    else:
                        pe.wait_ge(s("gvt"), k)
                        pe.wait_ge(s("gat"), k)
                    for h in range(H):
                        tr(bank(4)[0:n, h * P:(h + 1) * P], gv[:, h, cs], P)
                    for j in range(2):
                        tr(bank(5)[0:n, j * P:(j + 1) * P], qk[:, 2 + j, cs], P)
                    for j in range(2):
                        dst = bank(5)[0:n, 256 + j * P:256 + (j + 1) * P].rearrange("p (r t) -> p r t", r=2)[:, :, 0:n]
                        ins = mm(dst, kd[:, j, cs], qz[:, j, :, cs], start=True, stop=True)
                    ins.then_inc(s("t1"), 1)
                if 1 <= k <= NCH:
                    if k >= 2:
                        pe.wait_ge(s("t3_copied"), k - 1)
                    for j in range(2):
                        ins = mm(bank(7)[:, j * 256:(j + 1) * 256], ket[:, j, :], gvt[:, 2 * j:2 * j + 2, :],
                                 start=True, stop=True)
                    ins.then_inc(s("ds"), 1)

            def v_gd(h):
                pe.wait_ge(s("vb"), h + 1)
                if h:
                    pe.wait_ge(s("ss_new"), h)

                else:
                    pe.wait_ge(s("gvt"), NCH + 1)
                    pe.wait_ge(s("gat"), NCH + 1)
                for g in range(2):
                    ins = mm(bank(4 + g), ket[0:TS, h // 2, :], vb[:, 4 * g:4 * g + 4, :], start=True, stop=True)
                ins.then_inc(s("sds"), 1)

            def v_cs(w):
                pe.wait_ge(s("ns"), 1)
                pe.wait_ge(s("rg_copied"), 2)
                for i in range(4):
                    ins = tr(bank(4 + w)[0:27, i * P:(i + 1) * P], ns[:, w, i, :], P)
                ins.then_inc(s("state_tr"), 1)

            def v_rg(i):
                pe.wait_ge(s("xc"), i + 1)
                if i == 0:
                    pe.wait_ge(s("bd_in"), 64)
                    pe.wait_ge(s("ss_new"), H)
                    pe.wait_ge(s("t3_copied"), NCH + 1)
                else:
                    pe.wait_ge(s("rg_copied"), i)
                if i == 2:
                    pe.wait_ge(s("state_rows"), 2)
                for w in range(2):
                    for r in range(2):
                        n = CONVM // 2
                        ins = mm(bank(4 + 2 * w + r)[:, 0:n], bd[:, w, i, :], rt[i % 2][:, r * n:(r + 1) * n],
                                 start=True, stop=True)
                ins.then_inc(s("rg_mm"), 1)

            def v_rh(_):
                pe.wait_ge(s("or"), 4)
                pe.wait_ge(s("rg_copied"), 4)
                for i in range(4):
                    ins = tr(bank(4)[0:9, i * P:(i + 1) * P], rhn[:, i, :], P)
                ins.then_inc(s("state_tr"), 1)

            def v_mqk(h):
                if h == 0:
                    pe.wait_ge(s("wq_in"), 48)
                    pe.wait_ge(s("state_rows"), 3)
                pe.wait_ge(s("mcv"), h + 1)
                for w in range(2):
                    if h:
                        pe.wait_ge(s("mq" if w == 0 else "mk"), h)
                    for r in range(2):
                        ins = mm(bank(4 + 2 * w + r)[:, 0:HT], wq[:, w, h, :], mcv[:, h, r * HT:(r + 1) * HT],
                                 start=True, stop=True)
                    ins.then_inc(s("mqk_mm"), 1)

            def v_mA(c):
                n = MCH if c < NMC else TS
                cs = mcols(c)
                if c == 0:
                    pe.wait_ge(s("mq"), H)
                    pe.wait_ge(s("mk"), H)
                else:
                    v_m3(c - 1)
                    pe.wait_ge(s("mC"), c)
                for h in range(H):
                    ins = mm(bank(7)[0:n, h * P:h * P + n], sel[:, h, 0:n], rowb[:, cs], start=True, stop=True)
                ins.then_inc(s("mF"), 1)
                for h in range(H):
                    x = pm[:, h, CW - 1 + MCH * c:CW - 1 + MCH * (c + 1)] if c < NMC else mus[:, h, :]
                    mm(bank(5)[0:n, h * P:(h + 1) * P], x, wq[:, 2, h, :], start=True, stop=True)
                for h in range(H):
                    ins = tr(bank(4)[0:n, h * P:(h + 1) * P], mk[:, h, cs], P)
                ins.then_inc(s("mA"), 1)
                if c:
                    pe.wait_ge(s("m3_copied"), c)
                for h in range(H):
                    ins = mm(bank(6)[0:n, h * P:h * P + n], mk[:, h, cs], mq[:, h, cs], start=True, stop=True)
                ins.then_inc(s("mKQ"), 1)

            def v_mB(c):
                pe.wait_ge(s("pt"), c + 1)
                pe.wait_ge(s("kw"), c + 1)
                pe.wait_ge(s("vt"), c + 1)
                for h in range(H):
                    mm(bank(4 + h // 2)[:, (h % 2) * 129:(h % 2) * 129 + 129], pt[:, h, :], vt[:, h, :],
                       start=True, stop=True)
                if c:
                    pe.wait_ge(s("mC"), c)
                else:
                    pe.wait_ge(s("ct0"), 1)
                for h in range(H):
                    ins = mm(bank(6 + h // 2)[:, (h % 2) * 129:(h % 2) * 129 + 129], mq[:, h, mcols(c)], ct[:, h, :],
                             start=True, stop=True)
                ins.then_inc(s("mB"), 1)

            def v_mC(c):
                pe.wait_ge(s("num"), c + 1)
                for h in range(H):
                    ins = mm(bank(4 + h // 2)[:, (h % 2) * 129:(h % 2) * 129 + 129], kw[:, h, :], vt[:, h, :],
                             start=True, stop=True)
                ins.then_inc(s("mU"), 1)

            def v_m3(c):
                n = MCH if c < NMC else TS
                pe.wait_ge(s("hn"), c + 1)
                for h in range(H):
                    ins = tr(bank(6)[:, h * P:h * P + n], ti[0:n, h, 0:P], n)
                ins.then_inc(s("m3"), 1)

            def v_sH(h):
                pe.wait_ge(s(f"ch_in{h}"), 16)
                if h == 0:
                    pe.wait_ge(s("kw"), NMC + 1)
                    pe.wait_ge(s("vt"), NMC + 1)
                    pe.wait_ge(s("pt"), NMC + 1)
                else:
                    pe.wait_ge(s("ch_new"), h)
                for b in range(NB):
                    ins = tr(ps[:, 2048 + b * P:2048 + (b + 1) * P], ch_buf[h % 3][:, b, :], P)
                ins.then_inc(s("ch_tr"), 1)

            def v_sI(h):
                pe.wait_ge(s("cts"), 2 * h + 2)
                pe.wait_ge(s("qbm"), h + 1)
                if h:
                    pe.wait_ge(s("snum"), h)
                for b in range(NB):
                    mm(bank(6)[0:TS, 0:129], qbm[:, b, :], cts[:, b, :], start=b == 0, stop=b == NB - 1)
                mm(bank(7)[0:TS, 0:129], pt[0:TS, h, 0:TS], vt[0:TS, h, :], start=True, stop=True)
                mm(bank(7)[:, 256:256 + NB], kw[0:TS, h, :], blk[:], start=True, stop=True)
                for g in range(2):
                    ins = mm(bank(4 + g), vt[0:TS, h, 0:P], kwb[:, 4 * g:4 * g + 4, :], start=True, stop=True)
                ins.then_inc(s("sI"), 1)

            def v_mout(_):
                pe.wait_ge(s("ch_new"), H)
                for h in range(H):
                    tr(bank(4)[:, h * P:(h + 1) * P], ct[:, h, 0:P], P)
                tr(bank(5)[0:H, 0:P], ct[:, :, P], P)
                tr(bank(5)[0:NB * H, P:2 * P], nt, P).then_inc(s("state_tr"), 1)

            def nothing(_):
                pass

            parts = {"a2": v_a2, "rowt": v_rows, "gla": v_gla, "gd": v_gd, "cs": v_cs, "rg": v_rg,
                     "rh": v_rh, "mqk": v_mqk, "mA": v_mA, "mB": v_mB, "mC": v_mC, "m3": v_m3, "sH": v_sH,
                     "sI": v_sI, "mout": v_mout}

            def visit(u, part):
                for what, k in visits.get((u, part), []):
                    parts.get(what, nothing)(k)

            def gb_unit(n, slot, hi, lo, u, between, ready=None):
                pe.wait_ge(s("lo"), u + 1)
                if not isinstance(n, int) or n:
                    pe.wait_ge(s("gate_ev"), n)
                gemm(halves(0), slot, 0, KT_IN, x_of(xh), x_of(xl)).then_inc(s("gate_mm"), 1)
                between()
                if not isinstance(n, int) or n:
                    pe.wait_ge(s("br_ev"), n)
                gemm(halves(1), slot, KT_IN, 4, x_of(hi), x_of(lo), ready=ready).then_inc(s("gemm"), 1)

            start()
            for u in range(1, U_GB):
                if u >= 2:
                    pe.wait_ge(s("evac"), u - 1)
                unit(u, u % 2, u % 2, xh, xl)
                visit(u, 0)
            pe.wait_ge(s("evac"), U_GB)
            for n in range(2 * KD):
                u = U_GB + n

                def between():
                    visit(u, 1)
                    if n == 0:
                        pe.wait_ge(s("og"), 1)
                    if n == KD:
                        pe.wait_ge(s("or"), 4)

                gb_unit(n, u % 2, *((ogh, ogl) if n < KD else (orh, orl)), u, between)
                visit(u, 0)
            with pe.Fori(0, KD // 2) as i:
                for r in range(2):
                    gb_unit(i * 2 + (2 * KD + r), (U_GB + r) % 2, omh, oml, i * 2 + (U_GB + 2 * KD + r),
                            lambda: None, ready="om")

            pe.wait_ge(s("gate_ev"), 3 * KD)
            unit(U_OUT, U_OUT % 2, 0, mh, ml, ready="ml")
            pe.wait_ge(s("late_in"), 32)
            pe.wait_ge(s("state_rows"), 5)
            pe.wait_ge(s("m3_copied"), NMC + 1)
            for j in range(KD):
                if j >= 2:
                    pe.wait_ge(s("xt"), j - 1)
                for t in range(4):
                    tr(pair(2 + j % 2)[:, t * P:(t + 1) * P], xp2[:, t, j * P:(j + 1) * P], P)
                tr(pair(2 + j % 2)[:, SEQ:T], xs2[:, j * P:(j + 1) * P], TS).then_inc(s("xt_tr"), 1)

            unit(U_OUT + 1, (U_OUT + 1) % 2, 1, mh, ml)
            with pe.Fori(0, KD // 2 - 1) as i:
                for r in range(2):
                    pe.wait_ge(s("x1"), i * 2 + (r + 1))
                    unit(i * 2 + (U_OUT + 2 + r), (U_OUT + r) % 2, r, mh, ml)

            pe.wait_ge(s("late_in"), 48)
            pe.wait_ge(s("xt"), KD)
            for f in range(2 * NF):
                g, q = f // 32, f % 32
                ins = tr(bank(4 + g)[:, q * 16:q * 16 + 16], fraw[:, f * P:(f + 1) * P], 2 * NB)
            ins.then_inc(s("fst_tr"), 1)
            pe.wait_ge(s("ssa"), KD + 1)
            for r in range(2):
                ins = mm(halves(3)[:, r, :], ones[:], ssa[:, r * HT:(r + 1) * HT], start=True, stop=True)
            ins.then_inc(s("ss_mm"), 1)

            pe.wait_ge(s("x1"), KD - 1)
            unit(U_UP, U_UP % 2, 0, xh, xl, ready="xl2")
            pe.wait_ge(s("x1"), KD)
            unit(U_UP + 1, (U_UP + 1) % 2, 1, xh, xl)
            with pe.Fori(0, NF - 1) as j:
                for r in range(2):
                    pe.wait_ge(s("uev"), j * 2 + (r + 1))
                    unit(j * 2 + (U_UP + 2 + r), (U_UP + r) % 2, r, xh, xl)

            def down(m, half, dst):
                pe.wait_ge(s("lo"), m * 2 + (U_DOWN + half + 1))
                gemm(halves(dst), (U_DOWN + half) % 2, 0, KT_DOWN, x_of(hh, half * KT_DOWN), x_of(hl, half * KT_DOWN),
                     first=half == 0, last=half == 1).then_inc(s("gemm"), 1)

            def by_token(r):
                for t in range(5):
                    n = P if t < 4 else TS
                    ins = tr(pair(2 + r)[0:n, t * P:(t + 1) * P], yb[:, r, t * P:t * P + n], P)
                ins.then_inc(s("y_tr"), 1)

            for m in range(2):
                pe.wait_ge(s("uev"), 2 * NF - 1 + m)
                if m == 0:
                    pe.wait_ge(s("hl"), KT_DOWN)
                down(m, 0, m)
                if m == 0:
                    pe.wait_ge(s("hl"), NF)
                down(m, 1, m)
                if m == 0:
                    pe.wait_ge(s("fns"), 2 * NF)
                    pe.wait_ge(s("rstd"), 1)
                    for g in range(6):
                        if g >= 2:
                            pe.wait_ge(s(f"fout{g % 2}"), g // 2)
                        for q in range(8 if g < 5 else 2 * NF - 40):
                            ins = tr(pair(2 + g % 2)[0:2 + 2 * NB, q * P:(q + 1) * P], fns[:, 8 * g + q, :], P)
                        ins.then_inc(s("fns_tr"), 1)
            for r in range(2):
                pe.wait_ge(s(f"fout{r}"), 3)
            pe.wait_ge(s("x2"), 1)
            by_token(0)
            with pe.Fori(0, KD // 2 - 1) as i:
                for r in range(2):
                    pe.wait_ge(s("x2"), i * 2 + (r + 1))
                    down(i * 2 + (r + 2), 0, r)
                    down(i * 2 + (r + 2), 1, r)
                    pe.wait_ge(s("x2"), i * 2 + (r + 2))
                    pe.wait_ge(s("y_gain"), i * 2 + (r + 1))
                    by_token(1 - r)
            pe.wait_ge(s("x2"), KD)
            pe.wait_ge(s("y_gain"), KD - 1)
            by_token(1)
            pe.wait_ge(s("yss"), KD)
            pe.wait_ge(s("y_gain"), KD)
            for t in range(5):
                n = P if t < 4 else TS
                ins = mm(bank(4)[0:n, t:t + 1], yss[:, t * P:t * P + n], ones[:, 0:1], start=True, stop=True)
            ins.then_inc(s("ss_mm"), 1)
        @block.scalar
        def _(act):
            func = nc.scalar.activation
            done = [0]

            def then(ins):
                done[0] += 1
                ins.then_inc(s("act_step"), 1)
                act.wait_ge(s("act_step"), done[0])

            eps, one = cst[:, 0:1], cst[:, 1:2]
            outs = [0]

            def store(dst, src):
                outs[0] += 16
                act.dma_start(dst, src).then_inc(s("out"), 16)

            def hi(u):
                slot, kt = u % 2, kt_of(u)
                act.wait_ge(s(f"stage{slot}"), 16 * (u // 2 + 1))
                if u == 0:
                    act.wait_ge(s("small_in"), 32)
                if kt == KT_GB:
                    act.wait_ge(s(f"branch{slot}"), 16 * ((u - U_GB - (u - U_GB) % 2) // 2 + 1))
                if u >= 2:
                    act.wait_ge(s("gemm"), u - 1)
                func(whi[:, slot, 0:kt], stage[:, slot, 0:kt], ACT.Copy).then_inc(s("hi"), 1)

            def hi_at(k, u0, kt):
                slot = u0 % 2
                act.wait_ge(s(f"stage{slot}"), k * 16 + 16 * (u0 // 2 + 1))
                if kt == KT_GB:
                    act.wait_ge(s(f"branch{slot}"), k * 16 + 16 * ((u0 - U_GB) // 2 + 1))
                act.wait_ge(s("gemm"), k * 2 + (u0 - 1))
                func(whi[:, slot, 0:kt], stage[:, slot, 0:kt], ACT.Copy).then_inc(s("hi"), 1)

            for t in (0, 2):
                act.dma_start(xtok[:, t, :], io["x_prompt"][0, t * P:(t + 1) * P, :]).then_inc(s(f"tokens{t}"), 16)
            act.dma_start(xtok[0:TS, 4, :], io["x_sample"].rearrange("b t d -> (b t) d")).then_inc(s("tokens4"), 16)
            act.wait_ge(s("cleared"), 2)
            func(cst[:, 3:4], one, ACT.Sqrt)
            for t in range(5):
                n = P if t < 4 else TS
                act.wait_ge(s(f"tokens{t}"), 16)
                then(func(junk[0:n], xtok[0:n, t, :], ACT.Square, accum_out=mstat[0:n, t:t + 1]))
                func(mstat[0:n, 5 + t:6 + t], mstat[0:n, t:t + 1], ACT.Sqrt, bias=eps[0:n], scale=1.0 / D_MODEL)\
                    .then_inc(s("rms"), 1)
            hi(0)
            hi(1)
            act.wait_ge(s("gain"), 1)
            for j in range(KD):
                act.wait_ge(s("xn_mm"), j + 1)
                func(xh[:, j, :], pair(j % 4)[:, 0:T], ACT.Copy, scale=par[:, P_G1 + j:P_G1 + j + 1]).then_inc(s("xh"), 1)

            def to_padded(dst, src, bias):
                func(dst[:, CW - 1:CW - 1 + HT], src[:, 0, :], ACT.Identity, bias=bias)
                func(dst[:, CW - 1 + HT:PW], src[:, 1, 0:SEQ - HT], ACT.Identity, bias=bias)
                return func(sam(dst[:, PW:PADM])[:, :, CW - 1:SW], src[:, 1, SEQ - HT:HT].rearrange("p (b t) -> p b t", t=LS),
                            ACT.Identity, bias=bias)

            def evac(u):
                src = halves(u % 2)
                act.wait_ge(s("gemm"), u + 1)
                if u == U_SMALL:
                    act.wait_ge(s("bsmall_in"), 48)
                    act.wait_ge(s("xl"), KD)
                    func(split(ga[:]), src[0:RANK], ACT.Identity, bias=cst[0:RANK, 2:3])
                    func(split(rowi[:]), src[32:32 + H], ACT.Identity, bias=cst[32:32 + H, 2:3])
                    ins = func(split(rowf[:, 0:T]), src[64:64 + H], ACT.Identity, bias=cst[64:64 + H, 2:3])
                elif u < U_MU:
                    i = u - U_QKV
                    if i == 0:
                        act.wait_ge(s("par"), 2)
                    dst = qk[:, i, :] if i < 4 else gv[:, i - 4, :]
                    ins = func(split(dst), src, ACT.Identity, bias=par[:, PB_QKV + i:PB_QKV + i + 1])
                elif u < U_RX:
                    i = u - U_MU
                    ins = to_padded(pm[:, i, :], src, par[:, PB_MU + i:PB_MU + i + 1])
                elif u < U_RY:
                    i = u - U_RX
                    ins = to_padded(rx[:, i, :], src, par[:, PB_RX + i:PB_RX + i + 1])
                elif u < U_GG:
                    i = u - U_RY
                    ins = func(split(ry[:, i, :]), src, ACT.Identity, bias=par[:, PB_RY + i:PB_RY + i + 1])
                elif u < U_MO:
                    i = u - U_GG
                    ins = func(split(gg[:, i, :]), src, ACT.Silu, bias=par[:, PB_GG + i:PB_GG + i + 1])
                else:
                    i = u - U_MO
                    if i == 0:
                        act.wait_ge(s("og"), 1)
                        act.wait_ge(s("ss_new"), H)
                    ins = func(split(mo[:, i, :]), src, ACT.Sigmoid, bias=par[:, PB_MO + i:PB_MO + i + 1])
                ins.then_inc(s("evac"), 1)

            a2v = ps[:, 2048:4096].rearrange("p (j a b) -> p j a b", j=2, a=2)[:, :, :, 0:HT]

            def v_a2(_):
                act.wait_ge(s("a2"), 1)
                for j in range(2):
                    func(split(g1[:, j, :]), a2v[:, j], ACT.Abs, bias=par[:, P_A2 + j:P_A2 + j + 1]).then_inc(s("g_abs"), 1)
                act.wait_ge(s("g_abs"), 2)
                func(lz, par[:, P_LAM:P_LAM + 4], ACT.Abs)
                then(func(ra[:, 0:T], rowf[:, 0:T], ACT.Abs))
                func(g1[:], g1[:], ACT.Exp, scale=-1.0)
                func(lz, lz, ACT.Exp, scale=-1.0).then_inc(s("lam"), 1)
                then(func(ra[:, 0:T], ra[:, 0:T], ACT.Exp, scale=-1.0))
                func(g1[:], g1[:], ACT.Ln, bias=one).then_inc(s("g_ln"), 1)
                func(ra[:, 0:T], ra[:, 0:T], ACT.Ln, bias=one[0:4]).then_inc(s("row_ln"), 1)

            def v_decays(_):
                act.wait_ge(s("bc"), 2)
                func(g1[:], bc[:], ACT.Exp, scale=1.0 / 16).then_inc(s("decays"), 1)
                func(kd[:], bc[:], ACT.Exp, scale=-1.0 / 16).then_inc(s("decays"), 1)

            def v_rows(_):
                act.wait_ge(s("cols"), 1)
                func(dcb, bank(5)[:, P:P + 48], ACT.Exp)
                func(ecol[:, 0:4, :], cols[:, 0:4, 32:100], ACT.Exp)
                func(ecol[0:TS, 4, :], cols[0:TS, 4, 32:100], ACT.Exp).then_inc(s("ecol"), 1)
                store(io["p_mlstm_m"].rearrange("l b h -> h (l b)"), rm[:, SEQ:SEQ + 1])
                store(io["s_mlstm_m"].rearrange("l b h -> h (l b)"), rm[:, SEQ + 5:SEQ + 5 * NB + 1:5])

            def v_gprep(_):
                act.wait_ge(s("out"), outs[0])
                for h in range(H):
                    act.dma_start(ss[64 * (h % 2):64 * (h % 2) + 64, h // 2], io["state_gla_S"][0].rearrange("b h k v -> h k b v")[h])\
                       .then_inc(s("ss_in"), 16)
                act.wait_ge(s("db"), 1)
                func(g1[:], g1[:], ACT.Exp, scale=1.0 / 16).then_inc(s("ee"), 1)
                for j in range(2):
                    func(dec[:, 16 * j:16 * j + NCH], bc[:, j, CHUNK - 1:SEQ:CHUNK], ACT.Exp, scale=1.0 / 16)
                    ins = func(dec[:, 16 * j + NCH:16 * j + 16], bc[:, j, SEQ + LS - 1:T:LS], ACT.Exp, scale=1.0 / 16)
                ins.then_inc(s("dec"), 1)

            def v_gla(k):
                if k >= 2:
                    c = k - 2
                    n = CHUNK if c < NCH else TS
                    act.wait_ge(s("t3"), c + 1)
                    func(gv[:, :, prompt_cols(c)], bank(7)[:, 0:H * CHUNK].rearrange("p (h t) -> p h t", h=H)[:, :, 0:n],
                         ACT.Copy).then_inc(s("t3_copied"), 1)
                if 1 <= k <= NCH + 1:
                    c = k - 1
                    n = CHUNK if c < NCH else TS
                    act.wait_ge(s("t2"), c + 1)
                    if c:
                        act.wait_ge(s("on"), c)
                    func(ot[0:n], bank(6)[0:n].rearrange("p (h d) -> p h d", h=H), ACT.Copy).then_inc(s("ot"), 1)
                if k <= NCH:
                    n = CHUNK if k < NCH else TS
                    act.wait_ge(s("t1"), k + 1)
                    if k:
                        act.wait_ge(s("ds"), k)
                    func(ket[0:n], bank(5)[0:n, 0:2 * P].rearrange("p (j d) -> p j d", j=2), ACT.Copy).then_inc(s("ket"), 1)
                    func(gvt[0:n], bank(4)[0:n].rearrange("p (h d) -> p h d", h=H), ACT.Copy).then_inc(s("gvt"), 1)
                if 1 <= k <= NCH + 1:
                    c = k - 1
                    n = CHUNK if c < NCH else TS
                    act.wait_ge(s("gsum"), c + 1)
                    func(grs[0:n], gsum[0:n], ACT.Sqrt, bias=eps[0:n], scale=1.0 / DV).then_inc(s("grs"), 1)
                if k == NCH:
                    act.wait_ge(s("gstate"), NCH)
                    for r in range(2):
                        store(io["p_gla_S"][0, 0].rearrange("(j r) k v -> r k j v", r=2)[r], gst[64 * r:64 * r + 64])

            def v_cs(w):
                act.wait_ge(s("state_tr"), w + 1)
                r = rout[w]
                func(r[:], bank(4 + w)[0:27], ACT.Copy).then_inc(s("state_rows"), 1)
                act.wait_ge(s("state_rows"), w + 1)
                name = ("mlstm_conv", "rglru_conv")[w]
                store(io["p_" + name][0, 0], r[0:3])
                store(io["s_" + name][0].rearrange("b w c -> (b w) c"), r[3:27])

            def v_gfin(_):
                act.wait_ge(s("out"), outs[0])
                act.nop().then_inc(s("stored"), 1)
                act.wait_ge(s("ss_new"), H)
                for h in range(H):
                    store(io["s_gla_S"][0].rearrange("b h k v -> h k b v")[h], ss[64 * (h % 2):64 * (h % 2) + 64, h // 2])

            def v_gelu(_):
                act.wait_ge(s("evac"), U_GG)
                func(ry[:], ry[:], ACT.Gelu_apprx_tanh)

            def v_rg(i):
                act.wait_ge(s("rg_mm"), i + 1)
                if i:
                    act.wait_ge(s("rg_o"), i)
                c0 = CONVM // 2
                v = [pair(2 + w).rearrange("p (a b) -> p a b", a=2)[:, :, 0:c0] for w in range(2)]
                func(rt[2][:, 0:CONVM].rearrange("p (a b) -> p a b", a=2), v[0], ACT.Sigmoid, bias=par[:, P_BR + i:P_BR + i + 1])
                func(rt[3][:, 0:CONVM].rearrange("p (a b) -> p a b", a=2), v[1], ACT.Sigmoid, bias=par[:, P_BI + i:P_BI + i + 1])\
                    .then_inc(s("rg_copied"), 1)
                act.wait_ge(s("rg_copied"), i + 1)
                act.wait_ge(s("c4"), 1)
                then(func(rt[2][:, 0:CONVM], rt[2][:, 0:CONVM], ACT.Tanh, scale=c4[:, i:i + 1]))
                func(rt[4][:, 0:CONVM], rt[2][:, 0:CONVM], ACT.Sqrt).then_inc(s("rg_u"), 1)

            def v_rh(_):
                act.wait_ge(s("out"), outs[0])
                act.wait_ge(s("state_tr"), 3)
                func(hrow[:], bank(4)[0:9], ACT.Copy).then_inc(s("state_rows"), 1)
                act.wait_ge(s("state_rows"), 3)
                store(io["p_rglru_h"][0], hrow[0:1])
                store(io["s_rglru_h"][0], hrow[1:9])

            def v_msilu(h):
                if h == 0:
                    act.wait_ge(s("out"), outs[0])
                act.wait_ge(s("mconv"), h + 1)
                acc = rt[h % 2]
                func(mcv[:, h, 0:SEQ], acc[:, 0:SEQ], ACT.Silu)
                func(mcv[:, h, SEQ:T].rearrange("p (b t) -> p b t", t=LS),
                     acc[:, PW:PW + NB * SW].rearrange("p (b w) -> p b w", w=SW)[:, :, 0:LS], ACT.Silu).then_inc(s("mcv"), 1)

            def v_mprep(_):
                act.wait_ge(s("out"), outs[0])
                act.nop().then_inc(s("stored"), 1)

            def v_mqk(h):
                act.wait_ge(s("mqk_mm"), 2 * h + 1)
                if h == 0:
                    act.wait_ge(s("mcv"), H)
                func(split(mq[:, h, :]), halves(2), ACT.Copy).then_inc(s("mq"), 1)
                if h == H - 1:
                    act.dma_start(ch_buf[0][:], io["state_mlstm_C"][0].rearrange("b h v k -> h v b k")[0])\
                       .then_inc(s("ch_in0"), 16)

            def v_mA(c):
                n = MCH if c < NMC else TS
                if c:
                    v_m3(c - 1)
                act.wait_ge(s("arg"), c + 1)
                for h in range(H):
                    ins = func(arg[0:n, h, 0:n], arg[0:n, h, 0:n], ACT.Exp, bias=cols[0:n, c, h:h + 1])
                ins.then_inc(s("mE"), 1)
                act.wait_ge(s("mA"), c + 1)
                if c:
                    act.wait_ge(s("mU"), min(c, NMC))
                for h in range(H):
                    ins = func(kw[0:n, h, :], bank(4)[0:n, h * P:(h + 1) * P], ACT.Copy, scale=ecol[0:n, c, 64 + h:65 + h])
                ins.then_inc(s("kw"), 1)

            def rms_of(c, n):
                act.wait_ge(s("msum"), c + 1)
                func(mrs[0:n], msum[0:n], ACT.Sqrt, bias=eps[0:n], scale=1.0 / P).then_inc(s("mrs"), 1)

            def v_mB(c):
                rms_of(c, MCH)

            def v_m3(c):
                n = MCH if c < NMC else TS
                act.wait_ge(s("m3"), c + 1)
                func(mq[:, :, mcols(c)], bank(6).rearrange("p (h t) -> p h t", h=H)[:, :, 0:n], ACT.Copy)\
                    .then_inc(s("m3_copied"), 1)

            def v_sH(h):
                if h == 0:
                    act.wait_ge(s("vt"), NMC + 1)
                    for q in (1, 2):
                        act.dma_start(ch_buf[q][:], io["state_mlstm_C"][0].rearrange("b h v k -> h v b k")[q])\
                           .then_inc(s(f"ch_in{q}"), 16)
                if h == 1:
                    act.wait_ge(s("ch_out"), 16)
                    act.dma_start(ch_buf[0][:], io["state_mlstm_C"][0].rearrange("b h v k -> h v b k")[3])\
                       .then_inc(s("ch_in3"), 16)
                act.wait_ge(s("ch_tr"), h + 1)
                if h:
                    act.wait_ge(s("sI"), h)
                func(cts[:, :, 0:P], ps[:, 2048:3072].rearrange("p (b k) -> p b k", b=NB), ACT.Copy).then_inc(s("cts"), 1)

            def v_sI(h):
                if h == H - 1:
                    rms_of(NMC, TS)
                act.wait_ge(s("ch_new"), h + 1)
                act.dma_start(io["s_mlstm_C"][0].rearrange("b h v k -> h v b k")[h], ch_buf[h % 3][:])\
                   .then_inc(s("ch_out"), 16)

            def v_mout(_):
                act.wait_ge(s("state_tr"), 4)
                act.wait_ge(s("hn"), NMC + 1)
                func(arg[:], bank(4).rearrange("p (h k) -> p h k", h=H), ACT.Copy).then_inc(s("state_rows"), 1)
                func(pt[0:NB * H, 0:2, :], bank(5)[0:NB * H, 0:2 * P].rearrange("p (a k) -> p a k", a=2), ACT.Copy)\
                    .then_inc(s("state_rows"), 1)
                act.wait_ge(s("state_rows"), 5)
                store(io["p_mlstm_C"][0, 0].rearrange("h v k -> v h k"), arg[:])
                store(io["p_mlstm_n"][0, 0], pt[0:H, 0, :])
                store(io["s_mlstm_n"][0].rearrange("b h k -> (b h) k"), pt[0:NB * H, 1, :])

            def v_mfin(_):
                act.wait_ge(s("ch_out"), 64)
                act.nop().then_inc(s("stored"), 1)

            def nothing(_):
                pass

            parts = {"a2": v_a2, "decays": v_decays, "rowt": v_rows, "gprep": v_gprep, "gla": v_gla,
                     "gfin": v_gfin, "cs": v_cs, "rg": v_rg, "rh": v_rh, "gelu": v_gelu, "mprep": v_mprep,
                     "msilu": v_msilu, "mqk": v_mqk, "mA": v_mA, "mB": v_mB, "m3": v_m3, "sH": v_sH,
                     "sI": v_sI, "mout": v_mout, "mfin": v_mfin}

            def visit(u, part):
                for what, k in visits.get((u, part), []):
                    parts.get(what, nothing)(k)

            for u in range(U_GB):
                act.wait_ge(s("gemm"), u + 1)
                hi(u + 2)
                evac(u)
                visit(u, 0)

            def gate(n, col):
                act.wait_ge(s("gate_mm"), n + 1)
                if not isinstance(n, int) or n:
                    act.wait_ge(s("br_ev"), n)
                func(split(sg[:]), halves(0), ACT.Sigmoid, bias=col).then_inc(s("gate_ev"), 1)

            for n in range(2 * KD):
                u = U_GB + n
                g = PB_GATE + GATE_OF[n // KD] * KD + n % KD
                gate(n, par[:, g:g + 1])
                visit(u, 1)
                act.wait_ge(s("gemm"), u + 1)
                hi(u + 2)
                visit(u, 0)

            def gb_mlstm(i, r, hi_next):
                gate(i * 2 + (2 * KD + r), par[:, bass.ds(i * 2 + (PB_GATE + KD + r), 1)])
                hi_next()
                act.wait_ge(s("br_ev"), i * 2 + (2 * KD + r + 1))
                func(mh[:, bass.ds(i * 2 + r, 1), :], mix[:, bass.ds(i * 2 + r, 1), :], ACT.Copy).then_inc(s("mh"), 1)

            u0 = U_GB + 2 * KD
            with act.Fori(0, KD // 2 - 1) as i:
                for r in range(2):
                    gb_mlstm(i, r, lambda: hi_at(i, u0 + 2 + r, KT_GB))
            for r in range(2):
                i = KD // 2 - 1
                gate(i * 2 + (2 * KD + r), par[:, PB_GATE + KD + 2 * i + r:PB_GATE + KD + 2 * i + r + 1])
                hi(U_OUT + r)
                act.wait_ge(s("br_ev"), 3 * KD - 1 + r)
                func(mh[:, 2 * i + r, :], mix[:, 2 * i + r, :], ACT.Copy).then_inc(s("mh"), 1)

            act.wait_ge(s("out"), outs[0])
            act.nop().then_inc(s("stored"), 1)
            with act.Fori(0, KD // 2) as i:
                for r in range(2):
                    hi_at(i, U_OUT + 2 + r, KT_IN)
                    m = bass.ds(i * 2 + r, 1)
                    act.wait_ge(s("x1"), i * 2 + (r + 1))
                    act.wait_ge(s("ssa"), i * 2 + (r + 1))
                    func(hp[:, 0:T], xt[:, m, :].rearrange("p a t -> p (a t)"), ACT.Square).then_inc(s("sq"), 1)
                    func(xh[:, m, :], xt[:, m, :], ACT.Copy, scale=par[:, bass.ds(i * 2 + (P_G2 + r), 1)])\
                        .then_inc(s("xh2"), 1)

            def up_hi(j):
                act.wait_ge(s("prod"), j + 1)
                dst = hh[:, bass.ds(j, 1), :].rearrange("p a t -> p (a t)")
                func(dst[:, 0:SEQ], hp[:, 0:SEQ], ACT.Copy)
                func(dst[:, SEQ:T].rearrange("p (b t) -> p b t", t=LS),
                     fsam(hp[:, FPW:PADF])[:, :, 0:LS], ACT.Copy).then_inc(s("hh"), 1)

            def gelu(j):
                act.wait_ge(s("ca"), j * 2 + 1)
                func(ca[:, 0, 0:CONVF], ca[:, 0, 0:CONVF], ACT.Gelu_apprx_tanh).then_inc(s("gelu"), 1)

            act.wait_ge(s("ss_mm"), 1)
            func(split(rstd[:]), halves(3), ACT.Sqrt, bias=eps, scale=1.0 / D_MODEL).then_inc(s("std"), 1)
            hi(U_UP + 2)
            hi(U_UP + 3)
            gelu(0)
            up_hi(0)
            with act.Fori(1, NF - 1) as j:
                for r in range(2):
                    hi_at(j, U_UP + 2 + r, KT_IN)
                gelu(j)
                up_hi(j)
            for r in range(2):
                hi(U_DOWN + r)
            gelu(NF - 1)
            up_hi(NF - 1)

            def square(m, r):
                act.wait_ge(s("x2"), m + 1)
                if not isinstance(m, int) or m:
                    act.wait_ge(s("yss"), m)
                func(ysq[:], yb[:, r, :], ACT.Square).then_inc(s("ysq"), 1)

            hi(U_DOWN + 2)
            hi(U_DOWN + 3)
            for g in range(0, 6, 2):
                act.wait_ge(s("fns_tr"), g + 1)
                func(fout[:, 8 * g * P:8 * (g + 1) * P], pair(2)[0:2 + 2 * NB], ACT.Copy).then_inc(s("fout0"), 1)
            square(0, 0)
            act.wait_ge(s("fout0"), 3)
            act.wait_ge(s("fout1"), 3)
            store(io["p_ffn_conv"][0, 0], fout[0:2])
            store(io["s_ffn_conv"][0].rearrange("b w f -> (b w) f"), fout[2:2 + 2 * NB])
            hi(U_DOWN + 4)
            act.wait_ge(s("out"), outs[0])
            act.nop().then_inc(s("stored"), 1)
            hi(U_DOWN + 5)
            square(1, 1)
            with act.Fori(0, KD // 2 - 2) as i:
                for r in range(2):
                    for q in range(2):
                        act.wait_ge(s(f"stage{(U_DOWN + q) % 2}"), i * 32 + 16 * ((U_DOWN + 6 + 2 * r + q) // 2 + 1))
                        act.wait_ge(s("gemm"), i * 4 + (U_DOWN + 5 + 2 * r + q))
                        slot = (U_DOWN + q) % 2
                        func(whi[:, slot, 0:KT_DOWN], stage[:, slot, 0:KT_DOWN], ACT.Copy).then_inc(s("hi"), 1)
                    square(i * 2 + (r + 2), r)
            hi(U_END - 2)
            hi(U_END - 1)
            for m in range(KD - 2, KD):
                square(m, m % 2)
            act.wait_ge(s("ss_mm"), 2)
            func(fstat[:, 0:4], bank(4)[:, 0:4], ACT.Sqrt, bias=eps, scale=1.0 / D_MODEL)
            func(fstat[0:TS, 4:5], bank(4)[0:TS, 4:5], ACT.Sqrt, bias=eps[0:TS], scale=1.0 / D_MODEL).then_inc(s("std"), 1)
            act.wait_ge(s("y_rstd"), 1)
            act.wait_ge(s("y_gain"), KD + 1)
            for t in (1, 3):
                then(func(ytok[:, t, :], ytok[:, t, :], ACT.Copy, scale=fstat[:, t:t + 1]))
                store(io["y_prompt"][0, t * P:(t + 1) * P, :], ytok[:, t, :])
            act.wait_ge(s("out"), outs[0])
        @block.vector
        def _(dve):
            v = nc.vector
            done = [0]

            def then(ins):
                done[0] += 1
                ins.then_inc(s("dve_step"), 1)
                dve.wait_ge(s("dve_step"), done[0])

            def conv(out, row, n, taps, w, b):
                then(v.tensor_scalar(out, row[:, 0:n], w(0), b, ALU.mult, ALU.add))
                for j in range(1, taps):
                    ins = v.scalar_tensor_tensor(out=out, in0=row[:, j:j + n], scalar=w(j), in1=out,
                                                 op0=ALU.mult, op1=ALU.add)
                    if j < taps - 1:
                        then(ins)
                return ins

            v.memset(stage[:, 0, 0:KT_IN], 0.0).then_inc(s("cleared"), 1)
            v.memset(cst[:, 0:1], EPS)
            v.memset(cst[:, 2:3], 0.0)
            v.memset(cst[:, 1:2], 1.0).then_inc(s("cleared"), 1)
            v.memset(bd[:], 0.0).then_inc(s("cleared"), 1)
            v.memset(ones[:], 1.0)
            v.memset(pm[:, :, 0:CW - 1], 0.0)
            v.memset(rx[:, :, 0:CW - 1], 0.0)
            v.memset(qz[0:64, :, 1, :], 0.0)
            v.memset(qz[64:P, :, 0, :], 0.0)
            then(v.memset(gst[:], 0.0))
            dve.wait_ge(s("par_tr"), 1)
            v.tensor_copy(par[:, P_G1:P_G1 + KD], bank(7)[:, 0:KD]).then_inc(s("gain"), 1)
            dve.wait_ge(s("ident"), 1)
            for t in range(5):
                n = P if t < 4 else TS
                dve.wait_ge(s("rms"), t + 1)
                then(v.reciprocal(mstat[0:n, 5 + t:6 + t], mstat[0:n, 5 + t:6 + t]))
                v.tensor_scalar(dt_[0:n, t, :], ident[0:n, :], mstat[0:n, 5 + t:6 + t], None, ALU.mult).then_inc(s("diag"), 1)
            for j in range(KD):
                dve.wait_ge(s("xh"), j + 1)
                v.scalar_tensor_tensor(out=xl[:, j, :], in0=pair(j % 4)[:, 0:T], scalar=par[:, P_G1 + j:P_G1 + j + 1],
                                       in1=xh[:, j, :].bitcast(F32), op0=ALU.mult, op1=ALU.subtract).then_inc(s("xl"), 1)
            dve.wait_ge(s("par_tr"), 2)
            v.tensor_copy(par[:, 0:P_LAM + 4], bank(4)[:, 0:P_LAM + 4])
            v.tensor_copy(par[:, P:PAR_N], bank(4)[:, P:PAR_N]).then_inc(s("par"), 1)
            dve.wait_ge(s("par_tr"), 3)
            for w, dst in enumerate((pm, rx)):
                for i in range(4):
                    c = (4 * w + i) * 24
                    v.tensor_copy(sam(dst[:, i, PW:PADM])[:, :, 0:CW - 1],
                                  bank(5)[:, c:c + 24].rearrange("p (b w) -> p b w", w=CW - 1))
            v.tensor_copy(h0t, bank(5)[:, 192:224])
            v.tensor_copy(nt, bank(5)[:, 224:256]).then_inc(s("par"), 1)
            dve.wait_ge(s("par"), 2)
            then(v.memset(r64[:], 1.0))
            then(v.memset(r64[:, 0:SEQ:CHUNK], 0.0))
            then(v.memset(r64[:, SEQ:T:LS], 0.0))

            a2v = ps[:, 2048:4096].rearrange("p (j a b) -> p j a b", j=2, a=2)[:, :, :, 0:HT]

            def v_a2(_):
                dve.wait_ge(s("g_abs"), 2)
                for j in range(2):
                    ins = v.tensor_scalar(split(kd[:, j, :]), a2v[:, j], par[:, P_A2 + j:P_A2 + j + 1], 0.0, ALU.add, ALU.min)
                then(ins)
                dve.wait_ge(s("g_ln"), 1)
                then(v.tensor_tensor(kd[:], kd[:], g1[:], ALU.subtract))
                for j in range(2):
                    v.tensor_tensor_scan(bc[:, j, :], r64[:], kd[:, j, :], 0.0, ALU.mult, ALU.add).then_inc(s("bc"), 1)
                dve.wait_ge(s("lam"), 1)
                then(v.tensor_scalar(lz2, lz, 2.0, None, ALU.add))
                then(v.reciprocal(lz2, lz2))
                then(v.tensor_tensor(lz, lz, lz2, ALU.mult))
                then(v.tensor_tensor(lz2, lz, lz, ALU.mult))
                then(v.tensor_scalar(lp, lz2, 1.0 / 17, None, ALU.mult))
                for k in range(15, 1, -2):
                    then(v.scalar_tensor_tensor(out=lp, in0=lp, scalar=1.0 / k, in1=lz2, op0=ALU.add, op1=ALU.mult))
                then(v.scalar_tensor_tensor(out=lp, in0=lp, scalar=1.0, in1=lz, op0=ALU.add, op1=ALU.mult))
                then(v.tensor_scalar(lz2, par[:, P_LAM:P_LAM + 4], 0.0, -4.0, ALU.min, ALU.mult))
                v.scalar_tensor_tensor(out=c4, in0=lp, scalar=8.0, in1=lz2, op0=ALU.mult, op1=ALU.add).then_inc(s("c4"), 1)

            def tokens(ap, off=0):
                return (ap[:, off:off + SEQ].rearrange("p (c t) -> p c t", t=MCH),
                        ap[:, off + SEQ:off + T].rearrange("p (b t) -> p b t", t=LS))

            def v_rows(_):
                then(v.memset(big[:], 0.0))
                then(v.memset(rl0[:], NEG))
                then(v.memset(ri0[:], 0.0))
                then(v.memset(rr[:], 1.0))
                then(v.memset(rr[:, 0:SEQ:MCH], 0.0))
                then(v.memset(rr[:, SEQ:T:LS], 0.0))
                dve.wait_ge(s("evac"), 1)
                dve.wait_ge(s("row_ln"), 1)
                then(v.tensor_scalar(lf[:, 0:T], rowf[:, 0:T], 0.0, None, ALU.min))
                then(v.tensor_tensor(lf[:, 0:T], lf[:, 0:T], ra[:, 0:T], ALU.subtract))
                m0 = [x[:, 1 + SEQ:1 + SEQ + 5 * NB].rearrange("p (b w) -> p b w", w=LS + 1) for x in (rl0, ri0, rm)]
                v.tensor_copy(rl0[:, 1:1 + SEQ], lf[:, 0:SEQ])
                v.tensor_copy(m0[0][:, :, 1:], tokens(lf)[1])
                v.tensor_copy(ri0[:, 1:1 + SEQ], rowi[:, 0:SEQ])
                dve.wait_ge(s("wa2_m0_in"), 32)
                v.tensor_copy(m0[1][:, :, 0:1], m0s.unsqueeze(2))
                then(v.tensor_copy(m0[1][:, :, 1:], tokens(rowi)[1]))
                then(v.tensor_tensor_scan(rm[:], rl0[:], ri0[:], 0.0, ALU.add, ALU.max))
                then(v.tensor_tensor_scan(rF[:, 0:T], rr[:, 0:T], lf[:, 0:T], 0.0, ALU.mult, ALU.add))
                v.tensor_copy(rmm[:, 0:SEQ], rm[:, 1:1 + SEQ])
                then(v.tensor_copy(tokens(rmm)[1], m0[2][:, :, 1:]))
                then(v.tensor_tensor(rowb[:], rF[:, 0:T], rmm[:, 0:T], ALU.subtract))
                then(v.tensor_tensor(big[0:4], rowi[:], rF[:, 0:T], ALU.subtract))
                before = (rm[:, 0:SEQ:MCH], rm[:, 1 + SEQ:1 + SEQ + 5 * NB:5])
                last = (rowb[:, MCH - 1:SEQ:MCH], rowb[:, SEQ + LS - 1:T:LS])
                for q, n in ((0, MCH), (1, LS)):
                    v.tensor_tensor(tokens(big[32:36])[q], tokens(rowb)[q], each(before[q], n), ALU.add)
                    v.tensor_tensor(tokens(big[96:100])[q], tokens(big[0:4])[q], each(last[q], n), ALU.add)
                v.tensor_scalar(big[64:68], rmm[:, 0:T], -1.0, None, ALU.mult)
                v.tensor_tensor(rr[:, 0:NMC], last[0], before[0], ALU.add)
                v.tensor_tensor(rr[:, NMC:NMC + NB], last[1], before[1], ALU.add).then_inc(s("rows"), 1)

            def v_rowt(_):
                dve.wait_ge(s("rows_tr"), 1)
                v.tensor_copy(cols[:, 0:4, :], bank(4)[:, 0:400].rearrange("p (c x) -> p c x", c=4))
                v.tensor_copy(cols[0:TS, 4, :], bank(5)[0:TS, 0:100]).then_inc(s("cols"), 1)

            def v_gprep(_):
                dve.wait_ge(s("evac"), U_MU)
                dve.wait_ge(s("decays"), 1)
                for r in range(2):
                    q = slice(64 * r, 64 * r + 64)
                    v.scalar_tensor_tensor(out=qz[q, :, r, :], in0=qk[q, 0:2, :], scalar=float(DK) ** -0.5, in1=g1[q],
                                           op0=ALU.mult, op1=ALU.mult).then_inc(s("qz"), 1)
                dve.wait_ge(s("qz"), 2)
                dve.wait_ge(s("decays"), 2)
                v.tensor_tensor(kd[:], qk[:, 2:4, :], kd[:], ALU.mult)
                for j in range(2):
                    v.tensor_tensor(g1[:, j, 0:SEQ].rearrange("p (c t) -> p c t", t=CHUNK),
                                    each(bc[:, j, CHUNK - 1:SEQ:CHUNK], CHUNK),
                                    bc[:, j, 0:SEQ].rearrange("p (c t) -> p c t", t=CHUNK), ALU.subtract)
                    ins = v.tensor_tensor(g1[:, j, SEQ:T].rearrange("p (c t) -> p c t", t=LS),
                                          each(bc[:, j, SEQ + LS - 1:T:LS], LS),
                                          bc[:, j, SEQ:T].rearrange("p (c t) -> p c t", t=LS), ALU.subtract)
                ins.then_inc(s("db"), 1)
                dve.wait_ge(s("ee"), 1)
                v.tensor_tensor(qk[:, 2:4, :], qk[:, 2:4, :], g1[:], ALU.mult).then_inc(s("ke"), 1)

            def v_gla(k):
                if k <= NCH:
                    n = CHUNK if k < NCH else TS
                    dve.wait_ge(s("ket"), k + 1)
                    if k == 0:
                        dve.wait_ge(s("masks"), 7)
                    if k:
                        dve.wait_ge(s("t2"), k)
                    mask = cau[0:n, 0:n] if k < NCH else caus[:]
                    a = bank(5)[0:n, 256:512].rearrange("p (h t) -> p h t", h=H)[:, :, 0:n]
                    v.tensor_tensor(gat[0:n, :, 0:n], a, mask.unsqueeze(1).broadcast_to([n, H, n]), ALU.mult)\
                        .then_inc(s("gat"), 1)
                if 1 <= k <= NCH:
                    dve.wait_ge(s("ds"), k)
                    if k == 1:
                        dve.wait_ge(s("dec"), 1)
                    for j in range(2):
                        for r in range(2):
                            q = slice(64 * r, 64 * r + 64)
                            ins = v.scalar_tensor_tensor(out=gst[q, j, :], in0=gst[q, j, :],
                                                         scalar=dec[q, 16 * j + k - 1:16 * j + k],
                                                         in1=bank(7)[q, (2 * j + r) * P:(2 * j + r + 1) * P],
                                                         op0=ALU.mult, op1=ALU.add)
                    ins.then_inc(s("gstate"), 1)
                    dve.wait_ge(s("gstate"), k)
                if k == NCH:
                    for h in range(H):
                        q = qz[:, h // 2, h % 2, SEQ:T].unsqueeze(1).broadcast_to([P, NB, TS])
                        ins = v.tensor_tensor(qb[:, h // 2, h % 2], q, blkc[:], ALU.mult)
                    ins.then_inc(s("qb"), 1)
                if 1 <= k <= NCH + 1:
                    c = k - 1
                    n = CHUNK if c < NCH else TS
                    dve.wait_ge(s("ot"), c + 1)
                    then(v.tensor_tensor(gsq[0:n], ot[0:n], ot[0:n], ALU.mult))
                    v.tensor_reduce(gsum[0:n], gsq[0:n], X, ALU.add).then_inc(s("gsum"), 1)
                    dve.wait_ge(s("grs"), c + 1)
                    then(v.reciprocal(grs[0:n], grs[0:n]))
                    if c:
                        dve.wait_ge(s("t3"), c)
                    v.tensor_tensor(on[0:n], ot[0:n], each(grs[0:n], DV), ALU.mult).then_inc(s("on"), 1)

            def v_csn(_):
                dve.wait_ge(s("evac"), U_RY)
                for w, src in enumerate((pm, rx)):
                    for i in range(4):
                        v.tensor_copy(ns[:, w, i, 0:3], src[:, i, SEQ:PW])
                        ins = v.tensor_copy(ns[:, w, i, 3:27].rearrange("p (b w) -> p b w", w=3),
                                            sam(src[:, i, PW:PADM])[:, :, LS:SW])
                ins.then_inc(s("ns"), 1)

            def v_gd(h):
                def values(h):
                    v.tensor_tensor(vb[:], gvt[0:TS, h, :].unsqueeze(1).broadcast_to([TS, NB, DV]), each(blk[:], DV),
                                    ALU.mult).then_inc(s("vb"), 1)

                if h == 0:
                    dve.wait_ge(s("t2"), NCH + 1)
                    dve.wait_ge(s("gvt"), NCH + 1)
                    values(0)
                j, q = h // 2, slice(64 * (h % 2), 64 * (h % 2) + 64)
                then(v.tensor_tensor(ss[q, j], ss[q, j], each(dec[q, 16 * j + NCH:16 * j + 16], DV), ALU.mult))
                dve.wait_ge(s("sds"), h + 1)
                v.tensor_tensor(ss[q, j], ss[q, j], ps[q, 2048:3072].rearrange("p (b v) -> p b v", b=NB), ALU.add)\
                    .then_inc(s("ss_new"), 1)
                if h < H - 1:
                    values(h + 1)

            def v_gfin(_):
                dve.wait_ge(s("evac"), U_MO)
                dve.wait_ge(s("t3_copied"), NCH + 1)
                for h in range(H):
                    ins = v.scalar_tensor_tensor(out=gv[:, h, :], in0=gv[:, h, :], scalar=par[:, P_GG + h:P_GG + h + 1],
                                                 in1=gg[:, h, :], op0=ALU.mult, op1=ALU.mult)
                then(ins)
                then(v.tensor_copy(ogh[:], gv[:]))
                dve.wait_ge(s("stored"), 1)
                v.tensor_tensor(ogl[:], gv[:], ogh[:].bitcast(F32), ALU.subtract).then_inc(s("og"), 1)

            def v_rgc(i):
                dve.wait_ge(s("evac"), U_RY)

                conv(rt[i % 2][:, 0:CONVM], rx[:, i, :], CONVM, CW, lambda j: par[:, P_RCW + 4 * j + i:P_RCW + 4 * j + i + 1],
                     par[:, P_RCB + i:P_RCB + i + 1]).then_inc(s("xc"), 1)
                dve.wait_ge(s("xc"), i + 1)

            def v_rg(i):
                if 0 < i < 3:
                    v_rgc(i + 1)
                xc = rt[i % 2][:, 0:CONVM]
                a, h, b, r = (t[:, 0:CONVM] for t in rt[2:])
                dve.wait_ge(s("rg_u"), i + 1)
                if i:
                    dve.wait_ge(s("or"), i)
                then(v.tensor_scalar(r, a, 1.0, None, ALU.add))
                then(v.reciprocal(r, r))
                then(v.scalar_tensor_tensor(out=a, in0=a, scalar=1.0, in1=r, op0=ALU.subtract, op1=ALU.mult, reverse0=True))
                v.tensor_tensor(h, h, xc, ALU.mult)
                then(v.scalar_tensor_tensor(out=b, in0=b, scalar=2.0, in1=r, op0=ALU.mult, op1=ALU.mult))
                then(v.tensor_tensor(b, b, h, ALU.mult))
                v.memset(rt[2][:, PW - 1:PW - 1 + 7 * NB:SW], 0.0)
                then(v.tensor_copy(rt[4][:, PW - 1:PW - 1 + 7 * NB:SW], h0t[:, NB * i:NB * i + NB]))
                then(v.tensor_tensor_scan(h, a, b, 0.0, ALU.mult, ALU.add))
                v.tensor_copy(rhn[:, i, 0:1], h[:, SEQ - 1:SEQ])
                v.tensor_copy(rhn[:, i, 1:9], rt[3][:, PW + LS - 1:PADM:SW])
                v.tensor_tensor(r[:, 0:SEQ], h[:, 0:SEQ], ry[:, i, 0:SEQ], ALU.mult)
                v.tensor_tensor(r[:, SEQ:T].rearrange("p (b t) -> p b t", t=LS), sam(rt[3][:, PW:PADM])[:, :, 0:LS],
                                ry[:, i, SEQ:T].rearrange("p (b t) -> p b t", t=LS), ALU.mult).then_inc(s("rg_o"), 1)
                dve.wait_ge(s("rg_o"), i + 1)
                then(v.tensor_copy(orh[:, i, 0:T], rt[5][:, 0:T]))
                v.tensor_tensor(orl[:, i, :], rt[5][:, 0:T], orh[:, i, 0:T].bitcast(F32), ALU.subtract).then_inc(s("or"), 1)

            def v_mconv(h):
                if h >= 2:
                    dve.wait_ge(s("mcv"), h - 1)
                conv(rt[h % 2][:, 0:CONVM], pm[:, h, :], CONVM, CW,
                     lambda j: par[:, P_MCW + 4 * j + h:P_MCW + 4 * j + h + 1],
                     par[:, P_MCB + h:P_MCB + h + 1]).then_inc(s("mconv"), 1)

            def v_mprep(_):
                for h in range(H):
                    v.tensor_copy(mus[:, h, :].rearrange("p (b t) -> p b t", t=LS), sam(pm[:, h, PW:PADM])[:, :, CW - 1:SW])
                v.memset(vt[:, :, P:P + 1], 1.0)
                v.memset(ct[:], 0.0).then_inc(s("ct0"), 1)
                dve.wait_ge(s("ct0"), 1)

            def v_mqk(h):
                if h == 0:
                    dve.wait_ge(s("mcv"), H)
                    dve.wait_ge(s("stored"), 2)
                dve.wait_ge(s("mqk_mm"), 2 * h + 2)
                v.tensor_scalar(split(mk[:, h, :]), halves(3), float(P) ** -0.5, None, ALU.mult).then_inc(s("mk"), 1)

            def v_mA(c):
                n = MCH if c < NMC else TS
                dve.wait_ge(s("mF"), c + 1)
                mask = negm[:] if c < NMC else negs[:]
                v.tensor_tensor(arg[0:n, :, 0:n], bank(7)[0:n].rearrange("p (h t) -> p h t", h=H)[:, :, 0:n],
                                mask.unsqueeze(1).broadcast_to([n, H, n]), ALU.add).then_inc(s("arg"), 1)
                dve.wait_ge(s("mA"), c + 1)
                if c:
                    dve.wait_ge(s("mU"), min(c, NMC))
                v.tensor_copy(vt[0:n, :, 0:P], bank(5)[0:n].rearrange("p (h d) -> p h d", h=H)).then_inc(s("vt"), 1)
                dve.wait_ge(s("mE"), c + 1)
                dve.wait_ge(s("mKQ"), c + 1)
                v.tensor_tensor(pt[0:n, :, 0:n], arg[0:n, :, 0:n],
                                bank(6)[0:n].rearrange("p (h t) -> p h t", h=H)[:, :, 0:n], ALU.mult).then_inc(s("pt"), 1)

            def head_out(c, n):
                then(v.scalar_tensor_tensor(out=mden[0:n], in0=num[0:n, :, P], scalar=-1.0, in1=num[0:n, :, P],
                                            op0=ALU.mult, op1=ALU.max))
                then(v.tensor_tensor(mden[0:n], mden[0:n], ecol[0:n, c, 32:36], ALU.max))
                then(v.reciprocal(mrec[0:n], mden[0:n]))
                then(v.tensor_tensor(arg[0:n], num[0:n, :, 0:P], num[0:n, :, 0:P], ALU.mult))
                then(v.tensor_reduce(msum[0:n], arg[0:n], X, ALU.add))
                then(v.tensor_tensor(msum[0:n], msum[0:n], mrec[0:n], ALU.mult))
                v.tensor_tensor(msum[0:n], msum[0:n], mrec[0:n], ALU.mult).then_inc(s("msum"), 1)
                dve.wait_ge(s("mrs"), c + 1)
                then(v.reciprocal(mrs[0:n], mrs[0:n]))
                then(v.tensor_tensor(mrec[0:n], mrec[0:n], mrs[0:n], ALU.mult))
                v.tensor_tensor(ti[0:n, :, 0:P], num[0:n, :, 0:P], each(mrec[0:n], P), ALU.mult).then_inc(s("hn"), 1)

            def v_mB(c):
                dve.wait_ge(s("mB"), c + 1)
                if c:
                    dve.wait_ge(s("m3"), c)
                for g in range(2):
                    w = each(ecol[:, c, 2 * g:2 * g + 2], P + 1)
                    ins = v.tensor_tensor(ti[:, 2 * g:2 * g + 2, :], bank(6 + g)[:, 0:258].rearrange("p (h x) -> p h x", h=2), w,
                                          ALU.mult)
                then(ins)
                for g in range(2):
                    ins = v.tensor_tensor(num[:, 2 * g:2 * g + 2, :], ti[:, 2 * g:2 * g + 2, :],
                                          bank(4 + g)[:, 0:258].rearrange("p (h x) -> p h x", h=2), ALU.add)
                ins.then_inc(s("num"), 1)
                dve.wait_ge(s("num"), c + 1)
                head_out(c, MCH)

            def v_mC(c):
                dve.wait_ge(s("mU"), c + 1)
                for h in range(H):
                    ins = v.scalar_tensor_tensor(out=ct[:, h, :], in0=ct[:, h, :], scalar=dcb[:, 12 * h + c:12 * h + c + 1],
                                                 in1=bank(4 + h // 2)[:, (h % 2) * 129:(h % 2) * 129 + 129],
                                                 op0=ALU.mult, op1=ALU.add)
                ins.then_inc(s("mC"), 1)
                dve.wait_ge(s("mC"), c + 1)

            def v_sH(h):
                if h:
                    dve.wait_ge(s("sI"), h)
                dve.wait_ge(s("mqk_mm"), 2 * H)
                dve.wait_ge(s("kw"), NMC + 1)
                v.tensor_copy(cts[:, :, P], nt.rearrange("p (b h) -> p b h", h=H)[:, :, h]).then_inc(s("cts"), 1)
                v.tensor_tensor(kwb[:], kw[0:TS, h, :].unsqueeze(1).broadcast_to([TS, NB, P]), each(blk[:], P), ALU.mult)
                v.tensor_tensor(qbm[:], mq[:, h, SEQ:T].unsqueeze(1).broadcast_to([P, NB, TS]), blkc[:], ALU.mult)\
                    .then_inc(s("qbm"), 1)

            def v_sI(h):
                d = dcb[:, 12 * h + NMC:12 * h + NMC + NB]
                nh = nt.rearrange("p (b h) -> p b h", h=H)[:, :, h]
                c_ = ch_buf[h % 3]
                dve.wait_ge(s("ch_tr"), h + 1)
                then(v.tensor_tensor(c_[:], c_[:], each(d, P), ALU.mult))
                then(v.tensor_tensor(nh, nh, d, ALU.mult))
                dve.wait_ge(s("sI"), h + 1)
                v.tensor_tensor(nh, nh, bank(7)[:, 256:256 + NB], ALU.add)
                then(v.tensor_scalar(ti[0:TS, h, :], bank(6)[0:TS, 0:129], ecol[0:TS, NMC, h:h + 1], None, ALU.mult))
                v.tensor_tensor(num[0:TS, h, :], ti[0:TS, h, :], bank(7)[0:TS, 0:129], ALU.add).then_inc(s("snum"), 1)
                if h == H - 1:
                    dve.wait_ge(s("snum"), H)
                    dve.wait_ge(s("m3"), NMC)
                    head_out(NMC, TS)
                v.tensor_tensor(c_[:], c_[:], ps[:, 2048:3072].rearrange("p (b k) -> p b k", b=NB), ALU.add)\
                    .then_inc(s("ch_new"), 1)

            def v_mfin(_):
                dve.wait_ge(s("evac"), U_GB)
                dve.wait_ge(s("m3_copied"), NMC + 1)
                for h in range(H):
                    then(v.scalar_tensor_tensor(out=mq[:, h, :], in0=mq[:, h, :], scalar=par[:, P_MG + h:P_MG + h + 1],
                                                in1=mo[:, h, :], op0=ALU.mult, op1=ALU.mult))
                    if h == 0:
                        dve.wait_ge(s("stored"), 3)
                    then(v.tensor_copy(omh[:, h, :], mq[:, h, :]))
                    v.tensor_tensor(oml[:, h, :], mq[:, h, :], omh[:, h, :].bitcast(F32), ALU.subtract).then_inc(s("om"), 1)

            def nothing(_):
                pass

            parts = {"a2": v_a2, "csn": v_csn, "rgc": v_rgc, "mconv": v_mconv, "rows": v_rows,
                     "rowt": v_rowt, "gprep": v_gprep, "gla": v_gla, "gd": v_gd, "gfin": v_gfin,
                     "rgd": v_rg, "mprep": v_mprep, "mqk": v_mqk, "mA": v_mA, "mB": v_mB, "mC": v_mC,
                     "sH": v_sH, "sI": v_sI, "mfin": v_mfin}

            def visit(u, part):
                for what, k in visits.get((u, part), []):
                    parts.get(what, nothing)(k)

            for u in range(U_GB):
                visit(u, 0)

            def mixed(n, u, dst, add):
                dve.wait_ge(s("gemm"), u + 1)
                dve.wait_ge(s("gate_ev"), n + 1)
                if not add:
                    v.tensor_tensor(split(dst), split(sg[:]), halves(1), ALU.mult).then_inc(s("br_ev"), 1)
                    return
                v.tensor_tensor(split(sg[:]), split(sg[:]), halves(1), ALU.mult).then_inc(s("br_mul"), 1)
                dve.wait_ge(s("br_mul"), n + (1 - KD))
                v.tensor_tensor(dst, dst, sg[:], ALU.add).then_inc(s("br_ev"), 1)

            for n in range(2 * KD):
                visit(U_GB + n, 1)
                mixed(n, U_GB + n, mix[:, n % KD, :], n >= KD)
                visit(U_GB + n, 0)
            with dve.Fori(0, KD // 2) as i:
                for r in range(2):
                    n = i * 2 + (2 * KD + r)
                    m = bass.ds(i * 2 + r, 1)
                    mixed(n, i * 2 + (U_GB + 2 * KD + r), mix[:, m, :].rearrange("p a t -> p (a t)"), True)
                    dve.wait_ge(s("mh"), i * 2 + (r + 1))
                    v.tensor_tensor(ml[:, m, :], mix[:, m, :], mh[:, m, :].bitcast(F32), ALU.subtract).then_inc(s("ml"), 1)

            dve.wait_ge(s("stored"), 4)
            for j in range(KD):
                dve.wait_ge(s("xt_tr"), j + 1)
                v.tensor_copy(xt[:, j, :], pair(2 + j % 2)[:, 0:T]).then_inc(s("xt"), 1)
            v.memset(up[:, :, 0:FW - 1], 0.0)
            v.memset(ssa[:], 0.0).then_inc(s("ssa"), 1)

            def residual(k, r):
                m = bass.ds(k * 2 + r, 1) if not isinstance(k, int) else slice(2 * k + r, 2 * k + r + 1)
                dve.wait_ge(s("gemm"), k * 2 + (U_OUT + r + 1))
                x = xt[:, m, :].rearrange("p a t -> p (a t)")
                v.tensor_tensor(split(x), split(x), halves(r), ALU.add).then_inc(s("x1"), 1)
                dve.wait_ge(s("x1"), k * 2 + (r + 1))
                dve.wait_ge(s("sq"), k * 2 + (r + 1))
                v.tensor_tensor(ssa[:], ssa[:], hp[:, 0:T], ALU.add).then_inc(s("ssa"), 1)
                dve.wait_ge(s("xh2"), k * 2 + (r + 1))
                g = par[:, bass.ds(k * 2 + (P_G2 + r), 1)] if not isinstance(k, int) else par[:, P_G2 + 2 * k + r:P_G2 + 2 * k + r + 1]
                v.scalar_tensor_tensor(out=xl[:, m, :].rearrange("p a t -> p (a t)"), in0=x, scalar=g,
                                       in1=xh[:, m, :].rearrange("p a t -> p (a t)").bitcast(F32),
                                       op0=ALU.mult, op1=ALU.subtract).then_inc(s("xl2"), 1)
                dve.wait_ge(s("ssa"), k * 2 + (r + 2))

            for r in range(2):
                residual(0, r)
            with dve.Fori(1, KD // 2) as i:
                for r in range(2):
                    residual(i, r)
            dve.wait_ge(s("fst_tr"), 1)
            v.tensor_copy(fst[:, 0:32, :], bank(4).rearrange("p (f x) -> p f x", x=16)).then_inc(s("fst"), 1)
            v.tensor_copy(fst[:, 32:2 * NF, :], bank(5)[:, 0:(2 * NF - 32) * 16].rearrange("p (f x) -> p f x", x=16))\
                .then_inc(s("fst"), 1)
            dve.wait_ge(s("fst"), 2)

            def up_tile(j, r):
                f = j + NF * r
                dve.wait_ge(s("gemm"), j * 2 + (U_UP + r + 1))
                src, row = halves(r), up[:, r, :]
                fs = fst[:, bass.ds(f, 1), :].rearrange("p f (b w) -> p (f b) w", w=FW - 1)
                v.tensor_copy(fsam(row[:, FPW:PADF])[:, :, 0:FW - 1], fs)
                v.tensor_tensor(row[:, FW - 1:FW - 1 + HT], src[:, 0, :], rstd[:, 0:HT], ALU.mult)
                v.tensor_tensor(row[:, FW - 1 + HT:FPW], src[:, 1, 0:SEQ - HT], rstd[:, HT:SEQ], ALU.mult)
                v.tensor_tensor(fsam(row[:, FPW:PADF])[:, :, FW - 1:FSW],
                                src[:, 1, SEQ - HT:HT].rearrange("p (b t) -> p b t", t=LS),
                                rstd[:, SEQ:T].rearrange("p (b t) -> p b t", t=LS), ALU.mult).then_inc(s("uev"), 1)
                dve.wait_ge(s("uev"), j * 2 + (r + 1))
                fo = fns[:, bass.ds(f, 1), :].rearrange("p f x -> p (f x)")
                v.tensor_copy(fo[:, 0:2], row[:, SEQ:FPW])
                v.tensor_copy(fo[:, 2:18].rearrange("p (b w) -> p b w", w=2), fsam(row[:, FPW:PADF])[:, :, LS:FSW])\
                    .then_inc(s("fns"), 1)

                def w(t):
                    return par[:, bass.ds(j + (P_FW + 2 * NF * t + NF * r), 1)]

                out = ca[:, r, 0:CONVF]
                v.tensor_scalar(out, row[:, 0:CONVF], w(0), par[:, bass.ds(j + (P_FB + NF * r), 1)], ALU.mult, ALU.add)\
                    .then_inc(s("tap"), 1)
                for t in (1, 2):
                    dve.wait_ge(s("tap"), j * 4 + (2 * r + t))
                    v.scalar_tensor_tensor(out=out, in0=row[:, t:t + CONVF], scalar=w(t), in1=out, op0=ALU.mult, op1=ALU.add)\
                        .then_inc(s("tap" if t == 1 else "ca"), 1)

            def up_step(j):
                up_tile(j, 0)
                up_tile(j, 1)
                dve.wait_ge(s("gelu"), j + 1)
                dve.wait_ge(s("ca"), j * 2 + 2)
                v.tensor_tensor(hp[:, 0:CONVF], ca[:, 0, 0:CONVF], ca[:, 1, 0:CONVF], ALU.mult).then_inc(s("prod"), 1)
                dve.wait_ge(s("hh"), j + 1)
                hi_, lo_ = (t[:, bass.ds(j, 1), :].rearrange("p a t -> p (a t)") for t in (hh, hl))
                v.tensor_tensor(lo_[:, 0:SEQ], hp[:, 0:SEQ], hi_[:, 0:SEQ].bitcast(F32), ALU.subtract)
                v.tensor_tensor(lo_[:, SEQ:T].rearrange("p (b t) -> p b t", t=LS), fsam(hp[:, FPW:PADF])[:, :, 0:LS],
                                hi_[:, SEQ:T].rearrange("p (b t) -> p b t", t=LS).bitcast(F32), ALU.subtract)\
                    .then_inc(s("hl"), 1)

            dve.wait_ge(s("std"), 1)
            v.reciprocal(rstd[:], rstd[:]).then_inc(s("rstd"), 1)
            dve.wait_ge(s("rstd"), 1)
            with dve.Fori(0, NF) as j:
                up_step(j)

            def output(m, r, u):
                dve.wait_ge(s("gemm"), u + 1)
                x = xt[:, bass.ds(m, 1), :].rearrange("p a (h t) -> p (a h) t", h=2)
                v.tensor_tensor(split(yb[:, r, :]), x, halves(r), ALU.add).then_inc(s("x2"), 1)

            def squares(m, first=False):
                dve.wait_ge(s("ysq"), m + 1)
                if not first:
                    dve.wait_ge(s("yss"), m)
                v.tensor_tensor(yss[:], yss[:], ysq[:], ALU.add).then_inc(s("yss"), 1)

            def gained(m, r, col):
                dve.wait_ge(s("y_tr"), m + 1)
                src = pair(2 + r)
                v.tensor_tensor(ytok[:, 0:4, bass.ds(col, P)], src[:, 0:4 * P].rearrange("p (t c) -> p t c", t=4),
                                gfb[:, bass.ds(col, P)].unsqueeze(1).broadcast_to([P, 4, P]), ALU.mult)
                v.tensor_tensor(ytok[0:TS, 4, bass.ds(col, P)], src[0:TS, 4 * P:5 * P], gfb[0:TS, bass.ds(col, P)],
                                ALU.mult).then_inc(s("y_gain"), 1)

            v.memset(yss[:], 0.0).then_inc(s("y_gain"), 1)
            dve.wait_ge(s("y_gain"), 1)
            output(0, 0, U_DOWN + 1)
            for g in range(1, 6, 2):
                n = (8 if g < 5 else 2 * NF - 40) * P
                dve.wait_ge(s("fns_tr"), g + 1)
                v.tensor_copy(fout[:, 8 * g * P:8 * g * P + n], pair(3)[0:2 + 2 * NB, 0:n]).then_inc(s("fout1"), 1)
            squares(0, first=True)
            output(1, 1, U_DOWN + 3)
            dve.wait_ge(s("late_in"), 64)
            dve.wait_ge(s("stored"), 5)
            gained(0, 0, 0)
            squares(1)
            with dve.Fori(0, KD // 2 - 1) as i:
                for r in range(2):
                    dve.wait_ge(s("y_tr"), i * 2 + (r + 1))
                    output(i * 2 + (r + 2), r, i * 4 + (U_DOWN + 2 * r + 5))
                    gained(i * 2 + (r + 1), 1 - r, i * (2 * P) + (r + 1) * P)
                    squares(i * 2 + (r + 2))
            gained(KD - 1, 1, (KD - 1) * P)
            dve.wait_ge(s("std"), 2)
            v.reciprocal(fstat[:, 0:4], fstat[:, 0:4])
            v.reciprocal(fstat[0:TS, 4:5], fstat[0:TS, 4:5]).then_inc(s("y_rstd"), 1)
            dve.wait_ge(s("y_rstd"), 1)
            dve.wait_ge(s("y_gain"), KD + 1)
            for t in (0, 2, 4):
                n = P if t < 4 else TS
                v.tensor_scalar(ytok[0:n, t, :], ytok[0:n, t, :], fstat[0:n, t:t + 1], None, ALU.mult).then_inc(s("y"), 1)


def _shapes():
    D, NBT, HD = 1, NB, H
    out = [("y_prompt", (1, SEQ, D_MODEL)), ("y_sample", (NB, LS, D_MODEL))]
    for pre, b in (("p_", 1), ("s_", NBT)):
        out += [(pre + "gla_S", (D, b, HD, DK, DV)), (pre + "mlstm_C", (D, b, HD, P, P)), (pre + "mlstm_n", (D, b, HD, P)),
                (pre + "mlstm_m", (D, b, HD)), (pre + "mlstm_conv", (D, b, CW - 1, 512)), (pre + "rglru_h", (D, b, 512)),
                (pre + "rglru_conv", (D, b, CW - 1, 512)), (pre + "ffn_conv", (D, b, FW - 1, 2 * D_FF))]
    return out


def kernel(**inputs):
    import concourse.bacc as bacc
    from concourse.bass_utils import run_bass_kernel_spmd as run

    nc = bacc.Bacc("TRN2", target_bir_lowering=False, num_devices=1)
    arrays, io = {}, {}
    for name, value in inputs.items():
        a = np.ascontiguousarray(value)
        arrays[name] = a
        io[name] = nc.dram_tensor(name, a.shape, mybir.dt.from_np(a.dtype), kind="ExternalInput").ap()
    for name, shape in _shapes():
        io[name] = nc.dram_tensor(name, shape, F32, kind="ExternalOutput").ap()
    layer(nc, io)
    r = run(nc, [arrays], core_ids=[0])
    return tuple(r.results[0][name] for name, _ in _shapes())
```
